# Optimizing a Trainium2 kernel written in Bass

```python
import math
import jax, jax.numpy as jnp
from jax import lax
import numpy as np

D_MODEL = 1024
BATCH = 1
SEQ = 512
DEPTH = 2

GRID_W = 64
CTX_LEN = 256
N_MIXERS = 2
N_ATT_LAYERS = (DEPTH + 1) // 2
N_SSM_LAYERS = DEPTH // 2

ATT_HEADS = 16
ATT_KV_HEADS = 4
HEAD_DIM = 64
ATT_GROUP = ATT_HEADS // ATT_KV_HEADS
ATT_DIM = ATT_HEADS * HEAD_DIM
ATT_IN_DIM = ATT_DIM + 2 * ATT_KV_HEADS * HEAD_DIM
WINDOW = 128
BLOCK = 128
SPAN = BLOCK + 2 * WINDOW
ROPE_BASE = 10000.0
ROPE_AXIS_DIM = HEAD_DIM // 2

SSM_D_INNER = 2 * D_MODEL
SSM_HEAD_DIM = 64
SSM_HEADS = SSM_D_INNER // SSM_HEAD_DIM
SSM_GROUPS = 4
SSM_GROUP_HEADS = SSM_HEADS // SSM_GROUPS
SSM_STATE = 128
SSM_CONV_W = 5
SSM_CHUNK = 128
SSM_CONV_DIM = SSM_D_INNER + 2 * SSM_GROUPS * SSM_STATE
SSM_IN_DIM = SSM_D_INNER + SSM_CONV_DIM + 2 * SSM_HEADS
SSM_NORM_GROUPS = SSM_GROUPS

FF_DIM = 4 * D_MODEL
N_MOD = 6
ALPHA = (2.0 * DEPTH) ** 0.25
BETA = (8.0 * DEPTH) ** -0.25
LN_EPS = 1e-5
RMS_EPS = 1e-5
NEG_INF = -1e30


def layer_norm(x, g, b):
    xf = x.astype(jnp.float32)
    mu = jnp.mean(xf, axis=-1, keepdims=True)
    var = jnp.mean(jnp.square(xf - mu), axis=-1, keepdims=True)
    y = (xf - mu) * lax.rsqrt(var + LN_EPS) * g.astype(jnp.float32) + b.astype(jnp.float32)
    return y.astype(x.dtype)

def modulate(h, shift, scale):
    return h * (1.0 + scale) + shift

def squared_relu_mlp(h, w1, w2):
    return jnp.square(jax.nn.relu(h @ w1)) @ w2

def axial_rope_tables(rows):
    row = jnp.repeat(jnp.arange(rows), GRID_W).astype(jnp.float32)
    col = jnp.tile(jnp.arange(GRID_W), rows).astype(jnp.float32)
    inv_freq = ROPE_BASE ** (-jnp.arange(0, ROPE_AXIS_DIM, 2, dtype=jnp.float32) / ROPE_AXIS_DIM)
    ang_r = row[:, None] * inv_freq[None, :]
    ang_c = col[:, None] * inv_freq[None, :]
    return (jnp.cos(ang_r), jnp.sin(ang_r), jnp.cos(ang_c), jnp.sin(ang_c))

def rotate_half(x, cos, sin):
    x1, x2 = jnp.split(x, 2, axis=-1)
    return jnp.concatenate([x1 * cos - x2 * sin, x2 * cos + x1 * sin], axis=-1)

def apply_axial_rope(x, tables):
    cos_r, sin_r, cos_c, sin_c = tables
    bshape = (x.shape[1],) + (1,) * (x.ndim - 3) + (-1,)
    xf = x.astype(jnp.float32)
    xr = rotate_half(xf[..., :ROPE_AXIS_DIM], cos_r.reshape(bshape), sin_r.reshape(bshape))
    xc = rotate_half(xf[..., ROPE_AXIS_DIM:], cos_c.reshape(bshape), sin_c.reshape(bshape))
    return jnp.concatenate([xr, xc], axis=-1).astype(x.dtype)

def attention_mixer(u_lat, u_ctx, w_in, w_out, sink, rope, need_ctx_out):
    bsz, n, _ = u_lat.shape
    n_ctx = u_ctx.shape[1]
    nb = n // BLOCK
    scale = HEAD_DIM ** -0.5
    sink_f = sink.astype(jnp.float32).reshape(ATT_KV_HEADS, ATT_GROUP)

    def project(u):
        length = u.shape[1]
        q, k, v = jnp.split(u @ w_in, [ATT_DIM, ATT_DIM + ATT_KV_HEADS * HEAD_DIM], axis=-1)
        return (q.reshape(bsz, length, ATT_KV_HEADS, ATT_GROUP, HEAD_DIM),
                k.reshape(bsz, length, ATT_KV_HEADS, HEAD_DIM),
                v.reshape(bsz, length, ATT_KV_HEADS, HEAD_DIM))

    def sink_softmax(logits):
        s = jnp.broadcast_to(sink_f[None, :, :, None, None], logits.shape[:-1] + (1,))
        return jax.nn.softmax(jnp.concatenate([logits, s], axis=-1), axis=-1)

    q_l, k_l, v_l = project(u_lat)
    q_c, k_c, v_c = project(u_ctx)
    qr_l = apply_axial_rope(q_l, rope)
    kr_l = apply_axial_rope(k_l, rope)
    pad = ((0, 0), (WINDOW, WINDOW), (0, 0), (0, 0))
    k_pad = jnp.pad(kr_l, pad)
    v_pad = jnp.pad(v_l, pad)
    q_blocks = jnp.moveaxis(qr_l.reshape(bsz, nb, BLOCK, ATT_KV_HEADS, ATT_GROUP, HEAD_DIM), 1, 0)
    qp_blocks = jnp.moveaxis(q_l.reshape(bsz, nb, BLOCK, ATT_KV_HEADS, ATT_GROUP, HEAD_DIM), 1, 0)
    offs_q = jnp.arange(BLOCK)
    offs_k = jnp.arange(SPAN) - WINDOW

    def block_attend(args):
        blk, qb, qpb = args
        start = blk * BLOCK
        kw = lax.dynamic_slice_in_dim(k_pad, start, SPAN, axis=1)
        vw = lax.dynamic_slice_in_dim(v_pad, start, SPAN, axis=1)
        qi = start + offs_q
        kj = start + offs_k
        ok = (kj[None, :] >= 0) & (kj[None, :] < n) & (jnp.abs(qi[:, None] - kj[None, :]) <= WINDOW)
        s_win = jnp.einsum('blgrd,bsgd->bgrls', qb, kw).astype(jnp.float32) * scale
        s_win = jnp.where(ok, s_win, NEG_INF)
        s_ctx = jnp.einsum('blgrd,bsgd->bgrls', qpb, k_c).astype(jnp.float32) * scale
        p = sink_softmax(jnp.concatenate([s_win, s_ctx], axis=-1)).astype(vw.dtype)
        return (jnp.einsum('bgrls,bsgd->blgrd', p[..., :SPAN], vw)
                + jnp.einsum('bgrls,bsgd->blgrd', p[..., SPAN:SPAN + n_ctx], v_c))

    o = lax.map(block_attend, (jnp.arange(nb), q_blocks, qp_blocks))
    y_lat = jnp.moveaxis(o, 0, 1).reshape(bsz, n, ATT_DIM) @ w_out
    y_ctx = None
    if need_ctx_out:
        s = jnp.einsum('blgrd,bsgd->bgrls', q_c, k_c).astype(jnp.float32) * scale
        p = sink_softmax(s).astype(v_c.dtype)
        o_c = jnp.einsum('bgrls,bsgd->blgrd', p[..., :n_ctx], v_c)
        y_ctx = o_c.reshape(bsz, n_ctx, ATT_DIM) @ w_out
    return y_lat, y_ctx

def depthwise_conv(x, w, bias):
    ch = x.shape[-1]
    y = lax.conv_general_dilated(x, w[:, None, :].astype(x.dtype), window_strides=(1,),
                                 padding=[(SSM_CONV_W // 2, SSM_CONV_W // 2)],
                                 dimension_numbers=('NWC', 'WIO', 'NWC'), feature_group_count=ch)
    return y + bias

def segsum(a):
    t = a.shape[-1]
    a_rep = jnp.broadcast_to(a[..., None], a.shape + (t,))
    a_rep = jnp.where(jnp.tril(jnp.ones((t, t), dtype=bool), -1), a_rep, 0.0)
    cs = jnp.cumsum(a_rep, axis=-2)
    return jnp.where(jnp.tril(jnp.ones((t, t), dtype=bool)), cs, -jnp.inf)

def ssd_scan(xs, dt, a_neg, bm, cm, init_state, with_outputs):
    b, length, g, r, p = xs.shape
    n = bm.shape[-1]
    nc = length // SSM_CHUNK
    q = SSM_CHUNK
    dt4 = dt.reshape(b, length, g, r)
    x_dt = (xs.astype(jnp.float32) * dt4[..., None]).reshape(b, nc, q, g, r, p)
    a = jnp.moveaxis((dt4 * a_neg.reshape(g, r)).reshape(b, nc, q, g, r), 2, -1)
    a_cs = jnp.cumsum(a, axis=-1)
    bc = bm.astype(jnp.float32).reshape(b, nc, q, g, n)
    cc = cm.astype(jnp.float32).reshape(b, nc, q, g, n)
    decay_states = jnp.exp(a_cs[..., -1:] - a_cs)
    states = jnp.einsum('bcsgn,bcgrs,bcsgrp->bcgrpn', bc, decay_states, x_dt)
    states = jnp.concatenate([init_state[:, None], states], axis=1)
    chunk_a = jnp.pad(a_cs[..., -1], ((0, 0), (1, 0), (0, 0), (0, 0)))
    decay_chunk = jnp.exp(segsum(jnp.moveaxis(chunk_a, 1, -1)))
    new_states = jnp.einsum('bgrzc,bcgrpn->bzgrpn', decay_chunk, states)
    final_state = new_states[:, -1]
    if not with_outputs:
        return None, final_state
    prev_states = new_states[:, :-1]
    lmat = jnp.exp(segsum(a))
    cb = jnp.einsum('bclgn,bcsgn->bcgls', cc, bc)
    y_diag = jnp.einsum('bcgrls,bcsgrp->bclgrp', cb[:, :, :, None] * lmat, x_dt)
    y_off = jnp.einsum('bclgn,bcgrpn,bcgrl->bclgrp', cc, prev_states, jnp.exp(a_cs))
    return (y_diag + y_off).reshape(b, length, g, r, p), final_state

def ssm_mixer(u_lat, u_ctx, w_in, conv_w, conv_b, dt_bias, a_log, d_skip, norm_g, w_out, need_ctx_out):
    a_neg = -jnp.exp(a_log.astype(jnp.float32))
    bsz = u_lat.shape[0]

    def flip(t):
        return jnp.flip(t, axis=1)

    def prep(u):
        length = u.shape[1]
        z, xbc, dt = jnp.split(u @ w_in, [SSM_D_INNER, SSM_D_INNER + SSM_CONV_DIM], axis=-1)
        xbc = jax.nn.silu(depthwise_conv(xbc, conv_w, conv_b))
        xs, bm, cm = jnp.split(xbc, [SSM_D_INNER, SSM_D_INNER + SSM_GROUPS * SSM_STATE], axis=-1)
        xs = xs.reshape(bsz, length, SSM_GROUPS, SSM_GROUP_HEADS, SSM_HEAD_DIM)
        bm = bm.reshape(bsz, length, SSM_GROUPS, SSM_STATE)
        cm = cm.reshape(bsz, length, SSM_GROUPS, SSM_STATE)
        dt = jax.nn.softplus(dt.astype(jnp.float32).reshape(bsz, length, 2, SSM_HEADS)
                             + dt_bias.astype(jnp.float32))
        return z, xs, bm, cm, dt

    def finish(z, xs, y_f, y_b):
        length = xs.shape[1]
        y = y_f + y_b + xs.astype(jnp.float32) * d_skip.astype(jnp.float32).reshape(SSM_GROUPS, SSM_GROUP_HEADS, 1)
        y = y.reshape(bsz, length, SSM_D_INNER) * jax.nn.silu(z.astype(jnp.float32))
        y = y.reshape(bsz, length, SSM_NORM_GROUPS, -1)
        y = y * lax.rsqrt(jnp.mean(jnp.square(y), axis=-1, keepdims=True) + RMS_EPS)
        y = (y.reshape(bsz, length, SSM_D_INNER) * norm_g.astype(jnp.float32)).astype(z.dtype)
        return y @ w_out

    z_c, x_c, b_c, c_c, dt_c = prep(u_ctx)
    z_l, x_l, b_l, c_l, dt_l = prep(u_lat)
    init = jnp.zeros((bsz, SSM_GROUPS, SSM_GROUP_HEADS, SSM_HEAD_DIM, SSM_STATE), jnp.float32)
    yc_f, st_f = ssd_scan(x_c, dt_c[:, :, 0], a_neg[0], b_c, c_c, init, need_ctx_out)
    yc_b, st_b = ssd_scan(flip(x_c), flip(dt_c[:, :, 1]), a_neg[1], flip(b_c), flip(c_c), init, need_ctx_out)
    yl_f, _ = ssd_scan(x_l, dt_l[:, :, 0], a_neg[0], b_l, c_l, st_f, True)
    yl_b, _ = ssd_scan(flip(x_l), flip(dt_l[:, :, 1]), a_neg[1], flip(b_l), flip(c_l), st_b, True)
    y_lat = finish(z_l, x_l, yl_f, flip(yl_b))
    y_ctx = finish(z_c, x_c, yc_f, flip(yc_b)) if need_ctx_out else None
    return y_lat, y_ctx

def first_inputs(seed: int = 0) -> dict:
    key = jax.random.key(seed)
    ks = jax.random.split(key, 24)
    f = jnp.float32
    d = D_MODEL

    def nrm(k, shape, scale):
        return jax.random.normal(k, shape, f) * scale

    dt0 = jnp.exp(jax.random.uniform(ks[15], (N_SSM_LAYERS, 2, SSM_HEADS), f, math.log(1e-3), math.log(1e-1)))
    return {
        'x': nrm(ks[0], (BATCH, SEQ, d), 1.0),
        'c': nrm(ks[1], (BATCH, d), 1.0),
        'ctx': nrm(ks[2], (BATCH, CTX_LEN, d), 1.0),
        'c_ctx': nrm(ks[3], (d,), 1.0),
        'w_mod': nrm(ks[4], (DEPTH, d, N_MOD * d), 0.5 * d ** -0.5),
        'b_mod': nrm(ks[5], (DEPTH, N_MOD * d), 0.02),
        'ln_mix_g': 1.0 + nrm(ks[6], (DEPTH, d), 0.02),
        'ln_mix_b': nrm(ks[7], (DEPTH, d), 0.02),
        'ln_ff_g': 1.0 + nrm(ks[8], (DEPTH, d), 0.02),
        'ln_ff_b': nrm(ks[9], (DEPTH, d), 0.02),
        'att_w_in': nrm(ks[10], (N_ATT_LAYERS, d, ATT_IN_DIM), d ** -0.5),
        'att_w_out': nrm(ks[11], (N_ATT_LAYERS, ATT_DIM, d), BETA * ATT_DIM ** -0.5),
        'att_sink': nrm(ks[12], (N_ATT_LAYERS, ATT_HEADS), 0.5),
        'ssm_w_in': nrm(ks[13], (N_SSM_LAYERS, d, SSM_IN_DIM), d ** -0.5),
        'ssm_conv_w': nrm(ks[14], (N_SSM_LAYERS, SSM_CONV_W, SSM_CONV_DIM), SSM_CONV_W ** -0.5),
        'ssm_conv_b': nrm(ks[16], (N_SSM_LAYERS, SSM_CONV_DIM), 0.02),
        'ssm_dt_bias': dt0 + jnp.log(-jnp.expm1(-dt0)),
        'ssm_a_log': jnp.log(jax.random.uniform(ks[17], (N_SSM_LAYERS, 2, SSM_HEADS), f, 1.0, 16.0)),
        'ssm_d': 1.0 + nrm(ks[18], (N_SSM_LAYERS, SSM_HEADS), 0.1),
        'ssm_norm_g': 1.0 + nrm(ks[19], (N_SSM_LAYERS, SSM_D_INNER), 0.02),
        'ssm_w_out': nrm(ks[20], (N_SSM_LAYERS, SSM_D_INNER, d), BETA * SSM_D_INNER ** -0.5),
        'ff_w1': nrm(ks[21], (DEPTH, d, FF_DIM), d ** -0.5),
        'ff_w2': nrm(ks[22], (DEPTH, FF_DIM, d), BETA * FF_DIM ** -0.5),
    }

def first_block(x, c, ctx, c_ctx, w_mod, b_mod, ln_mix_g, ln_mix_b, ln_ff_g, ln_ff_b,
              att_w_in, att_w_out, att_sink, ssm_w_in, ssm_conv_w, ssm_conv_b, ssm_dt_bias,
              ssm_a_log, ssm_d, ssm_norm_g, ssm_w_out, ff_w1, ff_w2):
    rows = x.shape[1] // GRID_W
    rope = axial_rope_tables(rows)
    h_lat, h_ctx = x, ctx
    for i in range(DEPTH):
        last = i == DEPTH - 1
        j = i // N_MIXERS
        m_lat = (jax.nn.silu(c) @ w_mod[i] + b_mod[i])[:, None, :]
        m_ctx = (jax.nn.silu(c_ctx) @ w_mod[i] + b_mod[i])[None, None, :]
        sh_m_l, sc_m_l, g_m_l, sh_f_l, sc_f_l, g_f_l = jnp.split(m_lat, N_MOD, axis=-1)
        sh_m_c, sc_m_c, g_m_c, sh_f_c, sc_f_c, g_f_c = jnp.split(m_ctx, N_MOD, axis=-1)
        u_lat = modulate(h_lat, sh_m_l, sc_m_l)
        u_ctx = modulate(h_ctx, sh_m_c, sc_m_c)
        if i % N_MIXERS == 0:
            y_lat, y_ctx = attention_mixer(u_lat, u_ctx, att_w_in[j], att_w_out[j], att_sink[j], rope, not last)
        else:
            y_lat, y_ctx = ssm_mixer(u_lat, u_ctx, ssm_w_in[j], ssm_conv_w[j], ssm_conv_b[j], ssm_dt_bias[j],
                                     ssm_a_log[j], ssm_d[j], ssm_norm_g[j], ssm_w_out[j], not last)
        h_lat = layer_norm(ALPHA * h_lat + g_m_l * y_lat, ln_mix_g[i], ln_mix_b[i])
        f_lat = squared_relu_mlp(modulate(h_lat, sh_f_l, sc_f_l), ff_w1[i], ff_w2[i])
        h_lat = layer_norm(ALPHA * h_lat + g_f_l * f_lat, ln_ff_g[i], ln_ff_b[i])
        if not last:
            h_ctx = layer_norm(ALPHA * h_ctx + g_m_c * y_ctx, ln_mix_g[i], ln_mix_b[i])
            f_ctx = squared_relu_mlp(modulate(h_ctx, sh_f_c, sc_f_c), ff_w1[i], ff_w2[i])
            h_ctx = layer_norm(ALPHA * h_ctx + g_f_c * f_ctx, ln_ff_g[i], ln_ff_b[i])
    return h_lat


N_EVEN = (DEPTH + 1) // 2
N_ODD = DEPTH // 2
EPS = 1e-6

MIX_WIDTH = D_MODEL
FOURIER_WIDTH = MIX_WIDTH // 2
FOURIER_GROUPS = 4
FOURIER_GROUP_DIM = FOURIER_WIDTH // FOURIER_GROUPS
GLA_HEADS = 4
GLA_VAL_WIDTH = MIX_WIDTH - FOURIER_WIDTH
GLA_DV = GLA_VAL_WIDTH // GLA_HEADS
GLA_DK = GLA_DV // 2
GLA_KEY_WIDTH = GLA_HEADS * GLA_DK
GLA_GATE_RANK = 16
GLA_GATE_TEMP = 16.0
GLA_CHUNK = 64
EVEN_SPLITS = [FOURIER_WIDTH,
               FOURIER_WIDTH + GLA_KEY_WIDTH,
               FOURIER_WIDTH + 2 * GLA_KEY_WIDTH,
               FOURIER_WIDTH + 2 * GLA_KEY_WIDTH + GLA_VAL_WIDTH,
               FOURIER_WIDTH + 2 * GLA_KEY_WIDTH + 2 * GLA_VAL_WIDTH]
EVEN_IN_WIDTH = EVEN_SPLITS[-1] + GLA_GATE_RANK

HEAD_DIM_2 = 128
ATT_HEADS_2 = D_MODEL // HEAD_DIM_2
ATT_KV_HEADS_2 = 2
ATT_GROUP_2 = ATT_HEADS_2 // ATT_KV_HEADS_2
Q_WIDTH = ATT_HEADS_2 * HEAD_DIM_2
QKV_WIDTH = (ATT_HEADS_2 + 2 * ATT_KV_HEADS_2) * HEAD_DIM_2
Q_BLOCK = 128
ROPE_THETA = 10000.0
ROPE_AXIS_DIM_2 = HEAD_DIM_2 // 2

D_FF = ((8 * D_MODEL // 3 + 255) // 256) * 256
CONV_W = 3


def rms_norm(x, g):
    xf = x.astype(jnp.float32)
    y = xf * lax.rsqrt(jnp.mean(xf * xf, axis=-1, keepdims=True) + EPS)
    return (y * g.astype(jnp.float32)).astype(x.dtype)

def adaln(cv, w, b):
    m = jax.nn.silu(cv) @ w + b
    m = m.reshape(cv.shape[:-1] + (1, N_MOD, D_MODEL))
    return [m[..., k, :] for k in range(N_MOD)]

def dwconv_centred(x, w, b):
    L = x.shape[1]
    pad = CONV_W // 2
    xp = jnp.pad(x, ((0, 0), (pad, CONV_W - 1 - pad), (0, 0)))
    out = b
    for k in range(CONV_W):
        out = out + xp[:, k:k + L] * w[k]
    return out

def conv_ffn(h, w_up, w_conv, b_conv, w_down):
    u = dwconv_centred(h @ w_up, w_conv, b_conv)
    g, v = jnp.split(u, 2, axis=-1)
    return (jax.nn.silu(g) * v) @ w_down

def fourier_mix(u):
    B_, L, _ = u.shape
    ug = u.reshape(B_, L, FOURIER_GROUPS, FOURIER_GROUP_DIM).astype(jnp.float32)
    f = jnp.fft.fft2(ug, axes=(1, 3), norm='ortho').real
    return f.reshape(B_, L, FOURIER_WIDTH).astype(u.dtype)

def gla_scan(q, k, v, loga, s0):
    q, k, v = (t.astype(jnp.float32) for t in (q, k, v))
    B_, H, L, _ = q.shape
    n = L // GLA_CHUNK

    def to_chunks(t):
        return jnp.moveaxis(t.reshape(B_, H, n, GLA_CHUNK, t.shape[-1]), 2, 0)

    mask = jnp.tril(jnp.ones((GLA_CHUNK, GLA_CHUNK), bool))[:, :, None]

    def step(S, inp):
        qc, kc, vc, ac = inp
        b = jnp.cumsum(ac, axis=2)
        diff = b[:, :, :, None, :] - b[:, :, None, :, :]
        decay = jnp.exp(jnp.where(mask, diff, -jnp.inf))
        attn = jnp.einsum('bhid,bhjd,bhijd->bhij', qc, kc, decay)
        o = attn @ vc + jnp.einsum('bhid,bhde->bhie', qc * jnp.exp(b), S)
        b_last = b[:, :, -1:, :]
        S_new = (jnp.exp(b_last[:, :, 0, :, None]) * S
                 + jnp.einsum('bhjd,bhje->bhde', kc * jnp.exp(b_last - b), vc))
        return S_new, o

    s_fin, o = lax.scan(step, s0, (to_chunks(q), to_chunks(k), to_chunks(v), to_chunks(loga)))
    o = jnp.moveaxis(o, 0, 2).reshape(B_, H, L, v.shape[-1])
    return o, s_fin

def even_mix(h, s_f, s_b, w_in, w_gate, b_gate, g_gla, w_out):
    B_, L, _ = h.shape
    p = h @ w_in
    u_f, q, k, v, r, z = jnp.split(p, EVEN_SPLITS, axis=-1)

    def heads(t, d):
        return t.reshape(B_, L, GLA_HEADS, d).transpose(0, 2, 1, 3)

    q = heads(q, GLA_DK) * (GLA_DK ** -0.5)
    k = heads(k, GLA_DK)
    v = heads(v, GLA_DV)
    zf = z.astype(jnp.float32)
    loga = [heads(jax.nn.log_sigmoid(zf @ w_gate[d].astype(jnp.float32) + b_gate[d].astype(jnp.float32))
                  / GLA_GATE_TEMP, GLA_DK) for d in range(2)]

    def flip(t):
        return jnp.flip(t, axis=2)

    o_f, s_f = gla_scan(q, k, v, loga[0], s_f)
    o_b, s_b = gla_scan(flip(q), flip(k), flip(v), flip(loga[1]), s_b)
    o = o_f + flip(o_b)
    o = o * lax.rsqrt(jnp.mean(o * o, axis=-1, keepdims=True) + EPS)
    o = o.transpose(0, 2, 1, 3).reshape(B_, L, GLA_VAL_WIDTH) * g_gla.astype(jnp.float32)
    o = (o * jax.nn.silu(r.astype(jnp.float32))).astype(h.dtype)
    y = jnp.concatenate([fourier_mix(u_f), o], axis=-1) @ w_out
    return y, s_f, s_b

def axial_rope_tables_2(n_tokens):
    rows = n_tokens // GRID_W
    r, c = jnp.meshgrid(jnp.arange(rows), jnp.arange(GRID_W), indexing='ij')
    inv = ROPE_THETA ** (-jnp.arange(0, ROPE_AXIS_DIM_2, 2, dtype=jnp.float32) / ROPE_AXIS_DIM_2)
    ang = jnp.concatenate([r.reshape(-1, 1).astype(jnp.float32) * inv,
                           c.reshape(-1, 1).astype(jnp.float32) * inv], axis=-1)
    return jnp.cos(ang), jnp.sin(ang)

def apply_rope(t, cos, sin):
    tf = t.astype(jnp.float32)
    t1, t2 = jnp.split(tf, 2, axis=-1)
    return jnp.concatenate([t1 * cos - t2 * sin, t1 * sin + t2 * cos], axis=-1).astype(t.dtype)

def attn_q(h, w_q, g_q):
    B_, L, _ = h.shape
    q = rms_norm((h @ w_q).reshape(B_, L, ATT_HEADS_2, HEAD_DIM_2), g_q)
    return q.transpose(0, 2, 1, 3)

def attn_kv(h, w_kv, g_k):
    B_, L, _ = h.shape
    kv = (h @ w_kv).reshape(B_, L, 2, ATT_KV_HEADS_2, HEAD_DIM_2)
    k = rms_norm(kv[:, :, 0], g_k).transpose(0, 2, 1, 3)
    v = kv[:, :, 1].transpose(0, 2, 1, 3)
    return k, v

def grouped_attend(q, k, v):
    s = jnp.einsum('bkgqd,bksd->bkgqs', q, k).astype(jnp.float32) * (HEAD_DIM_2 ** -0.5)
    p = jax.nn.softmax(s, axis=-1).astype(v.dtype)
    return jnp.einsum('bkgqs,bksd->bkgqd', p, v)

def second_inputs(seed: int = 0) -> dict:
    key = jax.random.key(seed)
    ks = jax.random.split(key, 22)
    f32 = jnp.float32

    def nrm(k, shape, scale):
        return jax.random.normal(k, shape, f32) * scale

    def gain(k, shape):
        return 1.0 + 0.02 * jax.random.normal(k, shape, f32)

    return {
        'x': nrm(ks[0], (BATCH, SEQ, D_MODEL), 1.0),
        'c': nrm(ks[1], (BATCH, D_MODEL), 1.0),
        'ctx': nrm(ks[2], (BATCH, CTX_LEN, D_MODEL), 1.0),
        'c_ctx': nrm(ks[3], (D_MODEL,), 1.0),
        'w_mod': nrm(ks[4], (DEPTH, D_MODEL, N_MOD * D_MODEL), D_MODEL ** -0.5),
        'b_mod': nrm(ks[5], (DEPTH, N_MOD * D_MODEL), 0.02),
        'g_norm_mix': gain(ks[6], (DEPTH, D_MODEL)),
        'g_norm_ffn': gain(ks[7], (DEPTH, D_MODEL)),
        'g_norm_final': gain(ks[8], (D_MODEL,)),
        'w_even_in': nrm(ks[9], (N_EVEN, D_MODEL, EVEN_IN_WIDTH), D_MODEL ** -0.5),
        'w_gla_gate': nrm(ks[10], (N_EVEN, 2, GLA_GATE_RANK, GLA_KEY_WIDTH), GLA_GATE_RANK ** -0.5),
        'b_gla_gate': nrm(ks[11], (N_EVEN, 2, GLA_KEY_WIDTH), 0.1),
        'g_gla_out': gain(ks[12], (N_EVEN, GLA_VAL_WIDTH)),
        'w_even_out': nrm(ks[13], (N_EVEN, MIX_WIDTH, D_MODEL), MIX_WIDTH ** -0.5),
        'w_qkv': nrm(ks[14], (N_ODD, D_MODEL, QKV_WIDTH), D_MODEL ** -0.5),
        'g_q': gain(ks[15], (N_ODD, HEAD_DIM_2)),
        'g_k': gain(ks[16], (N_ODD, HEAD_DIM_2)),
        'w_att_out': nrm(ks[17], (N_ODD, Q_WIDTH, D_MODEL), Q_WIDTH ** -0.5),
        'w_ffn_up': nrm(ks[18], (DEPTH, D_MODEL, 2 * D_FF), D_MODEL ** -0.5),
        'w_ffn_conv': nrm(ks[19], (DEPTH, CONV_W, 2 * D_FF), CONV_W ** -0.5),
        'b_ffn_conv': nrm(ks[20], (DEPTH, 2 * D_FF), 0.02),
        'w_ffn_down': nrm(ks[21], (DEPTH, D_FF, D_MODEL), D_FF ** -0.5),
    }

def second_block(x, c, ctx, c_ctx, w_mod, b_mod, g_norm_mix, g_norm_ffn, g_norm_final,
              w_even_in, w_gla_gate, b_gla_gate, g_gla_out, w_even_out,
              w_qkv, g_q, g_k, w_att_out,
              w_ffn_up, w_ffn_conv, b_ffn_conv, w_ffn_down):
    B_, S, _ = x.shape
    cos, sin = axial_rope_tables_2(S)
    h_lat, h_ctx = x, ctx
    for i in range(DEPTH):
        last = i == DEPTH - 1
        j = i // 2
        sh1, sc1, ga1, sh2, sc2, ga2 = adaln(c, w_mod[i], b_mod[i])
        csh1, csc1, cga1, csh2, csc2, cga2 = adaln(c_ctx, w_mod[i], b_mod[i])
        a_lat = rms_norm(h_lat, g_norm_mix[i]) * (1 + sc1) + sh1
        a_ctx = rms_norm(h_ctx, g_norm_mix[i]) * (1 + csc1) + csh1
        if i % 2 == 0:
            zero = jnp.zeros((B_, GLA_HEADS, GLA_DK, GLA_DV), jnp.float32)
            o_ctx, s_f, s_b = even_mix(a_ctx, zero, zero, w_even_in[j], w_gla_gate[j],
                                       b_gla_gate[j], g_gla_out[j], w_even_out[j])
            o_lat, _, _ = even_mix(a_lat, s_f, s_b, w_even_in[j], w_gla_gate[j],
                                   b_gla_gate[j], g_gla_out[j], w_even_out[j])
        else:
            w_q = w_qkv[j][:, :Q_WIDTH]
            w_kv = w_qkv[j][:, Q_WIDTH:]
            q_l = apply_rope(attn_q(a_lat, w_q, g_q[j]), cos, sin)
            k_l, v_l = attn_kv(a_lat, w_kv, g_k[j])
            k_l = apply_rope(k_l, cos, sin)
            k_c, v_c = attn_kv(a_ctx, w_kv, g_k[j])
            k_all = jnp.concatenate([k_c, k_l], axis=2)
            v_all = jnp.concatenate([v_c, v_l], axis=2)
            nb = S // Q_BLOCK
            qb = jnp.moveaxis(q_l.reshape(B_, ATT_KV_HEADS_2, ATT_GROUP_2, nb, Q_BLOCK, HEAD_DIM_2), 3, 0)
            ob = lax.map(lambda blk: grouped_attend(blk, k_all, v_all), qb)
            o_lat = ob.transpose(1, 0, 4, 2, 3, 5).reshape(B_, S, Q_WIDTH) @ w_att_out[j]
            if not last:
                Lc = a_ctx.shape[1]
                q_c = attn_q(a_ctx, w_q, g_q[j]).reshape(B_, ATT_KV_HEADS_2, ATT_GROUP_2, Lc, HEAD_DIM_2)
                o_c = grouped_attend(q_c, k_c, v_c)
                o_ctx = o_c.transpose(0, 3, 1, 2, 4).reshape(B_, Lc, Q_WIDTH) @ w_att_out[j]
        h_lat = h_lat + ga1 * o_lat
        f_lat = rms_norm(h_lat, g_norm_ffn[i]) * (1 + sc2) + sh2
        h_lat = h_lat + ga2 * conv_ffn(f_lat, w_ffn_up[i], w_ffn_conv[i], b_ffn_conv[i], w_ffn_down[i])
        if not last:
            h_ctx = h_ctx + cga1 * o_ctx
            f_ctx = rms_norm(h_ctx, g_norm_ffn[i]) * (1 + csc2) + csh2
            h_ctx = h_ctx + cga2 * conv_ffn(f_ctx, w_ffn_up[i], w_ffn_conv[i], b_ffn_conv[i], w_ffn_down[i])
    return rms_norm(h_lat, g_norm_final)


def setup_inputs(seed=0):
    out = dict(first_inputs(seed))
    for name, value in second_inputs(seed + 1).items():
        if name != "x":
            out[name + "_2"] = value
    return out


def reference(
    x, c, ctx, c_ctx, w_mod, b_mod, ln_mix_g, ln_mix_b, ln_ff_g, ln_ff_b, att_w_in, att_w_out,
    att_sink, ssm_w_in, ssm_conv_w, ssm_conv_b, ssm_dt_bias, ssm_a_log, ssm_d, ssm_norm_g,
    ssm_w_out, ff_w1, ff_w2, c_2, ctx_2, c_ctx_2, w_mod_2, b_mod_2, g_norm_mix_2, g_norm_ffn_2,
    g_norm_final_2, w_even_in_2, w_gla_gate_2, b_gla_gate_2, g_gla_out_2, w_even_out_2, w_qkv_2,
    g_q_2, g_k_2, w_att_out_2, w_ffn_up_2, w_ffn_conv_2, b_ffn_conv_2, w_ffn_down_2,
):
    x = first_block(
        x, c, ctx, c_ctx, w_mod, b_mod, ln_mix_g, ln_mix_b, ln_ff_g, ln_ff_b, att_w_in,
        att_w_out, att_sink, ssm_w_in, ssm_conv_w, ssm_conv_b, ssm_dt_bias, ssm_a_log, ssm_d,
        ssm_norm_g, ssm_w_out, ff_w1, ff_w2,
    )
    return second_block(
        x, c_2, ctx_2, c_ctx_2, w_mod_2, b_mod_2, g_norm_mix_2, g_norm_ffn_2, g_norm_final_2,
        w_even_in_2, w_gla_gate_2, b_gla_gate_2, g_gla_out_2, w_even_out_2, w_qkv_2, g_q_2,
        g_k_2, w_att_out_2, w_ffn_up_2, w_ffn_conv_2, b_ffn_conv_2, w_ffn_down_2,
    )


_drawn_inputs = setup_inputs


def setup_inputs(seed=0):
    import zlib

    import numpy as np

    out = dict(_drawn_inputs(seed))
    spreads = {}
    factors = {'ctx': 5.061,
     'att_sink': 64.0,
     'ssm_conv_b': 8.0,
     'ssm_d': 8.0,
     'ssm_norm_g': 8.0,
     'g_norm_mix_2': 3.748,
     'g_norm_ffn_2': 3.149,
     'g_norm_final_2': 7.416,
     'g_gla_out_2': 7.207,
     'g_q_2': 8.0,
     'g_k_2': 8.0,
     'b_ffn_conv_2': 3.728}
    for name, (base, spread) in spreads.items():
        noise = np.random.default_rng([zlib.crc32(name.encode()), seed]).standard_normal(out[name].shape)
        drawn = base * np.exp(spread * noise) if base else spread * noise
        out[name] = __import__('jax').numpy.asarray(drawn.astype(out[name].dtype))
    for name, factor in factors.items():
        out[name] = (out[name] * factor).astype(out[name].dtype)
    return out
```

```python
import concourse.bass as bass
from concourse import mybir
from contextlib import ExitStack
import numpy as np

F32 = mybir.dt.float32
U32 = mybir.dt.uint32
ALU = mybir.AluOpType
ACT = mybir.ActivationFunctionType
AX = mybir.AxisListType

D = 1024
KD = D // 128
LAT, CTX = 512, 256
TL, TC = LAT // 128, CTX // 128
TOK = LAT + CTX
NT = TL + TC
RINGW = 8 * 512
DEPTH = 2
ALPHA = (2.0 * DEPTH) ** 0.25
LN_EPS, RMS_EPS, EPS2 = 1e-5, 1e-5, 1e-6
FF = 4 * D
DFF2 = ((8 * D // 3 + 255) // 256) * 256
NF2 = DFF2 // 128
F2_PARTS = [6, 6, 5, 5]
GRID_W = 64
HA, GA, DA = 16, 4, 64
HB_, GB_, DB = 8, 2, 128
WIN_NEG = -8e30
SSM_H, SSM_P, SSM_G, SSM_N = 32, 64, 4, 128
SSM_DI = SSM_H * SSM_P
SSM_GH = SSM_H // SSM_G
CONV_SSM = SSM_DI + 2 * SSM_G * SSM_N
GLA_H, GLA_DK, GLA_DV, GLA_R = 4, 64, 128, 16
GLA_LEVELS = 8
FW = 512


def constants():
    p = np.arange(128)
    r, c = p[:, None], p[None, :]
    sel = np.zeros((128, 2, 128), np.float32)
    sel[0, 0], sel[1, 1] = 1, 1
    small = dict(
        ident=(r == c), upto=(r <= c), downto=(r >= c), after=(r > c), before=(r < c),
        ones=np.ones((128, 128)), sel=sel.reshape(128, 256))
    inv = (10000.0 ** (-np.arange(0, 32, 2, dtype=np.float32) / np.float32(32))).astype(np.float32)
    tok = np.arange(LAT)
    row, col = (tok // GRID_W).astype(np.float32), (tok % GRID_W).astype(np.float32)
    dim = p % 64
    pos = np.where((dim < 32)[:, None], row[None], col[None]).astype(np.float32)
    ang = (pos * inv[dim % 16][:, None]).astype(np.float32)
    swap = np.zeros((128, 128), np.float32)
    for o in range(128):
        if o % 32 < 16:
            swap[o + 16, o] = -1.0
        else:
            swap[o - 16, o] = 1.0
    att = dict(cosT=np.cos(ang), sinT=np.sin(ang), swap=swap,
               maskl=np.where(c >= r, 0, WIN_NEG), maskr=np.where(c <= r, 0, WIN_NEG))
    inv2 = (10000.0 ** (-np.arange(0, 64, 2, dtype=np.float32) / np.float32(64))).astype(np.float32)
    ang2 = np.concatenate([row[:, None] * inv2, col[:, None] * inv2], 1).astype(np.float32)
    t2 = lambda a: a.reshape(TL, 128, 64).transpose(1, 0, 2).reshape(128, TL * 64)
    att2 = dict(cos2=t2(np.cos(ang2)), sin2=t2(np.sin(ang2)))
    def dft(n, s):
        k = np.outer(np.arange(n), np.arange(n)) % n
        a = 2 * np.pi * k / n
        return np.cos(a) * s, np.sin(a) * s
    cd, sd = dft(128, 1.0)
    cl, sl = dft(LAT, (LAT * 128.0) ** -0.5)
    cc, sc = dft(CTX, (CTX * 128.0) ** -0.5)
    tile = lambda a: a.reshape(-1, 128, a.shape[1]).transpose(1, 0, 2).reshape(128, -1)
    four = dict(dftd=np.concatenate([cd, sd], 1), cosl=tile(cl), sinl=tile(-sl), cosc=tile(cc), sinc=tile(-sc))
    masks = np.zeros((128, 2, GLA_LEVELS, 128), np.uint8)
    for v in range(GLA_LEVELS - 1):
        m = 64 >> v
        same = (r // (2 * m)) == (c // (2 * m))
        masks[:, 0, v] = same & ((c // m) % 2 == 1) & ((r // m) % 2 == 0)
        masks[:, 1, v] = same & ((c // m) % 2 == 0) & ((r // m) % 2 == 1)
    masks[:, 0, 7] = masks[:, 1, 7] = (r == c)
    out = {}
    for n, part in dict(c_small=small, c_att=att, c_att2=att2, c_four=four).items():
        blocks, at, x = [], {}, 0
        for k, v in part.items():
            v = np.asarray(v, np.float32)
            at[k] = (x, v.shape[1])
            x += v.shape[1]
            blocks.append(v)
        out[n] = (np.ascontiguousarray(np.concatenate(blocks, 1)), at)
    out["c_mask"] = (masks.reshape(128, -1).view(np.uint32), {})
    return out


def build(nc, d, layers=(0, 1, 2, 3), debug=None):
    at = d["at"]
    ctxs = ExitStack()
    with ctxs:
        def sb(name, shape, dt=F32):
            return ctxs.enter_context(nc.sbuf_tensor(name, shape, dt))

        sems = {}

        def S(name):
            if name not in sems:
                sems[name] = ctxs.enter_context(nc.semaphore(name))
            return sems[name]

        H = sb("H", [128, NT, D])
        UT = sb("UT", [128, KD, TOK])
        RING = sb("RING", [128, 2, RINGW])
        BIG = sb("BIG", [128, 24576])
        GATE = sb("GATE", [128, 2, 2, D])
        GB = sb("GB", [128, 2, D])
        CS = sb("CS", [128, d["c_small"].shape[1]])
        CV = sb("CV", [128, KD, 4])
        COL = sb("COL", [128, 4, KD, 2])
        GCOL = sb("GCOL", [128, 2, KD])
        MODC = sb("MODC", [128, 6 * KD, 2])
        ST = sb("ST", [128, 160])
        ST2 = sb("ST2", [128, 48])
        EPSC, RMSC = ST2[:, 40:41], ST2[:, 41:42]
        RES_TMP = sb("RES_TMP", [128, 512])
        PS = ctxs.enter_context(nc.psum_tensor("PS", [128, 4096], F32))

        def big(off, *shape):
            n = int(np.prod(shape))
            assert off + n <= 24576, (off, shape)
            v = BIG[:, off:off + n]
            if len(shape) == 2:
                v = v.rearrange("p (a b) -> p a b", a=shape[0])
            if len(shape) == 3:
                v = v.rearrange("p (a b c) -> p a b c", a=shape[0], b=shape[1])
            return v

        def cs(name):
            x, n = at["c_small"][name]
            return CS[:, x:x + n]

        ident = cs("ident")
        ones = cs("ones")
        sel = cs("sel").rearrange("p (a b) -> p a b", a=2)

        def bank(b, n=512, off=0):
            return PS[:, b * 512 + off:b * 512 + off + n]

        def ring(slot, kc=8, cols=512):
            return RING[:, slot, 0:kc * cols].rearrange("p (k n) -> p k n", k=kc)

        T0, nt, MOD_TILES = {}, 0, {}
        next_of = {a: b for a, b in zip(layers, layers[1:])}
        for L in layers:
            if L == layers[0]:
                MOD_TILES[L] = list(range(nt, nt + 12))
                nt += 12
            T0[L, "in"] = nt
            ahead = L in next_of
            if L == 1:
                per_group = 7 if ahead else 4
                if ahead:
                    MOD_TILES[next_of[L]] = [nt + 7 * g + 4 + s for g in range(SSM_G) for s in range(3)]
                nt += SSM_G * per_group
            else:
                nt += {0: 3, 2: 4, 3: 3}[L]
                if ahead:
                    MOD_TILES[next_of[L]] = list(range(nt, nt + 12))
                    nt += 12
            for name, n in [("out", 4 if L == 1 else 2), ("up", 8 if L < 2 else 11), ("down", 8)]:
                T0[L, name] = nt
                nt += n
        NTILES = nt

        def v(base, i, per):
            return base if i is None else base + i * per

        wfull = [S("weights_in_0"), S("weights_in_1")]
        wused = S("weights_used")

        class Flow:

            def __init__(self, name, slots):
                self.full, self.free, self.slots = S(name + "_full"), S(name + "_free"), slots

        class Link:

            def __init__(self, eng, name):
                self.eng, self.sem, self.n, self.i, self.per = eng, S(name), 0, None, 0

            def __call__(self, ins):
                self.n += 1
                ins.then_inc(self.sem, 1)
                self.eng.wait_ge(self.sem, v(self.n, self.i, self.per))
                return ins

            def go(self, ins):
                self.n += 1
                return ins.then_inc(self.sem, 1)

            def settle(self):
                self.eng.wait_ge(self.sem, self.n)

            def begin(self, i, per):
                self.i, self.per, self.start = i, per, self.n

            def end(self, count):
                assert self.n - self.start == self.per, (self.n - self.start, self.per)
                self.n = self.start + self.per * count
                self.i = None

        def tiles_of(L):
            return (TL, 1) if L in (1, 3) else (NT, 2)

        MOD_ROWS = {0: RES_TMP[:, :], 1: BIG[:, 24064:24576], 2: RES_TMP[:, :]}
        MOD_ROWS_START = BIG[:, 0:1024].rearrange("p (s n) -> p s n", s=2)
        BIAS_ROWS = UT[0:48, 0, 0:128]
        DIAGONALS = BIG[:, 6144:10240].rearrange("p (a k n) -> p a k n", a=4, k=KD)

        block = ctxs.enter_context(nc.Block())

        @block.sync
        def _(sp):
            state = {"t": 0}

            def load(dst, src, i=None, per=0):
                t = state["t"]
                if t >= 2:
                    sp.wait_ge(wused, v(t - 1, i, per))
                sp.dma_start(dst, src).then_inc(wfull[t % 2], 16)
                state["t"] += 1

            def columns(w, n_outer, per=2, cols=512):
                wv = w.rearrange("(k p) n -> p k n", p=128)
                first = 0
                if state["t"] == 0:
                    for s in range(per):
                        load(ring(s), wv[:, :, s * 512:(s + 1) * 512])
                    first = 1
                with sp.Fori(first, n_outer, 1) as i:
                    for s in range(per):
                        off = (i * per + s) * 512
                        load(ring(state["t"] % 2), wv[:, :, bass.ds(off, 512)], i - first, per)
                state["t"] += (n_outer - first - 1) * per

            def halves(w, parts):
                wv = w.rearrange("(k p) n -> p k n", p=128)
                if len(parts) % 2:
                    for h in range(2):
                        k0 = 0
                        for kc in parts:
                            load(ring(state["t"] % 2, kc), wv[:, k0:k0 + kc, h * 512:(h + 1) * 512])
                            k0 += kc
                    return
                with sp.Fori(0, 2, 1) as i:
                    k0 = 0
                    for kc in parts:
                        load(ring(state["t"] % 2, kc), wv[:, k0:k0 + kc, bass.ds(i * 512, 512)], i, len(parts))
                        k0 += kc
                state["t"] += len(parts)

            def mod_weights(L):
                return (d["w_mod"] if L < 2 else d["w_mod_2"])[L % 2]

            def mod_ahead(L):
                if L in next_of:
                    columns(mod_weights(next_of[L]), 6)

            for L in layers:
                if L == layers[0]:
                    columns(mod_weights(L), 6)
                if L == 0:
                    wv = d["att_w_in"][0].rearrange("(k p) n -> p k n", p=128)
                    for s in range(3):
                        load(ring(state["t"] % 2), wv[:, :, s * 512:(s + 1) * 512])
                    mod_ahead(L)
                    halves(d["att_w_out"][0], [8])
                elif L == 1:
                    wv = d["ssm_w_in"][0].rearrange("(k p) n -> p k n", p=128)
                    for g in range(SSM_G):
                        b0 = 2 * SSM_DI + g * SSM_N
                        for c0, n in ((b0, 128), (b0 + 512, 128), (SSM_DI + g * 512, 512), (g * 512, 512)):
                            load(ring(state["t"] % 2, 8, n), wv[:, :, c0:c0 + n])
                        if L in next_of:
                            mv = mod_weights(next_of[L]).rearrange("(k p) n -> p k n", p=128)
                            for s in range(3):
                                load(ring(state["t"] % 2), mv[:, :, (3 * g + s) * 512:(3 * g + s + 1) * 512])
                    halves(d["ssm_w_out"][0], [8, 8])
                elif L == 2:
                    wv = d["w_even_in_2"][0].rearrange("(k p) n -> p k n", p=128)
                    for s in range(4):
                        load(ring(state["t"] % 2), wv[:, :, s * 512:(s + 1) * 512])
                    mod_ahead(L)
                    halves(d["w_even_out_2"][0], [8])
                else:
                    wv = d["w_qkv_2"][0].rearrange("(k p) n -> p k n", p=128)
                    for s in range(3):
                        load(ring(state["t"] % 2), wv[:, :, s * 512:(s + 1) * 512])
                    halves(d["w_att_out_2"][0], [8])
                if L < 2:
                    columns(d["ff_w1"][L], 4)
                    halves(d["ff_w2"][L], [8] * 4)
                else:
                    columns(d["w_ffn_up_2"][L - 2], 5)
                    wv = d["w_ffn_up_2"][L - 2].rearrange("(k p) n -> p k n", p=128)
                    load(ring(state["t"] % 2), wv[:, :, 5120:5632])
                    halves(d["w_ffn_down_2"][L - 2], F2_PARTS)
            assert state["t"] == NTILES
            ov = d["out"].rearrange("(t p) n -> p t n", p=128)
            if layers[-1] == 3:
                for t in range(TL):
                    sp.wait_ge(S("output_ready"), t + 1)
                    sp.dma_start(ov[:, t, :], H[:, t, :]).then_inc(S("output_stored"), 16)
                sp.wait_ge(S("output_stored"), 16 * TL)
            else:
                sp.wait_ge(S("layer_done"), len(layers))
                sp.dma_start(ov, H[:, 0:TL, :]).then_inc(S("output_stored"), 16)
                sp.dma_start(d["out_ctx"].rearrange("(t p) n -> p t n", p=128), H[:, TL:NT, :]).then_inc(S("output_stored"), 16)
                sp.wait_ge(S("output_stored"), 32)

        C_QK = big(0, 4, TOK)
        C_V = big(3072, NT, FW)
        C_R = big(6144, NT, FW)
        C_LA = big(9216, NT, 512)
        C_S = big(9216, 12, 256)
        C_BT = big(12288, 4, TOK)
        C_QB = big(15360, 4, TOK)
        C_MIX = big(18432, 8, TOK)
        C_KE = big(21504, NT, 512)
        C_X = big(0, NT, D)
        C_TABS = big(12288, d["c_four"].shape[1])
        C_UF = big(21504, 4, TOK)
        UTF = UT[:, :, :].rearrange("p a b -> p (a b)")
        C_EXP = UTF[:, 0:1792].rearrange("p (v a b) -> p v a b", v=7, a=2)
        C_QL = UTF[:, 1792:3584].rearrange("p (v a b) -> p v a b", v=7, a=2)
        C_KL = UTF[:, 3584:5376].rearrange("p (v a b) -> p v a b", v=7, a=2)
        C_T1, C_T2 = UTF[:, 0:3072], UTF[:, 3072:6144]
        C_JUNK = UTF[:, 5888:6016]
        C_O = GB[:, 0, 512:1024]
        C_MASK = UTF[:, 5376:5888].bitcast(mybir.dt.uint8).rearrange("p (d v i) -> p d v i", d=2, v=GLA_LEVELS)
        C_WZ = GB[:, 0, 256:384].rearrange("p (k n) -> p k n", k=8)
        C_WG = GB[:, 0, 512:1024]
        C_ZT = GB[:, 1, 0:TOK]
        C_AT = GB[:, 1, :].rearrange("p (d h i) -> p d h i", d=2, h=4)
        C_GAIN = RES_TMP[:, :]
        C_DL = GB[:, 0, 384:408].rearrange("p (a t) -> p a t", a=4)

        def four(name):
            x, n = at["c_four"][name]
            return C_TABS[:, x:x + n]

        def gla_orders():
            return ([4, 5, 0, 1, 2, 3], [5, 4, 3, 2, 1, 0])

        def level_views(dr, t, v_):
            m = 64 >> v_
            b = C_BT[:, 2 * dr:2 * dr + 2, t * 128:(t + 1) * 128].rearrange("p a (n m) -> p a n m", m=2 * m)
            r = m - 1 if dr == 0 else m
            ref = b[:, :, :, r:r + 1].to_broadcast([128, 2, 64 // m, 2 * m])
            e = C_EXP[:, v_].rearrange("p a (n m) -> p a n m", m=2 * m)
            return e, b, ref

        SSM_YT = big(0, 16, LAT)

        SN = big(8192, 9, 512)
        SSM_XT = big(8192, 4, TOK)
        SSM_XDT = big(12800, 2, 2, 512)
        SSM_BT = big(12800, TOK)
        SSM_CT = big(14848, LAT)
        SSM_X = big(15360, NT, 512)
        SSM_WDT = big(15360, KD, 2 * SSM_H)
        SSM_BK = big(18432, NT, SSM_N)
        SSM_GM = big(19200, 2, TL, 128)
        SSM_T1 = big(20224, 512)
        SSM_DT = big(20736, NT, 64)
        SSM_A = big(21120, NT, 64)
        SSM_WD = big(21504, NT, 64)
        SSM_EACS = big(21888, NT, 64)
        SSM_ETOT = big(22272, NT, 64)
        SSM_ACS = big(22656, NT, 64)
        SSM_DTB = big(23040, 64)
        SSM_ALOG = big(23104, 64)
        SSM_DSK = big(23168, 32)
        SSM_CW = big(23200, 6, 24)
        SSM_XW = GB[:, 0, :].rearrange("p (s n) -> p s n", s=2)
        SSM_DM = GB[:, :, :].rearrange("p a (s n) -> p (a s) n", s=2)
        SSM_T2 = RES_TMP[:, :]
        SSM_NG = H[:, TL:NT, :].rearrange("p t n -> p (t n)")

        def ssm_z(t):
            return GATE[:, t // 2, 1, t % 2 * 512:t % 2 * 512 + 512]

        SSM_ORDERS = ([4, 5, 0, 1, 2, 3], [5, 4, 3, 2, 1, 0])

        def sn_slot(dr, j):
            return 8 if j == 1 else dr * 4 + j - 2

        def by_head(a, n=8):
            return a.rearrange("p (h e) -> p h e", h=n)

        flows = {}
        SHARED = {(0, "v"): "tiles_to_vector", (1, "dt"): "tiles_to_vector", (1, "acs"): "tiles_to_vector", (2, "kt"): "tiles_to_vector",
                  (0, "q"): "chunks_to_scalar", (2, "uf"): "chunks_to_scalar", (2, "qk"): "chunks_to_scalar",
                  (1, "conv"): "chunks_to_vector", (2, "bt"): "chunks_to_vector",
                  (1, "z"): "latent_tiles_to_scalar", (3, "q"): "latent_tiles_to_scalar",
                  (2, "la"): "tiles_to_scalar", (2, "ec"): "tiles_to_scalar", (3, "kv"): "tiles_to_scalar",
                  (1, "xt"): "turned_to_scalar", (2, "ft"): "turned_to_scalar", (3, "turned"): "turned_to_scalar",
                  (1, "state"): "pairs_to_vector", (2, "fx"): "pairs_to_vector", (2, "st"): "pairs_to_vector"}

        def flow(L, name, slots):
            if name in ("mod_rows", "mod_columns", "bias", "gates", "um_v", "um_s", "uf_v", "uf_s"):
                key = name
            elif name in ("mixed", "down"):
                key = f"{name}_{slots}"
            elif name == "up":
                key = name + ("_squared" if L < 2 else "_conv")
            else:
                key = SHARED.get((L, name), name if name in ("scores", "probsT", "heads") else f"L{L}_{name}")
            if key not in flows:
                flows[key] = Flow(key, slots)
            return flows[key]

        A_Q = big(0, 8, TOK)
        A_QR = big(6144, 8, LAT)
        CONV_W2 = GB[:, 0, 0:4 * 2 * NF2].rearrange("p (a j) -> p a j", a=4)
        CONV_Y = big(NF2 * TOK, 2, TOK)
        SQ_TMP = GB[:, 1, :]
        second = [L for L in layers if L >= 2]
        first = [L for L in layers if L < 2]
        NORM_FINAL = 64 * len(first) + 16

        A_KD = big(10240, GA, TOK)
        A_KC = big(13312, 2, TOK)
        A_V = big(14848, NT, GA * DA)
        A_CONST = big(16384, d["c_att"].shape[1])
        A_P = big(18048, 2, 768)
        A_PT = big(19584, 2, 768)
        A_O = big(21120, 2, D)
        A_SINK = big(23168, HA)
        A_ROT = big(23184, LAT)

        B_QK = big(0, NT, 1280)
        B_QT = big(7680, HB_, LAT)
        B_KT = big(11776, GB_, TOK)
        B_V = big(13312, NT, GB_ * DB)
        B_CONST = big(14848, 512)
        B_P = big(15360, 2, 768)
        B_PT = big(16896, 2, 768)
        B_O = big(18432, 2, D)
        B_SQ = big(20480, 1280)
        B_G = big(21760, 256)
        B_T2 = big(22016, 1280)

        def catt(name):
            x, n = at["c_att"][name]
            return A_CONST[:, x:x + n]

        def att_units(L):
            units = []
            if L == 0:
                for t in range(NT):
                    for h in range(HA):
                        g, half = h // 4, (h % 2) * 64
                        rows = slice(half, half + 64)
                        ql = A_Q[rows, h // 2, t * 128:(t + 1) * 128]
                        vg = slice(g * DA, (g + 1) * DA)
                        cprod = (512, 256, ql, A_KD[rows, g, LAT:TOK])
                        cvals = [A_V[:, TL + j, vg] for j in range(TC)]
                        if t >= TL:
                            units.append(dict(t=t, h=h, first=512, prods=[cprod], masks=[], vals=cvals))
                            continue
                        k0, k1 = max(t - 1, 0), min(t + 2, TL)
                        n = (k1 - k0) * 128
                        first = 512 - n
                        qr = A_QR[rows, h // 2, t * 128:(t + 1) * 128]
                        masks = []
                        if t > 0:
                            masks.append((first, "maskl"))
                        if t < TL - 1:
                            masks.append((384, "maskr"))
                        units.append(dict(t=t, h=h, first=first, masks=masks,
                                          prods=[(first, n, qr, A_KD[rows, g, k0 * 128:k1 * 128]), cprod],
                                          vals=[A_V[:, k, vg] for k in range(k0, k1)] + cvals))
            else:
                for t in range(TL):
                    for h in range(HB_):
                        g = h // 4
                        q = B_QT[:, h, t * 128:(t + 1) * 128]
                        units.append(dict(t=t, h=h, first=0, masks=[],
                                          prods=[(0, 512, q, B_KT[:, g, 0:512]), (512, 256, q, B_KT[:, g, 512:768])],
                                          vals=[B_V[:, k, g * DB:(g + 1) * DB] for k in range(NT)]))
            return units

        def att_frame(L):
            if L == 0:
                return HA, DA, A_P, A_PT, A_O, DA ** -0.5
            return HB_, DB, B_P, B_PT, B_O, DB ** -0.5

        def mod_tiles_before(L):
            return 12 * layers.index(L)

        def nth(L):
            return layers.index(L) + 1

        def tokens_so_far(L):
            return sum(tiles_of(l)[0] for l in layers[:layers.index(L) + 1])

        def units_before(L):
            return NT * HA if L == 3 and 0 in layers else 0

        def turns_ahead(L):
            return NT if L == 3 and 0 in layers else 0

        def o_slot(n, dv):
            return bank(6, dv)

        def turn_step(L, t):
            return (t + 1) * att_frame(L)[0] + 3

        def turns_before(L, step):
            return max(0, (step - 4) // att_frame(L)[0])

        def nth_probsT(L, n):
            return n + 1 + turns_before(L, n + 1)

        def nth_turn(L, t, n):
            return min(turn_step(L, t), n) + t + 1

        @block.tensor
        def _(pe):
            mm, tr = nc.tensor.matmul, nc.tensor.transpose
            taken = {}
            start = {}
            settled = []

            def place(f, i=None, per=0):
                taken[f] = taken.get(f, 0) + 1
                pe.wait_ge(f.free, v(taken[f], i, per))
                return (taken[f] - start.get(f, 0) - 1) % f.slots

            def stage(*fs):
                for f in settled:
                    pe.wait_ge(f.free, taken[f] + f.slots)
                settled[:] = fs
                for f in fs:
                    start[f] = taken.get(f, 0)

            def weights(t, i=None, per=0):
                pe.wait_ge(wfull[t % 2], v(16 * (t // 2 + 1), i, 8 * per))
                return t % 2

            def used(ins):
                ins.then_inc(wused, 1)

            def mod_rows(L, m, bank_, alone=True):
                fr, fc = flow(L, "mod_rows", 2), flow(L, "mod_columns", 1)
                if alone and m:
                    pe.wait_ge(fc.free, taken[fc] + 1)
                place(fr)
                t = MOD_TILES[L][m]
                w = ring(weights(t))
                lc = 0 if L < 2 else 2
                for k in range(KD):
                    ins = mm(bank(bank_)[0:2, :], CV[:, k, lc:lc + 2], w[:, k, :], start=k == 0, stop=k == KD - 1)
                used(ins)

            def mod_columns(L, m, bank_, rows):
                fr, fc = flow(L, "mod_rows", 2), flow(L, "mod_columns", 1)
                pe.wait_ge(fr.free, mod_tiles_before(L) + m + 1 + fr.slots)
                place(fc)
                for c in range(4):
                    ins = tr(bank(bank_, 2, 2 * c), rows[0:2, c * 128:(c + 1) * 128], ident[0:2, 0:2])
                ins.then_inc(fc.full, 1)

            def modulation_start(L):
                fr, fc = flow(L, "mod_rows", 2), flow(L, "mod_columns", 1)
                stage(fr, fc)
                pe.wait_ge(S("conditioning_ready"), 1)
                for m in range(13):
                    if m < 12:
                        mod_rows(L, m, 5 + m % 2, alone=False)
                    if m:
                        mod_columns(L, m - 1, 7, MOD_ROWS_START[:, (m - 1) % 2, :])

            def mod_flows_too(L):
                if L in next_of:
                    settled.extend([flow(L, "mod_rows", 2), flow(L, "mod_columns", 1)])

            def bias_columns(L):
                f = flow(L, "bias", 1)
                stage(f)
                pe.wait_ge(S("mod_bias_in"), 16 * nth(L))
                place(f)
                tr(bank(0, 48), BIAS_ROWS, ident[0:48, 0:48]).then_inc(f.full, 1)

            def gates(L):
                f = flow(L, "gates", 4)
                stage(f)
                for a in range(4):
                    pe.wait_ge(S("diagonals_ready"), 4 * nth(L) - 3 + a)
                    b = 2 * place(f)
                    for h in range(2):
                        m = mm(bank(b + h), ones, DIAGONALS[:, a, 4 * h:4 * h + 4, :], start=True, stop=True)
                    m.then_inc(f.full, 1)

            def transposed_input(L, which, src):
                nt_, _ = tiles_of(L)
                if L == 1 and which == "m" or L == 3 and which == "m":
                    nt_ = NT
                a, b = flow(L, "u" + which + "_v", 2), flow(L, "u" + which + "_s", 2)
                stage(a, b)
                pe.wait_ge(S(f"{which}_tokens_ready"), NT * nth(L) if which == "m" else tokens_so_far(L))
                for k in range(KD):
                    f = (a, b)[k % 2]
                    x = (2 * place(f) + k % 2) * 1024
                    for t in range(nt_):
                        m = tr(PS[:, x + t * 128:x + (t + 1) * 128], src[:, t, k * 128:(k + 1) * 128], ident)
                    m.then_inc(f.full, 1)

            def by_channel(t, f, n, chunks, last_used=True, i=None, per=0, done=0, nlat=LAT, nctx=CTX):
                slot = weights(t, i, per)
                w = ring(slot, 8, 512 if chunks[-1] >= 1 else 128)
                for c in chunks:
                    x = place(f, i, done) * 1024
                    for k in range(KD):
                        a = w[:, k, c * 128:(c + 1) * 128]
                        if nlat:
                            m = mm(PS[:, x:x + nlat], a, UT[:, k, 0:nlat], start=k == 0, stop=k == KD - 1)
                        if nctx:
                            m = mm(PS[:, x + 512:x + 512 + nctx], a, UT[:, k, LAT:LAT + nctx], start=k == 0, stop=k == KD - 1)
                    if last_used and c == chunks[-1]:
                        used(m)
                    else:
                        m.then_inc(f.full, 1)

            def by_token(t0, parts, f, inp, ntok, cols=(0, 512), wcols=512, i=None, per=0, done=0):
                k0, kn = 0, sum(parts)
                for j, kc in enumerate(parts):
                    w = ring(weights(t0 + j, i, per), kc, wcols)
                    for k in range(kc):
                        kk = k0 + k
                        for t in range(ntok):
                            if kk == 0:
                                place(f, i, done)
                            m = mm(PS[:, t * 512:t * 512 + cols[1] - cols[0]], inp[:, kk, t * 128:(t + 1) * 128],
                                   w[:, k, cols[0]:cols[1]], start=kk == 0, stop=kk == kn - 1)
                            if kk == kn - 1 and t < ntok - 1:
                                m.then_inc(f.full, 1)
                    used(m)
                    k0 += kc

            def both_halves(L, name, parts, inp, f):
                t0 = T0[L, name]
                ntok, _ = tiles_of(L)
                n = len(parts)
                if n % 2:
                    for h in range(2):
                        by_token(t0 + h * n, parts, f, inp, ntok)
                else:
                    with pe.Fori(0, 2, 1) as i:
                        by_token(t0, parts, f, inp, ntok, i=i, per=n, done=ntok)
                    taken[f] += ntok

            def up(L, n_outer, f):
                t0 = T0[L, "up"]
                nctx = CTX if tiles_of(L)[0] == NT else 0
                with pe.Fori(0, n_outer, 1) as i:
                    for s in range(2):
                        by_channel(t0 + s, f, 0, range(4), i=i, per=2, done=8, nctx=nctx)
                taken[f] += 8 * (n_outer - 1)
                if L >= 2:
                    by_channel(t0 + 10, f, 0, range(4), nctx=nctx)

            def attend(L):
                heads, dv, P, PT, O, _ = att_frame(L)
                units = att_units(L)
                n = len(units)
                sf, tf, of = flow(L, "scores", 2), flow(L, "probsT", 1), flow(L, "heads", 1)
                stage(sf, tf, of)
                if L == 0:
                    pe.wait_ge(S("L0_keys_ready"), 1)
                u0, x0 = units_before(L), turns_ahead(L)
                ahead = L in next_of
                mod_flows_too(L)
                for step in range(n + 4):
                    if ahead and step % 8 == 3 and step < n:
                        mod_rows(next_of[L], step // 8, 7)
                    if ahead and step % 8 == 6 and step < n:
                        mod_columns(next_of[L], step // 8, 7, MOD_ROWS[L])
                    if step < n:
                        u = units[step]
                        x = place(sf) * 1024
                        for j, (col, w, a, b) in enumerate(u["prods"]):
                            m = mm(PS[:, x + col:x + col + w], a, b, start=True, stop=True)
                        m.then_inc(sf.full, 1)
                    if 1 <= step <= n:
                        u = units[step - 1]
                        pe.wait_ge(S("probs_ready"), u0 + step)
                        place(tf)
                        for j in range(len(u["vals"])):
                            m = tr(bank(4, 128, j * 128), P[:, (step - 1) % 2, u["first"] + j * 128:u["first"] + (j + 1) * 128], ident)
                        m.then_inc(tf.full, 1)
                    if 2 <= step <= n + 1:
                        u = units[step - 2]
                        pe.wait_ge(tf.free, 1 + u0 + x0 + nth_probsT(L, step - 2))
                        place(of)
                        for j, val in enumerate(u["vals"]):
                            m = mm(o_slot(step - 2, dv), PT[:, (step - 2) % 2, j * 128:(j + 1) * 128], val,
                                   start=j == 0, stop=j == len(u["vals"]) - 1)
                        m.then_inc(of.full, 1)
                    t = step // heads - 1
                    if t >= 0 and step == turn_step(L, t):
                        pe.wait_ge(of.free, of.slots + u0 + (t + 1) * heads)
                        place(tf)
                        for j in range(KD):
                            m = tr(bank(4, 128, j * 128), O[:, t % 2, j * 128:(j + 1) * 128], ident)
                        m.then_inc(tf.full, 1)
                        assert taken[tf] == u0 + x0 + nth_turn(L, t, n)

            def mixer0():
                t0 = T0[0, "in"]
                f, g, r = flow(0, "q", 4), flow(0, "v", NT), flow(0, "rot", 1)
                stage(f)
                by_channel(t0, f, 0, range(4))
                by_channel(t0 + 1, f, 0, range(4))
                by_channel(t0 + 2, f, 0, range(2), last_used=False)
                stage(g)
                by_token(t0 + 2, [8], g, UT, NT, cols=(256, 512))
                stage(r)
                pe.wait_ge(S("attention_constants_in"), 32)
                for c in range(10):
                    place(r)
                    src = A_Q[:, c, 0:LAT] if c < 8 else A_KC[:, c - 8, 0:LAT]
                    mm(bank(7), catt("swap"), src, start=True, stop=True).then_inc(r.full, 1)
                attend(0)


            def mixer2():
                t0 = T0[2, "in"]
                f = flow(2, "uf", 4)
                stage(f)
                by_channel(t0, f, 0, range(4))
                f = flow(2, "fx", 2)
                stage(f)
                pe.wait_ge(S("fourier_tables_in"), 16)
                for t in range(NT):
                    x = place(f) * 1024
                    for g in range(4):
                        m = mm(PS[:, x + g * 256:x + (g + 1) * 256], C_UF[:, g, t * 128:(t + 1) * 128], four("dftd"), start=True, stop=True)
                    m.then_inc(f.full, 1)
                f = flow(2, "ft", 2)
                stage(f)
                for g in range(4):
                    x = place(f) * 1024
                    for a, n, tt, kinds in ((0, LAT, range(TL), ("cosl", "sinl")), (512, CTX, range(TL, NT), ("cosc", "sinc"))):
                        for j, t in enumerate(tt):
                            for w, kind in enumerate(kinds):
                                m = mm(PS[:, x + a:x + a + n], C_X[:, t, g * 256 + w * 128:g * 256 + (w + 1) * 128],
                                       four(kind)[:, j * n:(j + 1) * n], start=j + w == 0, stop=j == len(tt) - 1 and w == 1)
                    m.then_inc(f.full, 1)
                f = flow(2, "qk", 4)
                stage(f)
                by_channel(t0 + 1, f, 0, range(4))
                f = flow(2, "z", 1)
                stage(f)
                pe.wait_ge(S("gate_weights_in"), 80)
                place(f)
                for k in range(KD):
                    mm(PS[0:16, 0:LAT], C_WZ[:, k, :], UT[:, k, 0:LAT], start=k == 0, stop=k == KD - 1)
                    m = mm(PS[0:16, 512:512 + CTX], C_WZ[:, k, :], UT[:, k, LAT:TOK], start=k == 0, stop=k == KD - 1)
                m.then_inc(f.full, 1)
                f = flow(2, "vr", NT)
                stage(f)
                by_token(t0 + 2, [8], f, UT, NT)
                by_token(t0 + 3, [8], f, UT, NT)
                f = flow(2, "la", NT)
                stage(f)
                for t in range(NT):
                    mm(bank(place(f)), C_ZT[0:17, t * 128:(t + 1) * 128], C_WG[0:17, :], start=True, stop=True).then_inc(f.full, 1)
                f = flow(2, "bt", 4)
                stage(f)
                pe.wait_ge(S("L2_decays_ready"), 1)
                for a in range(4):
                    x = place(f) * 1024
                    for t in range(NT):
                        m = mm(PS[:, x + t * 128:x + (t + 1) * 128], C_LA[:, t, a * 128:(a + 1) * 128], cs(("upto", "downto")[a // 2]), start=True, stop=True)
                    m.then_inc(f.full, 1)
                f = flow(2, "ec", NT)
                stage(f)
                for t in range(NT):
                    b = place(f)
                    for dr in range(2):
                        m = mm(bank(b, 256, dr * 256), cs(("after", "before")[dr]), C_LA[:, t, dr * 256:(dr + 1) * 256], start=True, stop=True)
                    m.then_inc(f.full, 1)
                f = flow(2, "kt", NT)
                stage(f)
                for t in range(NT):
                    b = place(f)
                    for a in range(2):
                        m = tr(bank(b, 128, a * 128), C_QK[:, 2 + a, t * 128:(t + 1) * 128], ident)
                    m.then_inc(f.full, 1)
                f = flow(2, "st", 2)
                stage(f)
                for dr in range(2):
                    for t in gla_orders()[dr][:-1]:
                        b = place(f)
                        for h in range(GLA_H):
                            half = (h % 2) * 64
                            m = mm(PS[half:half + 64, b * 512 + (h // 2) * 128:b * 512 + (h // 2) * 128 + 128],
                                   C_KE[:, t, dr * 256 + h * 64:dr * 256 + (h + 1) * 64], C_V[:, t, h * 128:(h + 1) * 128], start=True, stop=True)
                        m.then_inc(f.full, 1)
                lv, go, gt = flow(2, "levels", 2), flow(2, "mixed_heads", 1), flow(2, "turned", 1)
                stage(lv, go, gt)
                mod_flows_too(2)
                pe.wait_ge(S("L2_states_ready"), 1)

                def turn(t):
                    pe.wait_ge(S("L2_heads_ready"), t + 1)
                    b = 6 + place(gt)
                    for k in range(4):
                        m = tr(bank(b, 128, k * 128), C_O[:, k * 128:(k + 1) * 128], ident)
                    m.then_inc(gt.full, 1)

                for t in range(NT):
                    for dr in range(2):
                        pe.wait_ge(S("L2_levels_ready"), 2 * t + dr + 1)
                        for v_ in range(GLA_LEVELS):
                            b = place(lv) * 2
                            for h in (0, 1, 2, 3):
                                rows, a = slice((h % 2) * 64, (h % 2) * 64 + 64), h // 2
                                ts = slice(t * 128, (t + 1) * 128)
                                kk = C_KL[rows, v_, a, :] if v_ < 7 else C_QK[rows, 2 + a, ts]
                                qq = C_QL[rows, v_, a, :] if v_ < 7 else C_QK[rows, a, ts]
                                m = mm(bank(b + h % 2, 128, a * 128), kk, qq, start=True, stop=True)
                            m.then_inc(lv.full, 1)
                            if v_ == 3 and 2 in next_of and t + dr:
                                mod_columns(3, 2 * t + dr - 1, 7, MOD_ROWS[2])
                        if 2 in next_of:
                            mod_rows(3, 2 * t + dr, 7)
                    if t:
                        turn(t - 1)
                    pe.wait_ge(S("L2_attention_ready"), 2 * t + 2)
                    b = 4 + place(go)
                    first = [o[0] for o in gla_orders()]
                    for h in range(GLA_H):
                        rows, a = slice((h % 2) * 64, (h % 2) * 64 + 64), h // 2
                        ops = [(C_AT[:, dr, h % 2 * 2 + a, :], C_V[:, t, h * 128:(h + 1) * 128]) for dr in range(2)]
                        ops += [(C_QB[rows, 2 * dr + a, t * 128:(t + 1) * 128], C_S[rows, dr * 6 + t, a * 128:(a + 1) * 128])
                                for dr in range(2) if t != first[dr]]
                        for j, (x, y) in enumerate(ops):
                            m = mm(bank(b + h % 2, 128, a * 128), x, y, start=j == 0, stop=j == len(ops) - 1)
                    m.then_inc(go.full, 1)
                if 2 in next_of:
                    mod_columns(3, 11, 7, MOD_ROWS[2])
                turn(NT - 1)

            def mixer3():
                t0 = T0[3, "in"]
                f = flow(3, "q", TL)
                stage(f)
                by_token(t0, [8], f, UT, TL)
                by_token(t0 + 1, [8], f, UT, TL)
                f = flow(3, "kv", NT)
                stage(f)
                by_token(t0 + 2, [8], f, UT, NT)
                f = flow(3, "turned", 2)
                stage(f)
                for t in range(NT):
                    pe.wait_ge(S("L3_heads_normed"), t + 1)
                    for heads in ((range(8), range(8, 10)) if t < TL else (range(8, 10),)):
                        x = place(f) * 1024
                        for j, h in enumerate(heads):
                            m = tr(PS[:, x + j * 128:x + (j + 1) * 128], B_QK[:, t, h * 128:(h + 1) * 128], ident)
                        m.then_inc(f.full, 1)
                attend(3)

            def mixer1():
                f = flow(1, "dt", NT)
                stage(f)
                pe.wait_ge(S("ssm_vectors_in"), 160)
                for t in range(NT):
                    b = place(f)
                    for k in range(KD):
                        m = mm(bank(b, 64), UT[:, k, t * 128:(t + 1) * 128], SSM_WDT[:, k, :], start=k == 0, stop=k == KD - 1)
                    m.then_inc(f.full, 1)
                f = flow(1, "acs", NT)
                stage(f)
                pe.wait_ge(S("L1_a_ready"), 1)
                for t in range(NT):
                    b = place(f)
                    mm(bank(b, 32), cs("upto"), SSM_A[:, t, 0:32], start=True, stop=True)
                    mm(bank(b, 32, 32), cs("downto"), SSM_A[:, t, 32:64], start=True, stop=True)
                    mm(bank(b, 64, 64), ones, SSM_A[:, t, :], start=True, stop=True).then_inc(f.full, 1)
                cv, z, xt = flow(1, "conv", 4), flow(1, "z", TL), flow(1, "xt", 2)
                gf, sf, df, of, yf, tf = (flow(1, "bc", 1), flow(1, "state", 2), flow(1, "decay", 2), flow(1, "off", 1),
                                          flow(1, "diag", 1), flow(1, "turned", 1))
                for g in range(SSM_G):
                    t0 = T0[1, "in"] + per_group * g
                    stage(cv)
                    by_channel(t0, cv, 0, range(1))
                    by_channel(t0 + 1, cv, 0, range(1), nctx=0)
                    by_channel(t0 + 2, cv, 0, range(4))
                    stage(z, xt)
                    by_token(t0 + 3, [8], z, UT, TL)
                    for n in range(5):
                        pe.wait_ge(S("L1_channels_ready"), 6 * g + (2 + n + 1 if n < 4 else 1))
                        x = 2048 + place(xt) * 1024
                        src = SSM_XT[:, n, :] if n < 4 else SSM_BT
                        for t in range(NT):
                            m = tr(PS[:, x + t * 128:x + (t + 1) * 128], src[:, t * 128:(t + 1) * 128], ident)
                        m.then_inc(xt.full, 1)
                    stage(gf, sf, df, of, yf, tf)
                    mod_flows_too(1)
                    place(gf)
                    for c in range(TL):
                        cc = slice(c * 128, (c + 1) * 128)
                        m = mm(bank(0, 128, c * 128), SSM_BT[:, cc], SSM_CT[:, cc], start=True, stop=True)
                    m.then_inc(gf.full, 1)
                    for n in range(10):
                        c = SSM_ORDERS[n // 5][n % 5]
                        pe.wait_ge(S("L1_state_input_ready"), 10 * g + n + 1)
                        b = 1 + place(sf)
                        mm(bank(b), SSM_BK[:, c, :], SSM_XW[:, n % 2, :], start=True, stop=True).then_inc(sf.full, 1)

                    def turn(c):
                        pe.wait_ge(S("L1_normed"), TL * g + c + 1)
                        if c == 0:
                            pe.wait_ge(gf.free, 1 + taken[gf])
                        place(tf)
                        for k in range(4):
                            m = tr(bank(0, 128, k * 128), SSM_T1[:, k * 128:(k + 1) * 128], ident)
                        m.then_inc(tf.full, 1)

                    def sums(k):
                        q = k % 4
                        b = 3 + place(df)
                        for dr in range(2):
                            for hh in range(2):
                                col = dr * 32 + g * 8 + 2 * q + hh
                                m = mm(bank(b, 128, (2 * dr + hh) * 128), SSM_A[:, k // 4, col:col + 1].to_broadcast([128, 128]),
                                       cs(("upto", "downto")[dr]), start=True, stop=True)
                        m.then_inc(df.full, 1)

                    sums(0)
                    sums(1)
                    for k in range(16):
                        c, q = k // 4, k % 4
                        if k + 2 < 16:
                            sums(k + 2)
                        pe.wait_ge(S("L1_weights_ready"), 16 * g + k + 1)
                        if q == 0:
                            place(yf)
                        for hh in range(2):
                            h = 2 * q + hh
                            for dr in range(2):
                                m = mm(bank(5, 64, h * 64), SSM_DM[:, k % 4, (2 * dr + hh) * 128:(2 * dr + hh + 1) * 128],
                                       SSM_XDT[:, c % 2, dr, h * 64:(h + 1) * 64], start=dr == 0, stop=dr == 1)
                        m.then_inc(S("L1_weights_used"), 1)
                        if q == 1:
                            if c == 0:
                                pe.wait_ge(S("L1_states_ready"), g + 1)
                            place(of)
                            for dr in range(2):
                                sn = sn_slot(dr, c + 2 if dr == 0 else 5 - c)
                                m = mm(bank(6 + dr), SSM_CT[:, c * 128:(c + 1) * 128], SN[:, sn, :], start=True, stop=True)
                            m.then_inc(of.full, 1)
                        if q == 2 and c:
                            turn(c - 1)
                        if q == 3 and c < 3 and 1 in next_of:
                            mod_rows(next_of[1], 3 * g + c, 1)
                        if q == 2 and c and 1 in next_of:
                            mod_columns(next_of[1], 3 * g + c - 1, 1, MOD_ROWS[1])
                    turn(TL - 1)

            pe.wait_ge(S("constants_in"), 16)
            for L in layers:
                if L == layers[0]:
                    modulation_start(L)
                bias_columns(L)
                norm = L >= 2
                transposed_input(L, "m", big(0, NT, D) if norm else H)
                gates(L)
                (mixer0, mixer1, mixer2, mixer3)[L]()
                f = flow(L, "mixed", tiles_of(L)[0])
                stage(f)
                if L == 1:
                    both_halves(L, "out", [8, 8], SSM_YT, f)
                else:
                    both_halves(L, "out", [8], C_MIX if L == 2 else UT, f)
                transposed_input(L, "f", big(0, NT, D) if norm else H)
                f = flow(L, "up", 4)
                stage(f)
                up(L, 4 if L < 2 else 5, f)
                f = flow(L, "down", tiles_of(L)[0])
                stage(f)
                pe.wait_ge(S("hidden_ready"), nth(L))
                both_halves(L, "down", [8] * 4 if L < 2 else F2_PARTS, big(0, 32 if L < 2 else NF2, TOK), f)

        def rounds(n):
            return range(n)

        @block.vector
        def _(dve):
            V = nc.vector
            step = Link(dve, "vector_steps")
            got = {}
            fulls = {}

            def offer(f):
                if f in got:
                    return
                dve.sem_inc(f.free, f.slots)
                got[f] = 0
                fulls[f] = 0

            def ready(f, tile=None, i=None, per=0, tper=0):
                if tile is None:
                    fulls[f] += 1
                    dve.wait_ge(f.full, v(fulls[f], i, per))
                else:
                    dve.wait_ge(wused, v(tile + 1, i, tper))

            def give(f, ins, i=None, per=0):
                got[f] += 1
                ins.then_inc(f.free, 1)
                dve.wait_ge(f.free, v(f.slots + got[f], i, per))

            def post(name, n=1):
                dve.sem_inc(S(name), n)

            def modulation(L):
                f = flow(L, "bias", 1)
                offer(f)
                ready(f)
                dve.wait_ge(S("mod_sums_ready"), 12 * nth(L))
                give(f, V.tensor_tensor(MODC[:, :, :], MODC[:, :, :], bank(0, 48).unsqueeze(2).to_broadcast([128, 48, 2]), ALU.add))
                for a, seg in enumerate((0, 1, 3, 4)):
                    step.go(V.tensor_scalar(COL[:, a], MODC[:, seg * KD:(seg + 1) * KD, :], float(a % 2), None, ALU.add))
                if L >= 2:
                    dve.wait_ge(S("norm_gains_in"), 32 * (second.index(L) + 1))
                    step.settle()
                    for w in range(2):
                        step.go(V.tensor_tensor(COL[:, 2 * w + 1], COL[:, 2 * w + 1], GCOL[:, w, :].unsqueeze(2).to_broadcast([128, KD, 2]), ALU.mult))
                step.settle()
                post("columns_ready")

            def gates(L):
                for a in range(4):
                    seg = (2, 5)[a // 2]
                    step(V.tensor_tensor(DIAGONALS[:, a], ident.unsqueeze(1).to_broadcast([128, KD, 128]),
                                         MODC[:, seg * KD:(seg + 1) * KD, a % 2].unsqueeze(2).to_broadcast([128, KD, 128]), ALU.mult))
                    post("diagonals_ready")

            def transposed_input(L, which):
                f = flow(L, "u" + which + "_v", 2)
                offer(f)
                _, pieces = tiles_of(L)
                if which == "m":
                    pieces = 2
                w = 2 * (which == "f")
                for k in range(0, KD, 2):
                    ready(f)
                    x = (k // 2 % 2) * 2048
                    for p in range(pieces):
                        a, n = ((0, LAT), (LAT, CTX))[p]
                        ins = V.tensor_scalar(UT[:, k, a:a + n], PS[:, x + a:x + a + n], COL[:, w + 1, k, p:p + 1], COL[:, w, k, p:p + 1], ALU.mult, ALU.add)
                        if p == pieces - 1:
                            give(f, ins)
                        else:
                            step(ins)

            def residual(L, which, f, t0, n, uses):
                ntok, _ = tiles_of(L)
                gi = 0 if which == "m" else 1
                tmp = RES_TMP[:, :]
                offer(f)
                for h in range(2):
                    for t in range(ntok):
                        if t == ntok - 1:
                            ready(f, t0 + (h + 1) * n - 1)
                        else:
                            ready(f)
                        lc = 1 if t >= TL else 0
                        hs = slice(h * 512, (h + 1) * 512)
                        give(f, V.tensor_tensor(tmp, bank(t), GATE[:, gi, lc, hs], ALU.mult))
                        if L < 2:
                            step(V.scalar_tensor_tensor(H[:, t, hs], H[:, t, hs], ALPHA, tmp, ALU.mult, ALU.add))
                            step(V.bn_stats(ST[:, t * 12 + h * 6:t * 12 + h * 6 + 6], H[:, t, hs]))
                        else:
                            step(V.tensor_tensor(H[:, t, hs], H[:, t, hs], tmp, ALU.add))
                            if h == 1 and (which == "m" or L == 3):
                                post(f"{which}_residual_ready")
                if L >= 2:
                    return
                for t in range(ntok):
                    step(V.bn_aggr(ST[:, 80 + 2 * t:82 + 2 * t], ST[:, t * 12:t * 12 + 12]))
                mv = ST[:, 80:80 + 2 * ntok].rearrange("p (t a) -> p t a", a=2)
                step(V.tensor_scalar(ST[:, 96:96 + ntok], mv[:, :, 1], LN_EPS, None, ALU.add))
                post("variance_ready")
                dve.wait_ge(S("deviation_ready"), 2 * layers.index(L) + 1 + gi)
                step(V.reciprocal(ST[:, 104:104 + ntok], ST[:, 112:112 + ntok]))
                dve.wait_ge(S("norm_vectors_in"), 32 * (2 * layers.index(L) + 1 + gi))
                for t in range(ntok):
                    ht = H[:, t, :]
                    step(V.scalar_tensor_tensor(ht, ht, mv[:, t, 0:1], GB[:, 0, :], ALU.subtract, ALU.mult))
                    step(V.scalar_tensor_tensor(ht, ht, ST[:, 104 + t:105 + t], GB[:, 1, :], ALU.mult, ALU.add))
                    if which == "m":
                        post("f_tokens_ready")
                post("norm_vectors_used")

            def rms_input(L, which, ntok):
                dve.wait_ge(S(f"{which}_rms_ready"), second.index(L) + 1)
                step(V.reciprocal(ST[:, 104:104 + ntok], ST2[:, 8:8 + ntok]))
                out = big(0, NT, D)
                for t in range(ntok):
                    step(V.tensor_scalar(out[:, t, :], H[:, t, :], ST[:, 104 + t:105 + t], None, ALU.mult))
                    post(f"{which}_tokens_ready")

            def attend(L):
                heads, dv, P, PT, O, scale = att_frame(L)
                units = att_units(L)
                n = len(units)
                sf, of = flow(L, "scores", 2), flow(L, "heads", 1)
                offer(of)
                got.setdefault(sf, 0)
                fulls.setdefault(sf, 0)
                u0, x0 = units_before(L), turns_ahead(L)
                for k in range(n + 2):
                    if k < n:
                        u = units[k]
                        ready(sf)
                        x = (k % 2) * 1024
                        for col, name in u["masks"]:
                            step(V.tensor_tensor(PS[:, x + col:x + col + 128], PS[:, x + col:x + col + 128], catt(name), ALU.add))
                        step(V.reduce_max(ST[:, 128 + k % 8:129 + k % 8], PS[:, x + u["first"]:x + 768], AX.X))
                        neg = ST[:, 136 + k % 8:137 + k % 8]
                        if L == 0:
                            step(V.tensor_scalar(neg, ST[:, 128 + k % 8:129 + k % 8], A_SINK[:, u["h"]:u["h"] + 1], -scale, ALU.max, ALU.mult))
                        else:
                            step(V.tensor_scalar(neg, ST[:, 128 + k % 8:129 + k % 8], -scale, None, ALU.mult))
                        post("maxima_ready")
                    if k >= 2:
                        j = k - 2
                        u = units[j]
                        dve.wait_ge(S("probs_ready"), u0 + j + 1)
                        r = ST[:, 144 + j % 8:145 + j % 8]
                        if L == 0:
                            step(V.tensor_tensor(r, ST2[:, 16 + j % 8:17 + j % 8], ST2[:, 24 + j % 8:25 + j % 8], ALU.add))
                            step(V.reciprocal(r, r))
                        else:
                            step(V.reciprocal(r, ST2[:, 16 + j % 8:17 + j % 8]))
                        ready(of)
                        t = u["t"]
                        if u["h"] == 0 and t >= 2:
                            dve.wait_ge(flow(L, "probsT", 1).full, u0 + x0 + nth_turn(L, t - 2, n))
                        give(of, V.tensor_scalar(O[:, t % 2, u["h"] * dv:(u["h"] + 1) * dv], o_slot(j, dv), r, None, ALU.mult))

            def mixer0():
                g, r = flow(0, "v", NT), flow(0, "rot", 1)
                offer(g)
                for t in range(NT):
                    ready(g, T0[0, "in"] + 2 if t == NT - 1 else None)
                    give(g, V.tensor_copy(A_V[:, t, :], bank(t, 256)))
                offer(r)
                dve.wait_ge(S("attention_constants_in"), 32)
                step(V.tensor_scalar(A_SINK, A_SINK, float(DA) ** 0.5, None, ALU.mult))
                cosT, sinT = catt("cosT"), catt("sinT")
                for c in range(10):
                    ready(r)
                    give(r, V.tensor_tensor(A_ROT, bank(7), sinT, ALU.mult))
                    if c < 8:
                        step(V.tensor_tensor(A_QR[:, c, :], A_Q[:, c, 0:LAT], cosT, ALU.mult))
                        step(V.tensor_tensor(A_QR[:, c, :], A_QR[:, c, :], A_ROT, ALU.add))
                    else:
                        kc = A_KC[:, c - 8, 0:LAT]
                        step(V.tensor_tensor(kc, kc, cosT, ALU.mult))
                        step(V.tensor_tensor(kc, kc, A_ROT, ALU.add))
                for g_ in range(GA):
                    h0 = (g_ % 2) * 64
                    for h in range(2):
                        step(V.tensor_copy(A_KD[h * 64:h * 64 + 64, g_, :], A_KC[h0:h0 + 64, g_ // 2, :]))
                post("L0_keys_ready")
                attend(0)

            def mixer2():
                f = flow(2, "fx", 2)
                offer(f)
                for t in range(NT):
                    ready(f)
                    give(f, V.tensor_copy(C_X[:, t, :], PS[:, t % 2 * 1024:t % 2 * 1024 + 1024]))
                step(V.memset(C_ZT[0:17, :], 1.0))
                post("L2_ones_ready")
                f = flow(2, "vr", NT)
                offer(f)
                t0 = T0[2, "in"]
                for t in range(NT):
                    ready(f, t0 + 2 if t == NT - 1 else None)
                    give(f, V.tensor_copy(C_V[:, t, :], bank(t)))
                dve.wait_ge(S("gate_weights_in"), 80)
                for t in range(NT):
                    dve.wait_ge(S("L2_r_ready"), t + 1)
                    step(V.tensor_tensor(C_R[:, t, :], C_R[:, t, :], C_GAIN, ALU.mult))
                la = C_LA[:, :, :].rearrange("p t n -> p (t n)")
                dve.wait_ge(S("L2_logits_ready"), 1)
                step(V.scalar_tensor_tensor(C_T1, la, -1.0, la, ALU.mult, ALU.min))
                post("L2_minus_abs_ready")
                step(V.tensor_scalar(la, la, 0.0, 1.0 / 16.0, ALU.min, ALU.mult))
                dve.wait_ge(S("L2_log_ready"), 1)
                step(V.scalar_tensor_tensor(la, C_T1, -1.0 / 16.0, la, ALU.mult, ALU.add))
                post("L2_decays_ready")
                step(V.memset(GB[:, 1, :], 0.0))
                f = flow(2, "bt", 4)
                offer(f)
                for a in range(4):
                    ready(f)
                    give(f, V.tensor_copy(C_BT[:, a, :], PS[:, a * 1024:a * 1024 + TOK]))
                    post("L2_sums_ready")
                f = flow(2, "kt", NT)
                offer(f)
                for t in range(NT):
                    ready(f)
                    dve.wait_ge(flow(2, "ec", NT).free, NT + NT + t + 1)
                    step(V.tensor_tensor(C_KE[:, t, 0:256], C_KE[:, t, 0:256], bank(t, 256), ALU.mult))
                    give(f, V.tensor_tensor(C_KE[:, t, 256:512], C_KE[:, t, 256:512], bank(t, 256), ALU.mult))
                dve.wait_ge(S("L2_query_decay_ready"), 1)
                for dr in range(2):
                    qb = C_QB[:, 2 * dr:2 * dr + 2, :]
                    last = qb.rearrange("p a (t l) -> p a t l", l=128)[:, :, :, 127 * (1 - dr)]
                    step(V.tensor_copy(C_DL[:, 2 * dr:2 * dr + 2, :], last))
                    step(V.tensor_tensor(qb, qb, C_QK[:, 0:2, :], ALU.mult))
                f = flow(2, "st", 2)
                offer(f)
                n = 0
                for dr in range(2):
                    o = gla_orders()[dr]
                    for j in range(NT - 1):
                        ready(f)
                        new = C_S[:, dr * 6 + o[j + 1], :]
                        if j == 0:
                            give(f, V.tensor_copy(new, bank(n % 2, 256)))
                        else:
                            old = C_S[:, dr * 6 + o[j], :]
                            dl = lambda a: C_DL[:, 2 * dr + a, o[j]:o[j] + 1]
                            step(V.scalar_tensor_tensor(new[:, 0:128], old[:, 0:128], dl(0), bank(n % 2, 128), ALU.mult, ALU.add))
                            give(f, V.scalar_tensor_tensor(new[:, 128:256], old[:, 128:256], dl(1), bank(n % 2, 128, 128), ALU.mult, ALU.add))
                        n += 1
                post("L2_states_ready")
                lv, go = flow(2, "levels", 2), flow(2, "mixed_heads", 1)
                offer(lv)
                got[go] = fulls[go] = 0
                dve.sem_inc(go.free, 1)
                dve.wait_ge(S("gla_masks_in"), 16)

                def differences(n):
                    t, dr = n // 2, n % 2
                    for v_ in range(7):
                        e, b, ref = level_views(dr, t, v_)
                        step(V.tensor_tensor(e, b, ref, ALU.subtract))
                    post("L2_differences_ready")

                def products(n):
                    t = n // 2
                    ts = slice(t * 128, (t + 1) * 128)
                    dve.wait_ge(S("L2_level_decays_ready"), n + 1)
                    for dst, a in ((C_QL, 0), (C_KL, 2)):
                        step(V.tensor_tensor(dst, C_EXP, C_QK[:, a:a + 2, ts].unsqueeze(1).to_broadcast([128, 7, 2, 128]), ALU.mult))
                    post("L2_levels_ready")

                differences(0)
                products(0)
                for n in range(2 * NT):
                    t, dr = n // 2, n % 2
                    if n + 1 < 2 * NT:
                        differences(n + 1)
                    if t:
                        dve.wait_ge(go.full, t)
                    for v_ in range(GLA_LEVELS):
                        ready(lv)
                        b = (n * GLA_LEVELS + v_) % 2 * 2
                        data = PS[:, b * 512:b * 512 + 1024].rearrange("p (s x) -> p s x", s=2)[:, :, 0:256]
                        give(lv, V.copy_predicated(C_AT[:, dr].rearrange("p (s a) i -> p s a i", s=2),
                                                   C_MASK[:, dr, v_, :].unsqueeze(1).unsqueeze(1).to_broadcast([128, 2, 2, 128]),
                                                   data.rearrange("p s (a i) -> p s a i", a=2)))
                    post("L2_attention_ready")
                    if n + 1 < 2 * NT:
                        products(n + 1)
                    if dr == 1:
                        dve.wait_ge(S("L2_head_rms_ready"), t + 1)
                        r = ST[:, 120:124]
                        step(V.reciprocal(r, ST2[:, 36:40]))
                        if t:
                            dve.wait_ge(flow(2, "turned", 1).full, t)
                        o3 = C_O.rearrange("p (a s e) -> p s a e", a=2, s=2)
                        ps = PS[:, 2048:3072].rearrange("p (s x) -> p s x", s=2)[:, :, 0:256].rearrange("p s (a e) -> p s a e", a=2)
                        r3 = r.rearrange("p (a s) -> p s a", s=2).unsqueeze(3).to_broadcast([128, 2, 2, 128])
                        give(go, V.tensor_tensor(o3, ps, r3, ALU.mult))
                        step(V.tensor_tensor(C_O, C_O, C_R[:, t, :], ALU.mult))
                        post("L2_heads_ready")

            def mixer3():
                dve.wait_ge(S("second_attention_constants_in"), 48)
                cos = B_CONST[:, 0:256].rearrange("p (t n) -> p t n", t=TL)
                sin = B_CONST[:, 256:512].rearrange("p (t n) -> p t n", t=TL)
                for t in range(NT):
                    dve.wait_ge(S("L3_qk_in"), t + 1)
                    h0 = 0 if t < TL else 8
                    nh = 10 - h0
                    qk = B_QK[:, t, h0 * 128:1280]
                    sq = B_SQ[:, h0 * 128:1280]
                    q3 = lambda a: a.rearrange("p (h e) -> p h e", e=128)
                    step(V.tensor_tensor(sq, qk, qk, ALU.mult))
                    step(V.reduce_sum(ST[:, 0:nh], q3(sq), AX.X))
                    post("L3_head_squares_ready")
                    dve.wait_ge(S("L3_head_rms_ready"), t + 1)
                    step(V.reciprocal(ST[:, 32:32 + nh], ST[:, 16:16 + nh]))
                    step(V.tensor_tensor(q3(qk), q3(qk), ST[:, 32:32 + nh].unsqueeze(2).to_broadcast([128, nh, 128]), ALU.mult))
                    if t < TL:
                        step(V.tensor_tensor(q3(qk[:, 0:1024]), q3(qk[:, 0:1024]), B_G[:, 0:128].unsqueeze(1).to_broadcast([128, 8, 128]), ALU.mult))
                    kk = q3(qk)[:, nh - 2:nh, :]
                    step(V.tensor_tensor(kk, kk, B_G[:, 128:256].unsqueeze(1).to_broadcast([128, 2, 128]), ALU.mult))
                    if t < TL:
                        q4 = lambda a: a.rearrange("p (h s e) -> p h s e", s=2, e=64)
                        c = cos[:, t, :].unsqueeze(1).to_broadcast([128, 10, 64])
                        s = sin[:, t, :].unsqueeze(1).to_broadcast([128, 10, 64])
                        x, a, b = q4(qk), q4(B_SQ), q4(B_T2)
                        for hf in range(2):
                            step(V.tensor_tensor(a[:, :, hf, :], x[:, :, hf, :], c, ALU.mult))
                            step(V.tensor_tensor(b[:, :, hf, :], x[:, :, 1 - hf, :], s, ALU.mult))
                        step(V.tensor_tensor(x[:, :, 0, :], a[:, :, 0, :], b[:, :, 0, :], ALU.subtract))
                        step(V.tensor_tensor(x[:, :, 1, :], a[:, :, 1, :], b[:, :, 1, :], ALU.add))
                    post("L3_heads_normed")
                attend(3)

            def mixer1():
                f = flow(1, "dt", NT)
                offer(f)
                dve.wait_ge(S("ssm_vectors_in"), 160)
                for t in range(NT):
                    ready(f)
                    give(f, V.tensor_tensor(SSM_DT[:, t, :], bank(t, 64), SSM_DTB, ALU.add))
                flat = lambda a: a.rearrange("p t n -> p (t n)")
                dt, am = flat(SSM_DT), flat(SSM_A)
                e, u, lg = flat(SSM_WD), flat(SSM_EACS), flat(SSM_ETOT)
                step(V.scalar_tensor_tensor(e, dt, -1.0, dt, ALU.mult, ALU.min))
                post("L1_minus_abs_ready")
                dve.wait_ge(S("L1_exp_ready"), 1)
                step(V.tensor_scalar(u, e, 1.0, None, ALU.add))
                post("L1_one_plus_ready")
                step(V.scalar_tensor_tensor(e, u, 1.0, e, ALU.subtract, ALU.subtract))
                dve.wait_ge(S("L1_log_ready"), 1)
                step(V.reciprocal(u, u))
                step(V.tensor_tensor(e, e, u, ALU.mult))
                step(V.tensor_tensor(lg, lg, e, ALU.subtract))
                step(V.scalar_tensor_tensor(dt, dt, 0.0, lg, ALU.max, ALU.add))
                step(V.scalar_tensor_tensor(SSM_A, SSM_DT, -1.0, SSM_ALOG.unsqueeze(1).to_broadcast([128, NT, 64]), ALU.mult, ALU.mult))
                post("L1_a_ready")
                f = flow(1, "acs", NT)
                offer(f)
                for t in range(NT):
                    ready(f)
                    step(V.tensor_copy(SSM_ACS[:, t, :], bank(t, 64)))
                    step(V.tensor_copy(SSM_ETOT[:, t, :], bank(t, 64, 64)))
                    give(f, V.tensor_tensor(SSM_WD[:, t, :], SSM_ETOT[:, t, :], SSM_ACS[:, t, :], ALU.subtract))
                post("L1_sums_ready")
                dve.wait_ge(S("L1_decays_ready"), 1)
                step(V.tensor_tensor(SSM_WD, SSM_WD, SSM_DT, ALU.mult))

                cv = flow(1, "conv", 4)
                gf, sf, df, of, yf, tf = (flow(1, "bc", 1), flow(1, "state", 2), flow(1, "decay", 2), flow(1, "off", 1),
                                          flow(1, "diag", 1), flow(1, "turned", 1))
                for f in (cv, gf, sf, df, of):
                    offer(f)
                dve.sem_inc(yf.free, 1)
                got[yf] = 0

                def heads_of(a, t, dr, g, w=8):
                    return a[:, t, dr * 32 + g * 8:dr * 32 + g * 8 + 8].unsqueeze(2).to_broadcast([128, 8, 64])

                for g in range(SSM_G):
                    t0 = T0[1, "in"] + per_group * g
                    for n in range(6):
                        ready(cv, t0 + n if n < 2 else t0 + 2 if n == 5 else None)
                        x = n % 4 * 1024
                        y, j = ((SSM_BT, 16 + g), (SSM_CT, 20 + g))[n] if n < 2 else (SSM_XT[:, n - 2, :], 4 * g + n - 2)
                        ends = ((0, LAT), (LAT, TOK))[:1 if n == 1 else 2]
                        w = lambda a: SSM_CW[:, a, j:j + 1]
                        m = ends[-1][1]
                        step(V.tensor_scalar(y[:, 0:m], PS[:, x:x + m], w(2), w(5), ALU.mult, ALU.add))
                        for k in (0, 1, 3, 4):
                            o = k - 2
                            for e_, (a, b) in enumerate(ends):
                                lo, hi = max(a, a - o), min(b, b - o)
                                ins = V.scalar_tensor_tensor(y[:, lo:hi], PS[:, x + lo + o:x + hi + o], w(k), y[:, lo:hi], ALU.mult, ALU.add)
                                if k == 4 and e_ == len(ends) - 1:
                                    give(cv, ins)
                                else:
                                    step(ins)
                        post("L1_convolved")
                    ready(gf)
                    for dr in range(2):
                        mask = cs(("upto", "downto")[dr]).unsqueeze(1).to_broadcast([128, TL, 128])
                        ins = V.tensor_tensor(SSM_GM[:, dr], bank(0).rearrange("p (c l) -> p c l", c=TL), mask, ALU.mult)
                        give(gf, ins) if dr else step(ins)
                    dve.wait_ge(S("L1_tokens_ready"), 5 * (g + 1))

                    def state_input(n):
                        c = SSM_ORDERS[n // 5][n % 5]
                        step(V.tensor_tensor(by_head(SSM_XW[:, n % 2, :]), by_head(SSM_X[:, c, :]), heads_of(SSM_WD, c, n // 5, g), ALU.mult))
                        post("L1_state_input_ready")

                    state_input(0)
                    state_input(1)
                    for n in range(10):
                        dr, j = n // 5, n % 5
                        ready(sf)
                        new = SN[:, sn_slot(dr, j + 1), :]
                        ps = bank(1 + n % 2)
                        if j == 0:
                            give(sf, V.tensor_copy(new, ps))
                        else:
                            old = SN[:, sn_slot(dr, j), :]
                            step(V.tensor_tensor(by_head(new), by_head(old), heads_of(SSM_ETOT, SSM_ORDERS[dr][j], dr, g), ALU.mult))
                            give(sf, V.tensor_tensor(new, new, ps, ALU.add))
                        if n + 2 < 10:
                            state_input(n + 2)
                    post("L1_states_ready")

                    def gated(c):
                        if c or g:
                            dve.wait_ge(tf.full, TL * g + c)
                        step.go(V.tensor_tensor(by_head(SSM_T2), by_head(SSM_X[:, c, :]), SSM_DSK[:, g * 8:(g + 1) * 8].unsqueeze(2).to_broadcast([128, 8, 64]), ALU.mult))
                        ready(of)
                        step(V.tensor_tensor(by_head(SSM_T1), by_head(bank(6)), heads_of(SSM_EACS, c, 0, g), ALU.mult))
                        step(V.tensor_tensor(SSM_T1, SSM_T1, SSM_T2, ALU.add))
                        give(of, V.tensor_tensor(by_head(SSM_T2), by_head(bank(7)), heads_of(SSM_EACS, c, 1, g), ALU.mult))
                        step(V.tensor_tensor(SSM_T1, SSM_T1, SSM_T2, ALU.add))
                        dve.wait_ge(S("L1_weights_used"), 16 * g + 4 * (c + 1))
                        give(yf, V.tensor_tensor(SSM_T1, SSM_T1, bank(5), ALU.add))
                        step(V.tensor_tensor(SSM_T1, SSM_T1, ssm_z(c), ALU.mult))
                        post("L1_gated")

                    def normed(c):
                        dve.wait_ge(S("L1_rms_ready"), TL * g + c + 1)
                        step(V.reciprocal(ST[:, 124:125], ST2[:, 33:34]))
                        dve.wait_ge(S("ssm_gain_in"), 16)
                        step(V.scalar_tensor_tensor(SSM_T1, SSM_T1, ST[:, 124:125], SSM_NG[:, g * 512:(g + 1) * 512], ALU.mult, ALU.mult))
                        post("L1_normed")

                    for k in range(19):
                        if k < 16:
                            c, q = k // 4, k % 4
                            if q == 0:
                                for dr in range(2):
                                    step.go(V.tensor_tensor(by_head(SSM_XDT[:, c % 2, dr, :]), by_head(SSM_X[:, c, :]), heads_of(SSM_DT, c, dr, g), ALU.mult))
                            ready(df)
                            if k >= 4 or g:
                                dve.wait_ge(S("L1_weights_used"), 16 * g + max(k - 3, 0))
                            dm = SSM_DM[:, k % 4, :]
                            for n in range(4):
                                col = n // 2 * 32 + g * 8 + 2 * q + n % 2
                                ins = V.tensor_scalar(dm[:, n * 128:(n + 1) * 128], bank(3 + k % 2, 128, n * 128), SSM_ACS[:, c, col:col + 1], 0.0, ALU.subtract, ALU.min)
                                give(df, ins) if n == 3 else step.go(ins)
                            post("L1_exponents_ready")
                        if 1 <= k <= 16:
                            c = (k - 1) // 4
                            dve.wait_ge(S("L1_exponentials_ready"), 16 * g + k)
                            dm = SSM_DM[:, (k - 1) % 4, :].rearrange("p (d h l) -> p d h l", d=2, h=2)
                            step(V.tensor_tensor(dm, dm, SSM_GM[:, :, c, :].unsqueeze(2).to_broadcast([128, 2, 2, 128]), ALU.mult))
                            post("L1_weights_ready")
                        if k >= 5 and k % 4 == 1:
                            gated((k - 2) // 4)
                        if k >= 6 and k % 4 == 2:
                            normed((k - 3) // 4)
                post("L1_scan_done")

            def feed_forward(L):
                f = flow(L, "up", 4)
                nlat = LAT
                _, pieces = tiles_of(L)
                ends = ((0, LAT), (LAT, TOK))[:pieces]
                hid = big(0, NF2, TOK)
                cw = CONV_W2
                n = TOK if pieces == 2 else LAT
                dve.wait_ge(S("conv_vectors_in"), 64 * (second.index(L) + 1))
                t0 = T0[L, "up"]
                offer(f)

                for tile in range(11):
                    for c in range(4):
                        j = tile * 4 + c
                        ready(f, t0 + tile if c == 3 else None)
                        x = (j % 4) * 1024
                        y = CONV_Y[:, j % 2, :]
                        if 2 <= j < NF2 + 2:
                            dve.wait_ge(S("gates_done"), NF2 * second.index(L) + j - 1)
                        w = lambda a: cw[:, a, j:j + 1]
                        step(V.tensor_scalar(y[:, 0:n], PS[:, x:x + n], w(1), w(3), ALU.mult, ALU.add))
                        for a, b in ends:
                            step(V.scalar_tensor_tensor(y[:, a + 1:b], PS[:, x + a:x + b - 1], w(0), y[:, a + 1:b], ALU.mult, ALU.add))
                        for e_, (a, b) in enumerate(ends):
                            ins = V.scalar_tensor_tensor(y[:, a:b - 1], PS[:, x + a + 1:x + b], w(2), y[:, a:b - 1], ALU.mult, ALU.add)
                            if e_ == len(ends) - 1:
                                give(f, ins)
                            else:
                                step(ins)
                        if j < NF2:
                            post("gates_convolved")
                        else:
                            h = hid[:, j - NF2, 0:n]
                            step(V.tensor_tensor(h, h, y[:, 0:n], ALU.mult))
                post("hidden_ready")
                post("conv_vectors_used")

            step(V.memset(EPSC, EPS2))
            step(V.memset(RMSC, RMS_EPS))
            post("eps_ready")
            for L in layers:
                ntok, _ = tiles_of(L)
                if L == layers[0]:
                    dve.wait_ge(S("tokens_in"), 32)
                    if L < 2:
                        post("m_tokens_ready", NT)
                elif L == 1:
                    post("m_tokens_ready", NT)
                modulation(L)
                if L >= 2:
                    rms_input(L, "m", NT)
                transposed_input(L, "m")
                gates(L)
                (mixer0, mixer1, mixer2, mixer3)[L]()
                n = 2 if L == 1 else 1
                residual(L, "m", flow(L, "mixed", ntok), T0[L, "out"], n, None)
                if L >= 2:
                    rms_input(L, "f", ntok)
                transposed_input(L, "f")
                if L >= 2:
                    feed_forward(L)
                residual(L, "f", flow(L, "down", ntok), T0[L, "down"], 4, None)
                post("layer_done")
            if layers[-1] == 3:
                dve.wait_ge(S("final_rms_ready"), 1)
                step(V.reciprocal(ST[:, 104:104 + TL], ST2[:, 8:8 + TL]))
                dve.wait_ge(S("norm_vectors_in"), NORM_FINAL)
                for t in range(TL):
                    step(V.scalar_tensor_tensor(H[:, t, :], H[:, t, :], ST[:, 104 + t:105 + t], GB[:, 0, :], ALU.mult, ALU.mult))
                    post("output_ready")

        @block.scalar
        def _(act):
            A = nc.scalar.activation
            step = Link(act, "scalar_steps")
            got, fulls = {}, {}

            def offer(f):
                if f in got:
                    return
                act.sem_inc(f.free, f.slots)
                got[f] = fulls[f] = 0

            def ready(f, tile=None, i=None, per=0, tper=0):
                if tile is None:
                    fulls[f] += 1
                    act.wait_ge(f.full, v(fulls[f], i, per))
                else:
                    act.wait_ge(wused, v(tile + 1, i, tper))

            def give(f, ins, i=None, per=0):
                got[f] += 1
                ins.then_inc(f.free, 1)
                act.wait_ge(f.free, v(f.slots + got[f], i, per))

            def post(name, n=1):
                act.sem_inc(S(name), n)

            def mod_rows(L, m, bank_, rows):
                f = flow(L, "mod_rows", 2)
                offer(f)
                ready(f, MOD_TILES[L][m])
                give(f, A(rows[0:2, :], bank(bank_)[0:2, :], ACT.Copy))

            def mod_columns(L, m, bank_):
                f = flow(L, "mod_columns", 1)
                offer(f)
                ready(f)
                give(f, A(MODC[:, 4 * m:4 * m + 4, :].rearrange("p a b -> p (a b)"), bank(bank_, 8), ACT.Copy))
                post("mod_sums_ready")

            def modulation_start(L):
                offer(flow(L, "mod_rows", 2))
                offer(flow(L, "mod_columns", 1))
                for m in range(13):
                    if m < 12:
                        mod_rows(L, m, 5 + m % 2, MOD_ROWS_START[:, m % 2, :])
                    if m:
                        mod_columns(L, m - 1, 7)

            def gates(L):
                f = flow(L, "gates", 4)
                offer(f)
                for a in range(4):
                    ready(f)
                    give(f, A(GATE[:, a // 2, a % 2, :], bank(2 * a, 1024), ACT.Copy))

            def transposed_input(L, which):
                f = flow(L, "u" + which + "_s", 2)
                offer(f)
                _, pieces = tiles_of(L)
                if which == "m":
                    pieces = 2
                w = 2 * (which == "f")
                act.wait_ge(S("columns_ready"), nth(L))
                for k in range(1, KD, 2):
                    ready(f)
                    x = (k // 2 % 2) * 2048 + 1024
                    for p in range(pieces):
                        a, n = ((0, LAT), (LAT, CTX))[p]
                        ins = A(UT[:, k, a:a + n], PS[:, x + a:x + a + n], ACT.Identity, scale=COL[:, w + 1, k, p:p + 1], bias=COL[:, w, k, p:p + 1])
                        if p == pieces - 1:
                            give(f, ins)
                        else:
                            step(ins)

            def root(L, which, ntok):
                act.wait_ge(S("variance_ready"), 2 * layers.index(L) + 1 + (which == "f"))
                step(A(ST[:, 112:112 + ntok], ST[:, 96:96 + ntok], ACT.Sqrt))
                post("deviation_ready")

            def rms(L, which, ntok, name, wait, base=0):
                for t in range(ntok):
                    if wait:
                        act.wait_ge(S(wait), base + t + 1)
                    step(A(SQ_TMP, H[:, t, :], ACT.Square, accum_out=ST2[:, t:t + 1]))
                step(A(ST2[:, 8:8 + ntok], ST2[:, 0:ntok], ACT.Sqrt, scale=1.0 / D, bias=EPSC[:, 0:1]))
                post(name)

            def attend(L):
                heads, dv, P, PT, O, scale = att_frame(L)
                units = att_units(L)
                n = len(units)
                sf, tf, of = flow(L, "scores", 2), flow(L, "probsT", 1), flow(L, "heads", 1)
                offer(sf)
                offer(tf)
                u0, x0 = units_before(L), turns_ahead(L)
                for k in range(n + 4):
                    if k < n:
                        u = units[k]
                        x = (k % 2) * 1024
                        act.wait_ge(S("maxima_ready"), u0 + k + 1)
                        if k >= 2:
                            act.wait_ge(tf.full, u0 + x0 + nth_probsT(L, k - 2))
                        if k >= 8:
                            act.wait_ge(of.free, of.slots + u0 + k - 7)
                        neg = ST[:, 136 + k % 8:137 + k % 8]
                        if L == 0:
                            step(A(ST2[:, 24 + k % 8:25 + k % 8], A_SINK[:, u["h"]:u["h"] + 1], ACT.Exp, scale=scale, bias=neg))
                        give(sf, A(P[:, k % 2, u["first"]:768], PS[:, x + u["first"]:x + 768], ACT.Exp, scale=scale, bias=neg,
                                   accum_out=ST2[:, 16 + k % 8:17 + k % 8]))
                        post("probs_ready")
                    if 1 <= k <= n:
                        w = 128 * len(units[k - 1]["vals"])
                        ready(tf)
                        if k >= 3:
                            act.wait_ge(of.full, u0 + k - 2)
                        give(tf, A(PT[:, (k - 1) % 2, 0:w], bank(4, w), ACT.Copy))
                    t = k // heads - 1
                    if t >= 0 and k == turn_step(L, t):
                        ready(tf)
                        give(tf, A(UT[:, :, t * 128:(t + 1) * 128], bank(4, D).rearrange("p (a b) -> p a b", a=KD), ACT.Copy))
                    if L in next_of and k % 8 == 4 and k < n:
                        mod_rows(next_of[L], k // 8, 7, MOD_ROWS[L])
                    if L in next_of and k % 8 == 7 and k < n:
                        mod_columns(next_of[L], k // 8, 7)

            def mixer0():
                t0 = T0[0, "in"]
                f = flow(0, "q", 4)
                offer(f)
                for c in range(10):
                    ready(f, t0 + c // 4 if c in (3, 7) else None)
                    x = (c % 4) * 1024
                    give(f, A(A_Q[:, c, :] if c < 8 else A_KC[:, c - 8, :], PS[:, x:x + TOK], ACT.Copy))
                attend(0)

            def mixer2():
                t0 = T0[2, "in"]
                f = flow(2, "uf", 4)
                offer(f)
                for c in range(4):
                    ready(f, t0 if c == 3 else None)
                    give(f, A(C_UF[:, c, :], PS[:, c * 1024:c * 1024 + TOK], ACT.Copy))
                f = flow(2, "ft", 2)
                offer(f)
                for g in range(4):
                    ready(f)
                    give(f, A(C_MIX[:, g, :], PS[:, g % 2 * 1024:g % 2 * 1024 + TOK], ACT.Copy))
                f = flow(2, "qk", 4)
                offer(f)
                for c in range(4):
                    ready(f, t0 + 1 if c == 3 else None)
                    give(f, A(C_QK[:, c, :], PS[:, c * 1024:c * 1024 + TOK], ACT.Copy, scale=GLA_DK ** -0.5 if c < 2 else 1.0))
                f = flow(2, "z", 1)
                offer(f)
                act.wait_ge(S("L2_ones_ready"), 1)
                ready(f)
                give(f, A(C_ZT[0:16, :], PS[0:16, 0:TOK], ACT.Copy))
                vr = flow(2, "vr", NT)
                for t in range(NT):
                    if t == NT - 1:
                        act.wait_ge(wused, t0 + 4)
                    else:
                        act.wait_ge(vr.full, NT - 1 + t + 1)
                    ins = A(C_R[:, t, :], bank(t), ACT.Silu)
                    ins.then_inc(vr.free, 1)
                    act.wait_ge(vr.free, NT + NT + t + 1)
                    post("L2_r_ready")
                f = flow(2, "la", NT)
                offer(f)
                for t in range(NT):
                    ready(f)
                    give(f, A(C_LA[:, t, :], bank(t), ACT.Copy))
                post("L2_logits_ready")
                act.wait_ge(S("L2_minus_abs_ready"), 1)
                step(A(C_T1, C_T1, ACT.Exp))
                step(A(C_T1, C_T1, ACT.Ln, bias=1.0))
                post("L2_log_ready")
                for a in range(4):
                    act.wait_ge(S("L2_sums_ready"), a + 1)
                    step(A(C_QB[:, a, :], C_BT[:, a, :], ACT.Exp))
                post("L2_query_decay_ready")
                f = flow(2, "ec", NT)
                offer(f)
                for t in range(NT):
                    ready(f)
                    give(f, A(C_KE[:, t, :], bank(t), ACT.Exp))
                go, gt = flow(2, "mixed_heads", 1), flow(2, "turned", 1)
                offer(gt)
                e = UTF[:, 0:1792]

                def level_decays(n):
                    act.wait_ge(S("L2_differences_ready"), n + 1)
                    step(A(e, e, ACT.Abs))
                    step(A(e, e, ACT.Exp, scale=-1.0))
                    post("L2_level_decays_ready")

                def turned(t):
                    ready(gt)
                    give(gt, A(C_MIX[:, 4:8, t * 128:(t + 1) * 128], bank(6).rearrange("p (a b) -> p a b", a=4), ACT.Copy))

                level_decays(0)
                for n in range(2 * NT):
                    t, dr = n // 2, n % 2
                    if n + 1 < 2 * NT:
                        level_decays(n + 1)
                    if n and 2 in next_of:
                        mod_columns(3, n - 1, 7)
                    if dr == 1:
                        if t:
                            turned(t - 1)
                        act.wait_ge(go.full, t + 1)
                        for h in range(GLA_H):
                            step(A(C_JUNK, bank(4 + h % 2, 128, h // 2 * 128), ACT.Square, accum_out=ST2[:, 32 + h:33 + h]))
                        step(A(ST2[:, 36:40], ST2[:, 32:36], ACT.Sqrt, scale=1.0 / GLA_DV, bias=EPSC))
                        post("L2_head_rms_ready")
                    if 2 in next_of:
                        mod_rows(3, n, 7, MOD_ROWS[2])
                if 2 in next_of:
                    mod_columns(3, 11, 7)
                turned(NT - 1)

            def mixer3():
                t0 = T0[3, "in"]
                f = flow(3, "q", TL)
                offer(f)
                for p in range(2):
                    for t in range(TL):
                        ready(f, t0 + p if t == TL - 1 else None)
                        give(f, A(B_QK[:, t, p * 512:(p + 1) * 512], bank(t), ACT.Copy))
                f = flow(3, "kv", NT)
                offer(f)
                for t in range(NT):
                    ready(f, t0 + 2 if t == NT - 1 else None)
                    step(A(B_QK[:, t, 1024:1280], bank(t, 256), ACT.Copy))
                    give(f, A(B_V[:, t, :], bank(t, 256, 256), ACT.Copy))
                    post("L3_qk_in")
                f = flow(3, "turned", 2)
                offer(f)
                n = 0
                for t in range(NT):
                    nh = 10 if t < TL else 2
                    act.wait_ge(S("L3_head_squares_ready"), t + 1)
                    step(A(ST[:, 16:16 + nh], ST[:, 0:nh], ACT.Sqrt, scale=1.0 / DB, bias=EPSC))
                    post("L3_head_rms_ready")
                    for w in ((0, 1) if t < TL else (1,)):
                        ready(f)
                        x = n % 2 * 1024
                        n += 1
                        dst = (B_QT if w == 0 else B_KT)[:, :, t * 128:(t + 1) * 128]
                        k = 8 if w == 0 else 2
                        give(f, A(dst, PS[:, x:x + k * 128].rearrange("p (a b) -> p a b", a=k), ACT.Copy))
                attend(3)

            def mixer1():
                act.wait_ge(S("ssm_vectors_in"), 160)
                step(A(SSM_ALOG, SSM_ALOG, ACT.Exp))
                flat = lambda a: a.rearrange("p t n -> p (t n)")
                e, u, lg = flat(SSM_WD), flat(SSM_EACS), flat(SSM_ETOT)
                act.wait_ge(S("L1_minus_abs_ready"), 1)
                step(A(e, e, ACT.Exp))
                post("L1_exp_ready")
                act.wait_ge(S("L1_one_plus_ready"), 1)
                step(A(lg, u, ACT.Ln))
                post("L1_log_ready")
                act.wait_ge(S("L1_sums_ready"), 1)
                step(A(flat(SSM_EACS), flat(SSM_ACS), ACT.Exp))
                step(A(flat(SSM_ETOT), flat(SSM_ETOT), ACT.Exp))
                step(A(flat(SSM_WD), flat(SSM_WD), ACT.Exp))
                post("L1_decays_ready")
                z, xt, tf = flow(1, "z", TL), flow(1, "xt", 2), flow(1, "turned", 1)
                for f in (z, xt, tf):
                    offer(f)

                def turned(g, c):
                    ready(tf)
                    give(tf, A(SSM_YT[:, g * 4:g * 4 + 4, c * 128:(c + 1) * 128], bank(0).rearrange("p (a b) -> p a b", a=4), ACT.Copy))

                for g in range(SSM_G):
                    t0 = T0[1, "in"] + per_group * g
                    for n in range(6):
                        act.wait_ge(S("L1_convolved"), 6 * g + n + 1)
                        y = (SSM_BT, SSM_CT)[n] if n < 2 else SSM_XT[:, n - 2, :]
                        step(A(y, y, ACT.Silu))
                        post("L1_channels_ready")
                    for t in range(TL):
                        ready(z, t0 + 3 if t == TL - 1 else None)
                        give(z, A(ssm_z(t), bank(t), ACT.Silu))
                    for n in range(5):
                        ready(xt)
                        src = PS[:, 2048 + n % 2 * 1024:2048 + n % 2 * 1024 + TOK].rearrange("p (t c) -> p t c", t=NT)
                        give(xt, A(SSM_X[:, :, n * 128:(n + 1) * 128] if n < 4 else SSM_BK, src, ACT.Copy))
                        post("L1_tokens_ready")
                    for k in range(18):
                        if k < 16:
                            act.wait_ge(S("L1_exponents_ready"), 16 * g + k + 1)
                            dm = SSM_DM[:, k % 4, :]
                            step(A(dm, dm, ACT.Exp))
                            post("L1_exponentials_ready")
                        if k >= 8 and k % 4 == 0:
                            turned(g, k // 4 - 2)
                        if k >= 5 and k % 4 == 1:
                            act.wait_ge(S("L1_gated"), TL * g + k // 4)
                            step(A(SSM_T2, SSM_T1, ACT.Square, accum_out=ST2[:, 32:33]))
                            step(A(ST2[:, 33:34], ST2[:, 32:33], ACT.Sqrt, scale=1.0 / 512, bias=RMSC))
                            post("L1_rms_ready")
                        if 1 in next_of and k in (5, 9, 13):
                            mod_rows(next_of[1], 3 * g + k // 4 - 1, 1, MOD_ROWS[1])
                        if 1 in next_of and k in (7, 11, 15):
                            mod_columns(next_of[1], 3 * g + k // 4 - 1, 1)
                    turned(g, TL - 1)

            def feed_forward(L):
                f = flow(L, "up", 4)
                _, pieces = tiles_of(L)
                n = TOK if pieces == 2 else LAT
                if L < 2:
                    offer(f)
                    hid = big(0, 32, TOK)
                    t0 = T0[L, "up"]
                    with act.Fori(0, 4, 1) as i:
                        step.begin(i, 8)
                        for s in range(2):
                            for c in range(4):
                                ready(f, t0 + s if c == 3 else None, i, 6, 2)
                                x = c * 1024
                                out = hid[:, bass.ds(i * 8 + s * 4 + c, 1), 0:n].rearrange("p a b -> p (a b)")
                                act.sem_inc(S("scalar_ticks"), 1)
                                give(f, A(out, PS[:, x:x + n], ACT.Relu), i, 8)
                                act.sem_inc(S("scalar_ticks"), 1)
                                step(A(out, out, ACT.Square))
                    step.end(4)
                    got[f] += 24
                    fulls[f] += 18
                    post("hidden_ready")
                    return
                hid = big(0, NF2, TOK)
                for j in range(NF2):
                    act.wait_ge(S("gates_convolved"), NF2 * second.index(L) + j + 1)
                    step(A(hid[:, j, 0:n], CONV_Y[:, j % 2, 0:n], ACT.Silu))
                    post("gates_done")

            act.wait_ge(S("eps_ready"), 1)
            act.wait_ge(S("conditioning_in"), 64)
            step(A(CV[:, :, :], CV[:, :, :], ACT.Silu))
            post("conditioning_ready")
            modulation_start(layers[0])
            for L in layers:
                ntok, _ = tiles_of(L)
                if L >= 2:
                    if L == layers[0]:
                        act.wait_ge(S("tokens_in"), 32)
                    else:
                        act.wait_ge(S("layer_done"), layers.index(L))
                    if L == 2:
                        act.wait_ge(S("second_context_in"), 16)
                    rms(L, "m", NT, "m_rms_ready", None)
                transposed_input(L, "m")
                gates(L)
                (mixer0, mixer1, mixer2, mixer3)[L]()
                if L < 2:
                    root(L, "m", ntok)
                else:
                    rms(L, "f", ntok, "f_rms_ready", "m_residual_ready", NT * second.index(L))
                transposed_input(L, "f")
                feed_forward(L)
                if L < 2:
                    root(L, "f", ntok)
            if layers[-1] == 3:
                rms(3, "final", TL, "final_rms_ready", "f_residual_ready")

        @block.gpsimd
        def _(pool):
            def bring(name, dst, src):
                pool.dma_start(dst, src, allow_slow_non_contiguous=True).then_inc(S(name), 16)

            def spread(a, n):
                return a.unsqueeze(0).to_broadcast([128, n])

            bring("conditioning_in", CV[:, :, 0], d["c"][0].rearrange("(k p) -> p k", p=128))
            bring("conditioning_in", CV[:, :, 1], d["c_ctx"].rearrange("(k p) -> p k", p=128))
            bring("conditioning_in", CV[:, :, 2], d["c_2"][0].rearrange("(k p) -> p k", p=128))
            bring("conditioning_in", CV[:, :, 3], d["c_ctx_2"].rearrange("(k p) -> p k", p=128))
            bring("constants_in", CS[:, :], d["c_small"])
            bring("tokens_in", H[:, 0:TL, :], d["x"][0].rearrange("(t p) n -> p t n", p=128))
            bring("tokens_in", H[:, TL:NT, :], d["ctx"][0].rearrange("(t p) n -> p t n", p=128))
            def bring_bias(L):
                bm = d["b_mod"] if L < 2 else d["b_mod_2"]
                bring("mod_bias_in", BIAS_ROWS, bm[L % 2].rearrange("(j p) -> j p", p=128))

            bring_bias(layers[0])
            for n, L in enumerate(layers):
                if n:
                    pool.wait_ge(S("layer_done"), n)
                l = L % 2
                if L == 2:
                    if n == 0:
                        pool.wait_ge(S("tokens_in"), 32)
                    bring("second_context_in", H[:, TL:NT, :], d["ctx_2"][0].rearrange("(t p) n -> p t n", p=128))
                if L == 0:
                    bring("attention_constants_in", A_CONST, d["c_att"])
                    bring("attention_constants_in", A_SINK, spread(d["att_sink"][0], HA))
                if L >= 2:
                    for w, gn in enumerate(("g_norm_mix_2", "g_norm_ffn_2")):
                        bring("norm_gains_in", GCOL[:, w, :], d[gn][l].rearrange("(k p) -> p k", p=128))
                if L == 2:
                    bring("fourier_tables_in", C_TABS, d["c_four"])
                    bring("gate_weights_in", C_WZ, d["w_even_in_2"][0].rearrange("(k p) n -> p k n", p=128)[:, :, 2048:2064])
                    for dr in range(2):
                        bring("gate_weights_in", C_WG[0:16, dr * 256:(dr + 1) * 256], d["w_gla_gate_2"][0, dr])
                    bring("gate_weights_in", C_WG[16:17, :].rearrange("p (a b) -> p a b", a=2), d["b_gla_gate_2"][0:1, :, :])
                    bring("gate_weights_in", C_GAIN, spread(d["g_gla_out_2"][0], 512))
                    pool.wait_ge(S("L2_decays_ready"), 1)
                    bring("gla_masks_in", UTF[:, 5376:5888].bitcast(U32), d["c_mask"])
                if L == 3:
                    bring("second_attention_constants_in", B_CONST, d["c_att2"])
                    bring("second_attention_constants_in", B_G[:, 0:128], spread(d["g_q_2"][0], 128))
                    bring("second_attention_constants_in", B_G[:, 128:256], spread(d["g_k_2"][0], 128))
                if L == 1:
                    bring("ssm_vectors_in", SSM_WDT, d["ssm_w_in"][0].rearrange("(k p) n -> p k n", p=128)[:, :, SSM_DI + CONV_SSM:SSM_DI + CONV_SSM + 64])
                    bring("ssm_vectors_in", SSM_DTB, spread(d["ssm_dt_bias"][0].rearrange("a b -> (a b)"), 64))
                    bring("ssm_vectors_in", SSM_ALOG, spread(d["ssm_a_log"][0].rearrange("a b -> (a b)"), 64))
                    bring("ssm_vectors_in", SSM_DSK, spread(d["ssm_d"][0], SSM_H))
                    for a in range(5):
                        bring("ssm_vectors_in", SSM_CW[:, a, :], d["ssm_conv_w"][0, a].rearrange("(j p) -> p j", p=128))
                    bring("ssm_vectors_in", SSM_CW[:, 5, :], d["ssm_conv_b"][0].rearrange("(j p) -> p j", p=128))
                    pool.wait_ge(flow(1, "um_v", 2).free, 2 + 4 * (n + 1))
                    pool.wait_ge(flow(1, "um_s", 2).free, 2 + 4 * (n + 1))
                    bring("ssm_gain_in", SSM_NG, spread(d["ssm_norm_g"][0], SSM_DI))
                    pool.wait_ge(S("L1_scan_done"), 1)
                if L < 2:
                    for w, kind in enumerate(("mix", "ff")):
                        if 2 * n + w:
                            pool.wait_ge(S("norm_vectors_used"), 2 * n + w)
                        bring("norm_vectors_in", GB[:, 0, :], spread(d[f"ln_{kind}_g"][l], D))
                        bring("norm_vectors_in", GB[:, 1, :], spread(d[f"ln_{kind}_b"][l], D))
                else:
                    for a in range(3):
                        bring("conv_vectors_in", CONV_W2[:, a, :], d["w_ffn_conv_2"][l, a].rearrange("(j p) -> p j", p=128))
                    bring("conv_vectors_in", CONV_W2[:, 3, :], d["b_ffn_conv_2"][l].rearrange("(j p) -> p j", p=128))
                if L in next_of:
                    pool.wait_ge(S("hidden_ready"), nth(L))
                    bring_bias(next_of[L])
            if layers[-1] == 3:
                pool.wait_ge(S("conv_vectors_used"), len(second))
                bring("norm_vectors_in", GB[:, 0, :], spread(d["g_norm_final_2"], D))


def kernel(**inputs):
    import numpy as _np
    import concourse.bacc as _bacc
    from concourse import mybir as _mybir
    from concourse.bass_utils import run_bass_kernel_spmd as _run

    nc = _bacc.Bacc("TRN2", target_bir_lowering=False, num_devices=1)
    arrays, d, at = {}, {}, {}
    for name, (a, where) in constants().items():
        at[name] = where
        arrays[name + "_dram"] = a
    for name in inputs:
        arrays[name + "_dram"] = _np.ascontiguousarray(inputs[name])
    for name, a in arrays.items():
        d[name[:-5]] = nc.dram_tensor(name, a.shape, _mybir.dt.from_np(a.dtype), kind="ExternalInput").ap()
    d["at"] = at
    d["out"] = nc.dram_tensor("out_dram", (LAT, D), F32, kind="ExternalOutput").ap()
    build(nc, d)
    r = _run(nc, [arrays], core_ids=[0])
    return r.results[0]["out_dram"].reshape(1, LAT, D)
```

```python
import concourse.bass as bass
from concourse import mybir
from contextlib import ExitStack
import numpy as np

F32 = mybir.dt.float32
U32 = mybir.dt.uint32
ALU = mybir.AluOpType
ACT = mybir.ActivationFunctionType
AX = mybir.AxisListType

D = 1024
KD = D // 128
LAT, CTX = 512, 256
TL, TC = LAT // 128, CTX // 128
TOK = LAT + CTX
NT = TL + TC
RINGW = 8 * 512
DEPTH = 2
ALPHA = (2.0 * DEPTH) ** 0.25
LN_EPS, RMS_EPS, EPS2 = 1e-5, 1e-5, 1e-6
FF = 4 * D
DFF2 = ((8 * D // 3 + 255) // 256) * 256
NF2 = DFF2 // 128
F2_PARTS = [6, 6, 5, 5]
GRID_W = 64
HA, GA, DA = 16, 4, 64
HB_, GB_, DB = 8, 2, 128
WIN_NEG = -8e30
SSM_H, SSM_P, SSM_G, SSM_N = 32, 64, 4, 128
SSM_DI = SSM_H * SSM_P
SSM_GH = SSM_H // SSM_G
CONV_SSM = SSM_DI + 2 * SSM_G * SSM_N
GLA_H, GLA_DK, GLA_DV, GLA_R = 4, 64, 128, 16
GLA_LEVELS = 8
FW = 512


def constants():
    p = np.arange(128)
    r, c = p[:, None], p[None, :]
    sel = np.zeros((128, 2, 128), np.float32)
    sel[0, 0], sel[1, 1] = 1, 1
    small = dict(
        ident=(r == c), upto=(r <= c), downto=(r >= c), after=(r > c), before=(r < c),
        ones=np.ones((128, 128)), sel=sel.reshape(128, 256))
    inv = (10000.0 ** (-np.arange(0, 32, 2, dtype=np.float32) / np.float32(32))).astype(np.float32)
    tok = np.arange(LAT)
    row, col = (tok // GRID_W).astype(np.float32), (tok % GRID_W).astype(np.float32)
    dim = p % 64
    pos = np.where((dim < 32)[:, None], row[None], col[None]).astype(np.float32)
    ang = (pos * inv[dim % 16][:, None]).astype(np.float32)
    swap = np.zeros((128, 128), np.float32)
    for o in range(128):
        if o % 32 < 16:
            swap[o + 16, o] = -1.0
        else:
            swap[o - 16, o] = 1.0
    att = dict(cosT=np.cos(ang), sinT=np.sin(ang), swap=swap,
               maskl=np.where(c >= r, 0, WIN_NEG), maskr=np.where(c <= r, 0, WIN_NEG))
    inv2 = (10000.0 ** (-np.arange(0, 64, 2, dtype=np.float32) / np.float32(64))).astype(np.float32)
    ang2 = np.concatenate([row[:, None] * inv2, col[:, None] * inv2], 1).astype(np.float32)
    t2 = lambda a: a.reshape(TL, 128, 64).transpose(1, 0, 2).reshape(128, TL * 64)
    att2 = dict(cos2=t2(np.cos(ang2)), sin2=t2(np.sin(ang2)))
    def dft(n, s):
        k = np.outer(np.arange(n), np.arange(n)) % n
        a = 2 * np.pi * k / n
        return np.cos(a) * s, np.sin(a) * s
    cd, sd = dft(128, 1.0)
    cl, sl = dft(LAT, (LAT * 128.0) ** -0.5)
    cc, sc = dft(CTX, (CTX * 128.0) ** -0.5)
    tile = lambda a: a.reshape(-1, 128, a.shape[1]).transpose(1, 0, 2).reshape(128, -1)
    four = dict(dftd=np.concatenate([cd, sd], 1), cosl=tile(cl), sinl=tile(-sl), cosc=tile(cc), sinc=tile(-sc))
    masks = np.zeros((128, 2, GLA_LEVELS, 128), np.uint8)
    for v in range(GLA_LEVELS - 1):
        m = 64 >> v
        same = (r // (2 * m)) == (c // (2 * m))
        masks[:, 0, v] = same & ((c // m) % 2 == 1) & ((r // m) % 2 == 0)
        masks[:, 1, v] = same & ((c // m) % 2 == 0) & ((r // m) % 2 == 1)
    masks[:, 0, 7] = masks[:, 1, 7] = (r == c)
    out = {}
    for n, part in dict(c_small=small, c_att=att, c_att2=att2, c_four=four).items():
        blocks, at, x = [], {}, 0
        for k, v in part.items():
            v = np.asarray(v, np.float32)
            at[k] = (x, v.shape[1])
            x += v.shape[1]
            blocks.append(v)
        out[n] = (np.ascontiguousarray(np.concatenate(blocks, 1)), at)
    out["c_mask"] = (masks.reshape(128, -1).view(np.uint32), {})
    return out


def build(nc, d, layers=(0, 1, 2, 3), debug=None):
    at = d["at"]
    ctxs = ExitStack()
    with ctxs:
        def sb(name, shape, dt=F32):
            return ctxs.enter_context(nc.sbuf_tensor(name, shape, dt))

        sems = {}

        def S(name):
            if name not in sems:
                sems[name] = ctxs.enter_context(nc.semaphore(name))
            return sems[name]

        H = sb("H", [128, NT, D])
        UT = sb("UT", [128, KD, TOK])
        RING = sb("RING", [128, 2, RINGW])
        BIG = sb("BIG", [128, 24576])
        GATE = sb("GATE", [128, 2, 2, D])
        GB = sb("GB", [128, 2, D])
        CS = sb("CS", [128, d["c_small"].shape[1]])
        CV = sb("CV", [128, KD, 4])
        COL = sb("COL", [128, 4, KD, 2])
        MODC = sb("MODC", [128, 6 * KD, 2])
        ST = sb("ST", [128, 160])
        ST2 = sb("ST2", [128, 48])
        EPSC, RMSC = ST2[:, 40:41], ST2[:, 41:42]
        RES_TMP = sb("RES_TMP", [128, 512])
        PS = ctxs.enter_context(nc.psum_tensor("PS", [128, 4096], F32))

        def big(off, *shape):
            n = int(np.prod(shape))
            assert off + n <= 24576, (off, shape)
            v = BIG[:, off:off + n]
            if len(shape) == 2:
                v = v.rearrange("p (a b) -> p a b", a=shape[0])
            if len(shape) == 3:
                v = v.rearrange("p (a b c) -> p a b c", a=shape[0], b=shape[1])
            return v

        def cs(name):
            x, n = at["c_small"][name]
            return CS[:, x:x + n]

        ident = cs("ident")
        ones = cs("ones")
        sel = cs("sel").rearrange("p (a b) -> p a b", a=2)

        def bank(b, n=512, off=0):
            return PS[:, b * 512 + off:b * 512 + off + n]

        def ring(slot, kc=8, cols=512):
            return RING[:, slot, 0:kc * cols].rearrange("p (k n) -> p k n", k=kc)

        T0, nt, MOD_TILES = {}, 0, {}
        next_of = {a: b for a, b in zip(layers, layers[1:])}
        for L in layers:
            if L == layers[0]:
                MOD_TILES[L] = list(range(nt, nt + 12))
                nt += 12
            T0[L, "in"] = nt
            ahead = L in next_of
            if L == 1:
                per_group = 7 if ahead else 4
                if ahead:
                    MOD_TILES[next_of[L]] = [nt + 7 * g + 4 + s for g in range(SSM_G) for s in range(3)]
                nt += SSM_G * per_group
            else:
                nt += {0: 3, 2: 4, 3: 3}[L]
                if ahead:
                    MOD_TILES[next_of[L]] = list(range(nt, nt + 12))
                    nt += 12
            for name, n in [("out", 4 if L == 1 else 2), ("up", 8 if L < 2 else 11), ("down", 8)]:
                T0[L, name] = nt
                nt += n
        NTILES = nt

        def v(base, i, per):
            return base if i is None else base + i * per

        wfull = [S("weights_in_0"), S("weights_in_1")]
        wused = S("weights_used")

        class Flow:

            def __init__(self, name, slots):
                self.full, self.free, self.slots = S(name + "_full"), S(name + "_free"), slots

        class Link:

            def __init__(self, eng, name):
                self.eng, self.sem, self.n, self.i, self.per = eng, S(name), 0, None, 0

            def __call__(self, ins):
                self.n += 1
                ins.then_inc(self.sem, 1)
                self.eng.wait_ge(self.sem, v(self.n, self.i, self.per))
                return ins

            def go(self, ins):
                self.n += 1
                return ins.then_inc(self.sem, 1)

            def settle(self):
                self.eng.wait_ge(self.sem, self.n)

            def begin(self, i, per):
                self.i, self.per, self.start = i, per, self.n

            def end(self, count):
                assert self.n - self.start == self.per, (self.n - self.start, self.per)
                self.n = self.start + self.per * count
                self.i = None

        def tiles_of(L):
            return (TL, 1) if L in (1, 3) else (NT, 2)

        MOD_ROWS = {0: RES_TMP[:, :], 1: BIG[:, 24064:24576], 2: RES_TMP[:, :]}
        MOD_ROWS_START = BIG[:, 0:1024].rearrange("p (s n) -> p s n", s=2)
        BIAS_ROWS = UT[0:48, 0, 0:128]
        GAIN_ROWS = UT[48:64, 0, 0:128]
        CONDITIONING_ROWS = BIG[0:32, 12000:12128]
        DIAGONALS = BIG[:, 6144:10240].rearrange("p (a k n) -> p a k n", a=4, k=KD)

        block = ctxs.enter_context(nc.Block())

        @block.sync
        def _(sp):
            state = {"t": 0}

            def load(dst, src, i=None, per=0):
                t = state["t"]
                if t >= 2:
                    sp.wait_ge(wused, v(t - 1, i, per))
                sp.dma_start(dst, src).then_inc(wfull[t % 2], 16)
                state["t"] += 1

            def columns(w, n_outer, per=2, cols=512):
                wv = w.rearrange("(k p) n -> p k n", p=128)
                first = 0
                if state["t"] == 0:
                    for s in range(per):
                        load(ring(s), wv[:, :, s * 512:(s + 1) * 512])
                    first = 1
                with sp.Fori(first, n_outer, 1) as i:
                    for s in range(per):
                        off = (i * per + s) * 512
                        load(ring(state["t"] % 2), wv[:, :, bass.ds(off, 512)], i - first, per)
                state["t"] += (n_outer - first - 1) * per

            def halves(w, parts):
                wv = w.rearrange("(k p) n -> p k n", p=128)
                if len(parts) % 2:
                    for h in range(2):
                        k0 = 0
                        for kc in parts:
                            load(ring(state["t"] % 2, kc), wv[:, k0:k0 + kc, h * 512:(h + 1) * 512])
                            k0 += kc
                    return
                with sp.Fori(0, 2, 1) as i:
                    k0 = 0
                    for kc in parts:
                        load(ring(state["t"] % 2, kc), wv[:, k0:k0 + kc, bass.ds(i * 512, 512)], i, len(parts))
                        k0 += kc
                state["t"] += len(parts)

            def mod_weights(L):
                return (d["w_mod"] if L < 2 else d["w_mod_2"])[L % 2]

            def mod_ahead(L):
                if L in next_of:
                    columns(mod_weights(next_of[L]), 6)

            for L in layers:
                if L == layers[0]:
                    columns(mod_weights(L), 6)
                if L == 0:
                    wv = d["att_w_in"][0].rearrange("(k p) n -> p k n", p=128)
                    for s in range(3):
                        load(ring(state["t"] % 2), wv[:, :, s * 512:(s + 1) * 512])
                    mod_ahead(L)
                    halves(d["att_w_out"][0], [8])
                elif L == 1:
                    wv = d["ssm_w_in"][0].rearrange("(k p) n -> p k n", p=128)
                    for g in range(SSM_G):
                        b0 = 2 * SSM_DI + g * SSM_N
                        for c0, n in ((b0, 128), (b0 + 512, 128), (SSM_DI + g * 512, 512), (g * 512, 512)):
                            load(ring(state["t"] % 2, 8, n), wv[:, :, c0:c0 + n])
                        if L in next_of:
                            mv = mod_weights(next_of[L]).rearrange("(k p) n -> p k n", p=128)
                            for s in range(3):
                                load(ring(state["t"] % 2), mv[:, :, (3 * g + s) * 512:(3 * g + s + 1) * 512])
                    halves(d["ssm_w_out"][0], [8, 8])
                elif L == 2:
                    wv = d["w_even_in_2"][0].rearrange("(k p) n -> p k n", p=128)
                    for s in range(4):
                        load(ring(state["t"] % 2), wv[:, :, s * 512:(s + 1) * 512])
                    mod_ahead(L)
                    halves(d["w_even_out_2"][0], [8])
                else:
                    wv = d["w_qkv_2"][0].rearrange("(k p) n -> p k n", p=128)
                    for s in (2, 0, 1):
                        load(ring(state["t"] % 2), wv[:, :, s * 512:(s + 1) * 512])
                    halves(d["w_att_out_2"][0], [8])
                if L < 2:
                    columns(d["ff_w1"][L], 4)
                    halves(d["ff_w2"][L], [8] * 4)
                else:
                    columns(d["w_ffn_up_2"][L - 2], 5)
                    wv = d["w_ffn_up_2"][L - 2].rearrange("(k p) n -> p k n", p=128)
                    load(ring(state["t"] % 2), wv[:, :, 5120:5632])
                    halves(d["w_ffn_down_2"][L - 2], F2_PARTS)
            assert state["t"] == NTILES
            ov = d["out"].rearrange("(t p) n -> p t n", p=128)
            if layers[-1] == 3:
                for t in range(TL):
                    sp.wait_ge(S("output_ready"), t + 1)
                    sp.dma_start(ov[:, t, :], H[:, t, :]).then_inc(S("output_stored"), 16)
                sp.wait_ge(S("output_stored"), 16 * TL)
            else:
                sp.wait_ge(S("layer_done"), len(layers))
                sp.dma_start(ov, H[:, 0:TL, :]).then_inc(S("output_stored"), 16)
                sp.dma_start(d["out_ctx"].rearrange("(t p) n -> p t n", p=128), H[:, TL:NT, :]).then_inc(S("output_stored"), 16)
                sp.wait_ge(S("output_stored"), 32)

        C_QK = big(0, 4, TOK)
        C_V = big(3072, NT, FW)
        C_R = big(6144, NT, FW)
        C_LA = big(9216, NT, 512)
        C_S = big(9216, 12, 256)
        C_BT = big(12288, 4, TOK)
        C_QB = big(15360, 4, TOK)
        C_MIX = big(18432, 8, TOK)
        C_KE = big(21504, NT, 512)
        C_X = big(0, NT, D)
        C_TABS = big(12288, d["c_four"].shape[1])
        C_UF = big(21504, 4, TOK)
        UTF = UT[:, :, :].rearrange("p a b -> p (a b)")
        C_EXP = UTF[:, 0:1792].rearrange("p (v a b) -> p v a b", v=7, a=2)
        C_QL = UTF[:, 1792:3584].rearrange("p (v a b) -> p v a b", v=7, a=2)
        C_KL = UTF[:, 3584:5376].rearrange("p (v a b) -> p v a b", v=7, a=2)
        C_T1 = big(12288, 3072)
        C_JUNK = UTF[:, 5888:6016]
        C_O = GB[:, 0, 512:1024]
        C_MASK = UTF[:, 5376:5888].bitcast(mybir.dt.uint8).rearrange("p (d v i) -> p d v i", d=2, v=GLA_LEVELS)
        C_WZ = GB[:, 0, 256:384].rearrange("p (k n) -> p k n", k=8)
        C_WG = GB[:, 0, 512:1024]
        C_ZT = GB[:, 1, 0:TOK]
        C_AT = GB[:, 1, :].rearrange("p (d h i) -> p d h i", d=2, h=4)
        C_GAIN = RES_TMP[:, :]
        C_DL = GB[:, 0, 384:408].rearrange("p (a t) -> p a t", a=4)

        def four(name):
            x, n = at["c_four"][name]
            return C_TABS[:, x:x + n]

        def gla_orders():
            return ([4, 5, 0, 1, 2, 3], [5, 4, 3, 2, 1, 0])

        def level_views(dr, t, v_):
            m = 64 >> v_
            b = C_BT[:, 2 * dr:2 * dr + 2, t * 128:(t + 1) * 128].rearrange("p a (n m) -> p a n m", m=2 * m)
            r = m - 1 if dr == 0 else m
            ref = b[:, :, :, r:r + 1].to_broadcast([128, 2, 64 // m, 2 * m])
            e = C_EXP[:, v_].rearrange("p a (n m) -> p a n m", m=2 * m)
            return e, b, ref

        SSM_YT = big(0, 16, LAT)

        SN = big(8192, 9, 512)
        SSM_XT = big(8192, 4, TOK)
        SSM_XDT = big(12800, 2, 2, 512)
        SSM_BT = big(12800, TOK)
        SSM_CT = big(14848, LAT)
        SSM_X = big(15360, NT, 512)
        SSM_WDT = big(15360, KD, 2 * SSM_H)
        SSM_BK = big(18432, NT, SSM_N)
        SSM_GM = big(19200, 2, TL, 128)
        SSM_T1 = big(20224, 512)
        SSM_DT = big(20736, NT, 64)
        SSM_A = big(21120, NT, 64)
        SSM_WD = big(21504, NT, 64)
        SSM_EACS = big(21888, NT, 64)
        SSM_ETOT = big(22272, NT, 64)
        SSM_ACS = big(22656, NT, 64)
        SSM_DTB = big(23040, 64)
        SSM_ALOG = big(23104, 64)
        SSM_DSK = big(23168, 32)
        SSM_CW = big(23200, 6, 24)
        SSM_CW_ROWS = BIG[0:24, 1024:1792]
        SSM_XW = GB[:, 0, :].rearrange("p (s n) -> p s n", s=2)
        SSM_DM = GB[:, :, :].rearrange("p a (s n) -> p (a s) n", s=2)
        SSM_T2 = RES_TMP[:, :]
        SSM_SKIP = big(23344, 512)
        SSM_NG = H[:, TL:NT, :].rearrange("p t n -> p (t n)")

        def ssm_z(t):
            return GATE[:, t // 2, 1, t % 2 * 512:t % 2 * 512 + 512]

        SSM_ORDERS = ([4, 5, 0, 1, 2, 3], [5, 4, 3, 2, 1, 0])

        def sn_slot(dr, j):
            return 8 if j == 1 else dr * 4 + j - 2

        def heads_of(a, t, dr, g):
            return a[:, t, dr * 32 + g * 8:dr * 32 + g * 8 + 8].unsqueeze(2).to_broadcast([128, 8, 64])

        def by_head(a, n=8):
            return a.rearrange("p (h e) -> p h e", h=n)

        flows = {}
        SHARED = {(0, "v"): "tiles_to_vector", (1, "dt"): "tiles_to_vector", (1, "acs"): "tiles_to_vector", (2, "kt"): "tiles_to_vector",
                  (0, "q"): "chunks_to_scalar", (2, "uf"): "chunks_to_scalar", (2, "qk"): "chunks_to_scalar",
                  (1, "conv"): "chunks_to_vector", (2, "bt"): "chunks_to_vector",
                  (1, "z"): "latent_tiles_to_scalar", (3, "q"): "latent_tiles_to_scalar",
                  (2, "la"): "tiles_to_scalar", (2, "ec"): "tiles_to_scalar", (3, "kv"): "tiles_to_scalar",
                  (1, "xt"): "turned_to_scalar", (2, "ft"): "turned_to_scalar", (3, "turned"): "turned_to_scalar",
                  (1, "state"): "pairs_to_vector", (2, "fx"): "pairs_to_vector", (2, "st"): "pairs_to_vector"}

        def flow(L, name, slots):
            if name in ("mod_rows", "mod_columns", "bias", "gates", "um_v", "um_s", "uf_v", "uf_s"):
                key = name
            elif name in ("mixed", "down"):
                key = f"{name}_{slots}"
            elif name == "up":
                key = name + ("_squared" if L < 2 else "_conv")
            else:
                key = SHARED.get((L, name), name if name in ("scores", "probsT", "heads") else f"L{L}_{name}")
            if key not in flows:
                flows[key] = Flow(key, slots)
            return flows[key]

        A_Q = big(0, 8, TOK)
        A_QR = big(6144, 8, LAT)
        CONV_W2 = GB[:, 0, 0:4 * 2 * NF2].rearrange("p (a j) -> p a j", a=4)
        CONV_ROWS = BIG[0:2 * NF2, 17920:18432]
        CONV_Y = big(NF2 * TOK, 2, TOK)
        SQ_TMP = GB[:, 1, :]
        second = [L for L in layers if L >= 2]
        first = [L for L in layers if L < 2]
        NORM_FINAL = 64 * len(first) + 16

        A_KD = big(10240, GA, TOK)
        A_KC = big(13312, 2, TOK)
        A_V = big(14848, NT, GA * DA)
        A_CONST = big(16384, d["c_att"].shape[1])
        A_P = big(18048, 2, 768)
        A_PT = big(19584, 2, 768)
        A_O = big(21120, 2, D)
        A_SINK = big(23168, HA)
        A_ROT = big(23184, LAT)

        B_QK = big(0, NT, 1280)
        B_QT = big(7680, HB_, LAT)
        B_KT = big(11776, GB_, TOK)
        B_V = big(13312, NT, GB_ * DB)
        B_CONST = big(14848, 512)
        B_P = big(15360, 2, 768)
        B_PT = big(16896, 2, 768)
        B_O = big(18432, 2, D)
        B_SQ = big(20480, 1280)
        B_G = big(21760, 256)
        B_T2 = big(22016, 1280)

        def head_pieces():
            return [(t, 1024, 2) for t in range(NT)] + [(t, w * 512, 4) for w in range(2) for t in range(TL)]

        def catt(name):
            x, n = at["c_att"][name]
            return A_CONST[:, x:x + n]

        def att_units(L):
            units = []
            if L == 0:
                for t in range(NT):
                    for h in range(HA):
                        g, half = h // 4, (h % 2) * 64
                        rows = slice(half, half + 64)
                        ql = A_Q[rows, h // 2, t * 128:(t + 1) * 128]
                        vg = slice(g * DA, (g + 1) * DA)
                        cprod = (512, 256, ql, A_KD[rows, g, LAT:TOK])
                        cvals = [A_V[:, TL + j, vg] for j in range(TC)]
                        if t >= TL:
                            units.append(dict(t=t, h=h, first=512, prods=[cprod], masks=[], vals=cvals))
                            continue
                        k0, k1 = max(t - 1, 0), min(t + 2, TL)
                        n = (k1 - k0) * 128
                        first = 512 - n
                        qr = A_QR[rows, h // 2, t * 128:(t + 1) * 128]
                        masks = []
                        if t > 0:
                            masks.append((first, "maskl"))
                        if t < TL - 1:
                            masks.append((384, "maskr"))
                        units.append(dict(t=t, h=h, first=first, masks=masks,
                                          prods=[(first, n, qr, A_KD[rows, g, k0 * 128:k1 * 128]), cprod],
                                          vals=[A_V[:, k, vg] for k in range(k0, k1)] + cvals))
            else:
                for t in range(TL):
                    for h in range(HB_):
                        g = h // 4
                        q = B_QT[:, h, t * 128:(t + 1) * 128]
                        units.append(dict(t=t, h=h, first=0, masks=[],
                                          prods=[(0, 512, q, B_KT[:, g, 0:512]), (512, 256, q, B_KT[:, g, 512:768])],
                                          vals=[B_V[:, k, g * DB:(g + 1) * DB] for k in range(NT)]))
            return units

        def att_frame(L):
            if L == 0:
                return HA, DA, A_P, A_PT, A_O, DA ** -0.5
            return HB_, DB, B_P, B_PT, B_O, DB ** -0.5

        def mod_tiles_before(L):
            return 12 * layers.index(L)

        def nth(L):
            return layers.index(L) + 1

        def tokens_so_far(L):
            return sum(tiles_of(l)[0] for l in layers[:layers.index(L) + 1])

        def units_before(L):
            return NT * HA if L == 3 and 0 in layers else 0

        border_tiles = TL if 1 in layers and 2 in layers else 0

        def normed_before(L, which):
            return sum(2 * tiles_of(l)[0] for l in first[:first.index(L)]) + (tiles_of(L)[0] if which == "f" else 0)

        def tiles_before(L, which):
            return sum(tiles_of(l)[0] for l in second[:second.index(L)]) if L in second else 0

        def turns_ahead(L):
            return NT if L == 3 and 0 in layers else 0

        def o_slot(n, dv):
            return bank(6, dv)

        def turn_step(L, t):
            return (t + 1) * att_frame(L)[0] + 3

        def turns_before(L, step):
            return max(0, (step - 4) // att_frame(L)[0])

        def nth_probsT(L, n):
            return n + 1 + turns_before(L, n + 1)

        def nth_turn(L, t, n):
            return min(turn_step(L, t), n) + t + 1

        @block.tensor
        def _(pe):
            mm, tr = nc.tensor.matmul, nc.tensor.transpose
            taken = {}
            start = {}
            settled = []

            def place(f, i=None, per=0):
                taken[f] = taken.get(f, 0) + 1
                pe.wait_ge(f.free, v(taken[f], i, per))
                return (taken[f] - start.get(f, 0) - 1) % f.slots

            def stage(*fs):
                for f in settled:
                    pe.wait_ge(f.free, taken[f] + f.slots)
                settled[:] = fs
                for f in fs:
                    start[f] = taken.get(f, 0)

            def weights(t, i=None, per=0):
                pe.wait_ge(wfull[t % 2], v(16 * (t // 2 + 1), i, 8 * per))
                return t % 2

            def used(ins):
                ins.then_inc(wused, 1)

            def mod_rows(L, m, bank_, alone=True):
                fr, fc = flow(L, "mod_rows", 2), flow(L, "mod_columns", 1)
                if alone and m:
                    pe.wait_ge(fc.free, taken[fc] + 1)
                place(fr)
                t = MOD_TILES[L][m]
                w = ring(weights(t))
                lc = 0 if L < 2 else 2
                for k in range(KD):
                    ins = mm(bank(bank_)[0:2, :], CV[:, k, lc:lc + 2], w[:, k, :], start=k == 0, stop=k == KD - 1)
                used(ins)

            def mod_columns(L, m, bank_, rows):
                fr, fc = flow(L, "mod_rows", 2), flow(L, "mod_columns", 1)
                pe.wait_ge(fr.free, mod_tiles_before(L) + m + 1 + fr.slots)
                place(fc)
                for c in range(4):
                    ins = tr(bank(bank_, 2, 2 * c), rows[0:2, c * 128:(c + 1) * 128], ident[0:2, 0:2])
                ins.then_inc(fc.full, 1)

            def modulation_start(L):
                fr, fc = flow(L, "mod_rows", 2), flow(L, "mod_columns", 1)
                stage(fr, fc)
                pe.wait_ge(S("conditioning_in"), 64)
                place(fc)
                tr(bank(7, 32), CONDITIONING_ROWS, ident[0:32, 0:32]).then_inc(fc.full, 1)
                pe.wait_ge(fc.free, taken[fc] + 1)
                for m in range(13):
                    if m < 12:
                        mod_rows(L, m, 5 + m % 2, alone=False)
                    if m:
                        mod_columns(L, m - 1, 7, MOD_ROWS_START[:, (m - 1) % 2, :])

            def mod_flows_too(L):
                if L in next_of:
                    settled.extend([flow(L, "mod_rows", 2), flow(L, "mod_columns", 1)])

            def bias_columns(L):
                f = flow(L, "bias", 1)
                stage(f)
                pe.wait_ge(S("mod_bias_in"), 16 * nth(L) + 32 * len([l for l in second if l <= L]))
                place(f)
                n = 48 if L < 2 else 64
                tr(bank(0, n), UT[0:n, 0, 0:128], ident[0:n, 0:n]).then_inc(f.full, 1)

            def gates(L):
                f = flow(L, "gates", 4)
                stage(f)
                for a in range(4):
                    pe.wait_ge(S("diagonals_ready"), 4 * nth(L) - 3 + a)
                    b = 2 * place(f)
                    for h in range(2):
                        m = mm(bank(b + h), ones, DIAGONALS[:, a, 4 * h:4 * h + 4, :], start=True, stop=True)
                    m.then_inc(f.full, 1)

            def transposed_input(L, which, src):
                nt_, _ = tiles_of(L)
                if L == 1 and which == "m" or L == 3 and which == "m":
                    nt_ = NT
                a, b = flow(L, "u" + which + "_v", 2), flow(L, "u" + which + "_s", 2)
                stage(a, b)
                pe.wait_ge(S(f"{which}_tokens_ready"), NT * nth(L) if which == "m" else tokens_so_far(L))
                for k in range(KD):
                    f = (a, b)[k % 2]
                    x = (2 * place(f) + k % 2) * 1024
                    for t in range(nt_):
                        m = tr(PS[:, x + t * 128:x + (t + 1) * 128], src[:, t, k * 128:(k + 1) * 128], ident)
                    m.then_inc(f.full, 1)

            def by_channel(t, f, chunks, last_used=True, i=None, per=0, done=0, nctx=CTX):
                slot = weights(t, i, per)
                w = ring(slot, 8, 512 if chunks[-1] >= 1 else 128)
                for c in chunks:
                    x = place(f, i, done) * 1024
                    for k in range(KD):
                        a = w[:, k, c * 128:(c + 1) * 128]
                        m = mm(PS[:, x:x + LAT], a, UT[:, k, 0:LAT], start=k == 0, stop=k == KD - 1)
                        if nctx:
                            m = mm(PS[:, x + 512:x + 512 + nctx], a, UT[:, k, LAT:LAT + nctx], start=k == 0, stop=k == KD - 1)
                    if last_used and c == chunks[-1]:
                        used(m)
                    else:
                        m.then_inc(f.full, 1)

            def by_token(t0, parts, f, inp, ntok, cols=(0, 512), wcols=512, i=None, per=0, done=0, first_bank=0):
                k0, kn = 0, sum(parts)
                for j, kc in enumerate(parts):
                    w = ring(weights(t0 + j, i, per), kc, wcols)
                    steps = [(k, t) for k in range(kc) for t in range(ntok)]
                    if j == len(parts) - 1:
                        steps = [(k, t) for t in range(ntok) for k in range(kc)]
                    for k, t in steps:
                        kk = k0 + k
                        if kk == 0:
                            place(f, i, done)
                        m = mm(bank(first_bank + t, cols[1] - cols[0]), inp[:, kk, t * 128:(t + 1) * 128],
                               w[:, k, cols[0]:cols[1]], start=kk == 0, stop=kk == kn - 1)
                        if kk == kn - 1 and t < ntok - 1:
                            m.then_inc(f.full, 1)
                    used(m)
                    k0 += kc

            def both_halves(L, name, parts, inp, f):
                t0 = T0[L, name]
                ntok, _ = tiles_of(L)
                n = len(parts)
                if n % 2:
                    for h in range(2):
                        by_token(t0 + h * n, parts, f, inp, ntok)
                else:
                    with pe.Fori(0, 2, 1) as i:
                        by_token(t0, parts, f, inp, ntok, i=i, per=n, done=ntok)
                    taken[f] += ntok

            def up(L, n_outer, f):
                t0 = T0[L, "up"]
                nctx = CTX if tiles_of(L)[0] == NT else 0
                with pe.Fori(0, n_outer, 1) as i:
                    for s in range(2):
                        by_channel(t0 + s, f, range(4), i=i, per=2, done=8, nctx=nctx)
                taken[f] += 8 * (n_outer - 1)
                if L >= 2:
                    by_channel(t0 + 10, f, range(4), nctx=nctx)

            def attend(L):
                heads, dv, P, PT, O, _ = att_frame(L)
                units = att_units(L)
                n = len(units)
                sf, tf, of = flow(L, "scores", 2), flow(L, "probsT", 1), flow(L, "heads", 1)
                stage(sf, tf, of)
                if L == 0:
                    pe.wait_ge(S("L0_keys_ready"), 1)
                u0, x0 = units_before(L), turns_ahead(L)
                ahead = L in next_of
                mod_flows_too(L)
                for step in range(n + 4):
                    if ahead and step % 8 == 3 and step < n:
                        mod_rows(next_of[L], step // 8, 7)
                    if ahead and step % 8 == 6 and step < n:
                        mod_columns(next_of[L], step // 8, 7, MOD_ROWS[L])
                    if step < n:
                        u = units[step]
                        x = place(sf) * 1024
                        for j, (col, w, a, b) in enumerate(u["prods"]):
                            m = mm(PS[:, x + col:x + col + w], a, b, start=True, stop=True)
                        m.then_inc(sf.full, 1)
                    if 1 <= step <= n:
                        u = units[step - 1]
                        pe.wait_ge(S("probs_ready"), u0 + step)
                        place(tf)
                        for j in range(len(u["vals"])):
                            m = tr(bank(4, 128, j * 128), P[:, (step - 1) % 2, u["first"] + j * 128:u["first"] + (j + 1) * 128], ident)
                        m.then_inc(tf.full, 1)
                    if 2 <= step <= n + 1:
                        u = units[step - 2]
                        pe.wait_ge(tf.free, 1 + u0 + x0 + nth_probsT(L, step - 2))
                        place(of)
                        for j, val in enumerate(u["vals"]):
                            m = mm(o_slot(step - 2, dv), PT[:, (step - 2) % 2, j * 128:(j + 1) * 128], val,
                                   start=j == 0, stop=j == len(u["vals"]) - 1)
                        m.then_inc(of.full, 1)
                    t = step // heads - 1
                    if t >= 0 and step == turn_step(L, t):
                        pe.wait_ge(of.free, of.slots + u0 + (t + 1) * heads)
                        place(tf)
                        for j in range(KD):
                            m = tr(bank(4, 128, j * 128), O[:, t % 2, j * 128:(j + 1) * 128], ident)
                        m.then_inc(tf.full, 1)
                        assert taken[tf] == u0 + x0 + nth_turn(L, t, n)

            def mixer0():
                t0 = T0[0, "in"]
                f, g, r = flow(0, "q", 4), flow(0, "v", NT), flow(0, "rot", 1)
                stage(f)
                by_channel(t0, f, range(4))
                by_channel(t0 + 1, f, range(4))
                by_channel(t0 + 2, f, range(2), last_used=False)
                stage(g)
                by_token(t0 + 2, [8], g, UT, NT, cols=(256, 512))
                stage(r)
                pe.wait_ge(S("attention_constants_in"), 32)
                for c in range(10):
                    place(r)
                    src = A_Q[:, c, 0:LAT] if c < 8 else A_KC[:, c - 8, 0:LAT]
                    mm(bank(7), catt("swap"), src, start=True, stop=True).then_inc(r.full, 1)
                attend(0)


            def mixer2():
                t0 = T0[2, "in"]
                f = flow(2, "uf", 4)
                stage(f)
                by_channel(t0, f, range(4))
                f = flow(2, "fx", 2)
                stage(f)
                pe.wait_ge(S("fourier_tables_in"), 16)
                for t in range(NT):
                    x = place(f) * 1024
                    for g in range(4):
                        m = mm(PS[:, x + g * 256:x + (g + 1) * 256], C_UF[:, g, t * 128:(t + 1) * 128], four("dftd"), start=True, stop=True)
                    m.then_inc(f.full, 1)
                f = flow(2, "ft", 2)
                stage(f)
                for g in range(4):
                    x = place(f) * 1024
                    for a, n, tt, kinds in ((0, LAT, range(TL), ("cosl", "sinl")), (512, CTX, range(TL, NT), ("cosc", "sinc"))):
                        for j, t in enumerate(tt):
                            for w, kind in enumerate(kinds):
                                m = mm(PS[:, x + a:x + a + n], C_X[:, t, g * 256 + w * 128:g * 256 + (w + 1) * 128],
                                       four(kind)[:, j * n:(j + 1) * n], start=j + w == 0, stop=j == len(tt) - 1 and w == 1)
                    m.then_inc(f.full, 1)
                f = flow(2, "qk", 4)
                stage(f)
                by_channel(t0 + 1, f, range(4))
                f = flow(2, "z", 1)
                stage(f)
                pe.wait_ge(S("gate_weights_in"), 80)
                place(f)
                for k in range(KD):
                    mm(PS[0:16, 0:LAT], C_WZ[:, k, :], UT[:, k, 0:LAT], start=k == 0, stop=k == KD - 1)
                    m = mm(PS[0:16, 512:512 + CTX], C_WZ[:, k, :], UT[:, k, LAT:TOK], start=k == 0, stop=k == KD - 1)
                m.then_inc(f.full, 1)
                f = flow(2, "la", NT)
                stage(f)
                for t in range(NT):
                    mm(bank(place(f)), C_ZT[0:17, t * 128:(t + 1) * 128], C_WG[0:17, :], start=True, stop=True).then_inc(f.full, 1)
                f = flow(2, "vr", NT)
                stage(f)
                by_token(t0 + 2, [8], f, UT, NT)
                stage(f)
                by_token(t0 + 3, [8], f, UT, NT)
                f = flow(2, "bt", 4)
                stage(f)
                pe.wait_ge(S("L2_decays_ready"), 1)
                for a in range(4):
                    x = place(f) * 1024
                    for t in range(NT):
                        m = mm(PS[:, x + t * 128:x + (t + 1) * 128], C_LA[:, t, a * 128:(a + 1) * 128], cs(("upto", "downto")[a // 2]), start=True, stop=True)
                    m.then_inc(f.full, 1)
                f = flow(2, "ec", NT)
                stage(f)
                for t in range(NT):
                    b = place(f)
                    for dr in range(2):
                        m = mm(bank(b, 256, dr * 256), cs(("after", "before")[dr]), C_LA[:, t, dr * 256:(dr + 1) * 256], start=True, stop=True)
                    m.then_inc(f.full, 1)
                f = flow(2, "kt", NT)
                stage(f)
                for t in range(NT):
                    b = place(f)
                    for a in range(2):
                        m = tr(bank(b, 128, a * 128), C_QK[:, 2 + a, t * 128:(t + 1) * 128], ident)
                    m.then_inc(f.full, 1)
                f = flow(2, "st", 2)
                stage(f)
                for dr in range(2):
                    for t in gla_orders()[dr][:-1]:
                        b = place(f)
                        for h in range(GLA_H):
                            half = (h % 2) * 64
                            m = mm(PS[half:half + 64, b * 512 + (h // 2) * 128:b * 512 + (h // 2) * 128 + 128],
                                   C_KE[:, t, dr * 256 + h * 64:dr * 256 + (h + 1) * 64], C_V[:, t, h * 128:(h + 1) * 128], start=True, stop=True)
                        m.then_inc(f.full, 1)
                lv, go, gt = flow(2, "levels", 2), flow(2, "mixed_heads", 1), flow(2, "turned", 1)
                stage(lv, go, gt)
                mod_flows_too(2)
                def turn(t):
                    pe.wait_ge(S("L2_heads_ready"), t + 1)
                    b = 6 + place(gt)
                    for k in range(4):
                        m = tr(bank(b, 128, k * 128), C_O[:, k * 128:(k + 1) * 128], ident)
                    m.then_inc(gt.full, 1)

                for t in range(NT):
                    for dr in range(2):
                        pe.wait_ge(S("L2_levels_ready"), 2 * t + dr + 1)
                        for v_ in range(GLA_LEVELS):
                            b = place(lv) * 2
                            for h in (0, 1, 2, 3):
                                rows, a = slice((h % 2) * 64, (h % 2) * 64 + 64), h // 2
                                ts = slice(t * 128, (t + 1) * 128)
                                kk = C_KL[rows, v_, a, :] if v_ < 7 else C_QK[rows, 2 + a, ts]
                                qq = C_QL[rows, v_, a, :] if v_ < 7 else C_QK[rows, a, ts]
                                m = mm(bank(b + h % 2, 128, a * 128), kk, qq, start=True, stop=True)
                            m.then_inc(lv.full, 1)
                            if v_ == 3 and 2 in next_of and t + dr:
                                mod_columns(3, 2 * t + dr - 1, 7, MOD_ROWS[2])
                        if 2 in next_of:
                            mod_rows(3, 2 * t + dr, 7)
                    if t:
                        turn(t - 1)
                    if t == 0:
                        pe.wait_ge(S("L2_states_ready"), 1)
                    pe.wait_ge(S("L2_attention_ready"), 2 * t + 2)
                    b = 4 + place(go)
                    first = [o[0] for o in gla_orders()]
                    for h in range(GLA_H):
                        rows, a = slice((h % 2) * 64, (h % 2) * 64 + 64), h // 2
                        ops = [(C_AT[:, dr, h % 2 * 2 + a, :], C_V[:, t, h * 128:(h + 1) * 128]) for dr in range(2)]
                        ops += [(C_QB[rows, 2 * dr + a, t * 128:(t + 1) * 128], C_S[rows, dr * 6 + t, a * 128:(a + 1) * 128])
                                for dr in range(2) if t != first[dr]]
                        for j, (x, y) in enumerate(ops):
                            m = mm(bank(b + h % 2, 128, a * 128), x, y, start=j == 0, stop=j == len(ops) - 1)
                    m.then_inc(go.full, 1)
                if 2 in next_of:
                    mod_columns(3, 11, 7, MOD_ROWS[2])
                turn(NT - 1)

            def mixer3():
                t0 = T0[3, "in"]
                f = flow(3, "kv", NT)
                stage(f)
                by_token(t0, [8], f, UT, NT)
                f = flow(3, "q", TL)
                stage(f)
                by_token(t0 + 1, [8], f, UT, TL)
                by_token(t0 + 2, [8], f, UT, TL)
                f = flow(3, "turned", 2)
                stage(f)
                for t in (0, 3):
                    pe.wait_ge(S("L3_heads_normed"), t + 3)
                    x = place(f) * 1024
                    for h in range(2):
                        for j in range(3):
                            m = tr(PS[:, x + h * 384 + j * 128:x + h * 384 + (j + 1) * 128], B_QK[:, t + j, 1024 + h * 128:1024 + (h + 1) * 128], ident)
                    m.then_inc(f.full, 1)
                for t in range(TL):
                    pe.wait_ge(S("L3_heads_normed"), NT + TL + t + 1)
                    x = place(f) * 1024
                    for h in range(8):
                        m = tr(PS[:, x + h * 128:x + (h + 1) * 128], B_QK[:, t, h * 128:(h + 1) * 128], ident)
                    m.then_inc(f.full, 1)
                attend(3)

            def mixer1():
                f = flow(1, "dt", NT)
                stage(f)
                pe.wait_ge(S("ssm_vectors_in"), 96)
                for t in range(NT):
                    b = place(f)
                    for k in range(KD):
                        m = mm(bank(b, 64), UT[:, k, t * 128:(t + 1) * 128], SSM_WDT[:, k, :], start=k == 0, stop=k == KD - 1)
                    m.then_inc(f.full, 1)
                fb = flow(1, "bias", 1)
                settled.append(fb)
                place(fb)
                for a in range(6):
                    m = tr(bank(7, 24, 24 * a), SSM_CW_ROWS[:, a * 128:(a + 1) * 128], ident[0:24, 0:24])
                m.then_inc(fb.full, 1)
                cv, z, xt = flow(1, "conv", 4), flow(1, "z", TL), flow(1, "xt", 2)
                gf, sf, df, of, yf, tf = (flow(1, "bc", 1), flow(1, "state", 2), flow(1, "decay", 2), flow(1, "off", 1),
                                          flow(1, "diag", 1), flow(1, "turned", 1))
                for g in range(SSM_G):
                    t0 = T0[1, "in"] + per_group * g
                    stage(cv)
                    by_channel(t0, cv, range(1))
                    by_channel(t0 + 1, cv, range(1), nctx=0)
                    by_channel(t0 + 2, cv, range(4))
                    if g == 0:
                        f = flow(1, "acs", NT)
                        stage(f)
                        pe.wait_ge(S("L1_a_ready"), 1)
                        for t in range(NT):
                            b = place(f)
                            mm(bank(b, 32), cs("upto"), SSM_A[:, t, 0:32], start=True, stop=True)
                            mm(bank(b, 32, 32), cs("downto"), SSM_A[:, t, 32:64], start=True, stop=True)
                            mm(bank(b, 64, 64), ones, SSM_A[:, t, :], start=True, stop=True).then_inc(f.full, 1)
                        stage(z)
                    else:
                        pe.wait_ge(cv.free, taken[cv] - 2 + cv.slots)
                    by_token(t0 + 3, [8], z, UT, TL, first_bank=4)
                    settled[:] = [cv, z]
                    stage(xt)
                    for n in range(5):
                        pe.wait_ge(S("L1_channels_ready"), 6 * g + (2 + n + 1 if n < 4 else 1))
                        x = place(xt) * 1024
                        src = SSM_XT[:, n, :] if n < 4 else SSM_BT
                        for t in range(NT):
                            m = tr(PS[:, x + t * 128:x + (t + 1) * 128], src[:, t * 128:(t + 1) * 128], ident)
                        m.then_inc(xt.full, 1)
                    stage(gf, sf, df, of, yf, tf)
                    mod_flows_too(1)
                    place(gf)
                    for c in range(TL):
                        cc = slice(c * 128, (c + 1) * 128)
                        m = mm(bank(0, 128, c * 128), SSM_BT[:, cc], SSM_CT[:, cc], start=True, stop=True)
                    m.then_inc(gf.full, 1)
                    for n in range(10):
                        c = SSM_ORDERS[n // 5][n % 5]
                        pe.wait_ge(S("L1_state_input_ready"), 10 * g + n + 1)
                        b = 1 + place(sf)
                        mm(bank(b), SSM_BK[:, c, :], SSM_XW[:, n % 2, :], start=True, stop=True).then_inc(sf.full, 1)

                    def turn(c):
                        pe.wait_ge(S("L1_normed"), TL * g + c + 1)
                        if c == 0:
                            pe.wait_ge(gf.free, 1 + taken[gf])
                        place(tf)
                        for k in range(4):
                            m = tr(bank(0, 128, k * 128), SSM_T1[:, k * 128:(k + 1) * 128], ident)
                        m.then_inc(tf.full, 1)

                    def sums(k):
                        q = k % 4
                        b = 3 + place(df)
                        for dr in range(2):
                            for hh in range(2):
                                col = dr * 32 + g * 8 + 2 * q + hh
                                m = mm(bank(b, 128, (2 * dr + hh) * 128), SSM_A[:, k // 4, col:col + 1].to_broadcast([128, 128]),
                                       cs(("upto", "downto")[dr]), start=True, stop=True)
                        m.then_inc(df.full, 1)

                    sums(0)
                    sums(1)
                    for k in range(16):
                        c, q = k // 4, k % 4
                        if k + 2 < 16:
                            sums(k + 2)
                        pe.wait_ge(S("L1_weights_ready"), 16 * g + k + 1)
                        if q == 0:
                            pe.wait_ge(S("L1_inputs_ready"), 2 * (TL * g + c + 1))
                            place(yf)
                        for hh in range(2):
                            h = 2 * q + hh
                            for dr in range(2):
                                m = mm(bank(5, 64, h * 64), SSM_DM[:, k % 4, (2 * dr + hh) * 128:(2 * dr + hh + 1) * 128],
                                       SSM_XDT[:, c % 2, dr, h * 64:(h + 1) * 64], start=dr == 0, stop=dr == 1)
                        m.then_inc(S("L1_weights_used"), 1)
                        if q == 1:
                            if c == 0:
                                pe.wait_ge(S("L1_states_ready"), g + 1)
                            place(of)
                            for dr in range(2):
                                sn = sn_slot(dr, c + 2 if dr == 0 else 5 - c)
                                m = mm(bank(6 + dr), SSM_CT[:, c * 128:(c + 1) * 128], SN[:, sn, :], start=True, stop=True)
                            m.then_inc(of.full, 1)
                        if q == 2 and c:
                            turn(c - 1)
                        if q == 3 and c < 3 and 1 in next_of:
                            mod_rows(next_of[1], 3 * g + c, 1)
                        if q == 2 and c and 1 in next_of:
                            mod_columns(next_of[1], 3 * g + c - 1, 1, MOD_ROWS[1])
                    turn(TL - 1)

            pe.wait_ge(S("constants_in"), 16)
            for L in layers:
                if L == layers[0]:
                    modulation_start(L)
                bias_columns(L)
                norm = L >= 2
                transposed_input(L, "m", big(0, NT, D) if norm else H)
                gates(L)
                (mixer0, mixer1, mixer2, mixer3)[L]()
                f = flow(L, "mixed", tiles_of(L)[0])
                stage(f)
                if L == 1:
                    both_halves(L, "out", [8, 8], SSM_YT, f)
                else:
                    both_halves(L, "out", [8], C_MIX if L == 2 else UT, f)
                transposed_input(L, "f", big(0, NT, D) if norm else H)
                if L >= 2:
                    fb = flow(L, "bias", 1)
                    stage(fb)
                    pe.wait_ge(S("conv_vectors_in"), 32 * (second.index(L) + 1))
                    place(fb)
                    for a in range(4):
                        m = tr(bank(0, 2 * NF2, 2 * NF2 * a), CONV_ROWS[:, a * 128:(a + 1) * 128], ident[0:2 * NF2, 0:2 * NF2])
                    m.then_inc(fb.full, 1)
                f = flow(L, "up", 4)
                stage(f)
                up(L, 4 if L < 2 else 5, f)
                f = flow(L, "down", tiles_of(L)[0])
                stage(f)
                pe.wait_ge(S("hidden_ready"), nth(L))
                both_halves(L, "down", [8] * 4 if L < 2 else F2_PARTS, big(0, 32 if L < 2 else NF2, TOK), f)

        @block.vector
        def _(dve):
            V = nc.vector
            step = Link(dve, "vector_steps")
            got = {}
            fulls = {}

            def offer(f):
                if f in got:
                    return
                dve.sem_inc(f.free, f.slots)
                got[f] = 0
                fulls[f] = 0

            def ready(f, tile=None, i=None, per=0, tper=0):
                if tile is None:
                    fulls[f] += 1
                    dve.wait_ge(f.full, v(fulls[f], i, per))
                else:
                    dve.wait_ge(wused, v(tile + 1, i, tper))

            def give(f, ins, i=None, per=0):
                got[f] += 1
                ins.then_inc(f.free, 1)
                dve.wait_ge(f.free, v(f.slots + got[f], i, per))

            def post(name, n=1):
                dve.sem_inc(S(name), n)

            def modulation(L):
                f = flow(L, "bias", 1)
                offer(f)
                ready(f)
                dve.wait_ge(S("mod_sums_ready"), 12 * nth(L))
                ins = V.tensor_tensor(MODC[:, :, :], MODC[:, :, :], bank(0, 48).unsqueeze(2).to_broadcast([128, 48, 2]), ALU.add)
                give(f, ins) if L < 2 else step(ins)
                for a, seg in enumerate((0, 1, 3, 4)):
                    step.go(V.tensor_scalar(COL[:, a], MODC[:, seg * KD:(seg + 1) * KD, :], float(a % 2), None, ALU.add))
                if L >= 2:
                    step.settle()
                    for w in range(2):
                        ins = V.tensor_tensor(COL[:, 2 * w + 1], COL[:, 2 * w + 1], bank(0, KD, 48 + w * KD).unsqueeze(2).to_broadcast([128, KD, 2]), ALU.mult)
                        give(f, ins) if w else step(ins)
                step.settle()
                post("columns_ready")

            def gates(L):
                for a in range(4):
                    seg = (2, 5)[a // 2]
                    step(V.tensor_tensor(DIAGONALS[:, a], ident.unsqueeze(1).to_broadcast([128, KD, 128]),
                                         MODC[:, seg * KD:(seg + 1) * KD, a % 2].unsqueeze(2).to_broadcast([128, KD, 128]), ALU.mult))
                    post("diagonals_ready")

            def transposed_input(L, which):
                f = flow(L, "u" + which + "_v", 2)
                offer(f)
                _, pieces = tiles_of(L)
                if which == "m":
                    pieces = 2
                w = 2 * (which == "f")
                for k in range(0, KD, 2):
                    ready(f)
                    x = (k // 2 % 2) * 2048
                    for p in range(pieces):
                        a, n = ((0, LAT), (LAT, CTX))[p]
                        ins = V.tensor_scalar(UT[:, k, a:a + n], PS[:, x + a:x + a + n], COL[:, w + 1, k, p:p + 1], COL[:, w, k, p:p + 1], ALU.mult, ALU.add)
                        if p == pieces - 1:
                            give(f, ins)
                        else:
                            step(ins)

            def residual(L, which, f, t0, n):
                ntok, _ = tiles_of(L)
                gi = 0 if which == "m" else 1
                tmp = RES_TMP[:, :]
                offer(f)
                for h in range(2):
                    for t in range(ntok):
                        if t == ntok - 1:
                            ready(f, t0 + (h + 1) * n - 1)
                        else:
                            ready(f)
                        lc = 1 if t >= TL else 0
                        hs = slice(h * 512, (h + 1) * 512)
                        give(f, V.tensor_tensor(tmp, bank(t), GATE[:, gi, lc, hs], ALU.mult))
                        if L < 2:
                            step(V.scalar_tensor_tensor(H[:, t, hs], H[:, t, hs], ALPHA, tmp, ALU.mult, ALU.add))
                            step(V.bn_stats(ST[:, t * 12 + h * 6:t * 12 + h * 6 + 6], H[:, t, hs]))
                            if h == 1:
                                step(V.bn_aggr(ST[:, 80 + 2 * t:82 + 2 * t], ST[:, t * 12:t * 12 + 12]))
                                step(V.tensor_scalar(ST[:, 96 + t:97 + t], ST[:, 81 + 2 * t:82 + 2 * t], LN_EPS, None, ALU.add))
                                post("variance_ready")
                                if t:
                                    norm(L, which, t - 1)
                                if t > 1 and which == "f" and next_of.get(L) == 2:
                                    rms_input(2, "m", t - 2)
                        else:
                            step(V.tensor_tensor(H[:, t, hs], H[:, t, hs], tmp, ALU.add))
                            if h == 1:
                                post(f"{which}_residual_ready")
                                if t:
                                    rms_after(L, which, t - 1)
                if L < 2:
                    norm(L, which, ntok - 1)
                    if which == "f" and next_of.get(L) == 2:
                        for t in range(ntok - 2, NT):
                            rms_input(2, "m", t)
                    post("norm_vectors_used")
                else:
                    rms_after(L, which, ntok - 1)

            def norm(L, which, t):
                dve.wait_ge(S("deviation_ready"), normed_before(L, which) + t + 1)
                step(V.reciprocal(ST[:, 104 + t:105 + t], ST[:, 112 + t:113 + t]))
                dve.wait_ge(S("norm_vectors_in"), 32 * (2 * layers.index(L) + 1 + (which == "f")))
                ht = H[:, t, :]
                step(V.scalar_tensor_tensor(ht, ht, ST[:, 80 + 2 * t:81 + 2 * t], GB[:, 0, :], ALU.subtract, ALU.mult))
                step(V.scalar_tensor_tensor(ht, ht, ST[:, 104 + t:105 + t], GB[:, 1, :], ALU.mult, ALU.add))
                if which == "m":
                    post("f_tokens_ready")
                elif next_of.get(L) == 2:
                    post("f_residual_ready")

            def rms_after(L, which, t):
                if which == "m":
                    rms_input(L, "f", t)
                elif L in next_of:
                    rms_input(next_of[L], "m", t)

            def rms_input(L, which, t):
                dve.wait_ge(S(f"{which}_rms_ready"), tiles_before(L, which) + t + 1 if which == "f" else NT * second.index(L) + t + 1)
                step(V.reciprocal(ST[:, 104 + t:105 + t], ST2[:, 8 + t:9 + t]))
                out = big(0, NT, D)
                step(V.tensor_scalar(out[:, t, :], H[:, t, :], ST[:, 104 + t:105 + t], None, ALU.mult))
                post(f"{which}_tokens_ready")

            def attend(L):
                heads, dv, P, PT, O, scale = att_frame(L)
                units = att_units(L)
                n = len(units)
                sf, of = flow(L, "scores", 2), flow(L, "heads", 1)
                offer(of)
                got.setdefault(sf, 0)
                fulls.setdefault(sf, 0)
                u0, x0 = units_before(L), turns_ahead(L)
                for k in range(n + 2):
                    if k < n:
                        u = units[k]
                        ready(sf)
                        x = (k % 2) * 1024
                        for col, name in u["masks"]:
                            step(V.tensor_tensor(PS[:, x + col:x + col + 128], PS[:, x + col:x + col + 128], catt(name), ALU.add))
                        step(V.reduce_max(ST[:, 128 + k % 8:129 + k % 8], PS[:, x + u["first"]:x + 768], AX.X))
                        neg = ST[:, 136 + k % 8:137 + k % 8]
                        if L == 0:
                            step(V.tensor_scalar(neg, ST[:, 128 + k % 8:129 + k % 8], A_SINK[:, u["h"]:u["h"] + 1], -scale, ALU.max, ALU.mult))
                        else:
                            step(V.tensor_scalar(neg, ST[:, 128 + k % 8:129 + k % 8], -scale, None, ALU.mult))
                        post("maxima_ready")
                    if k >= 2:
                        j = k - 2
                        u = units[j]
                        dve.wait_ge(S("probs_ready"), u0 + j + 1)
                        r = ST[:, 144 + j % 8:145 + j % 8]
                        if L == 0:
                            step(V.tensor_tensor(r, ST2[:, 16 + j % 8:17 + j % 8], ST2[:, 24 + j % 8:25 + j % 8], ALU.add))
                            step(V.reciprocal(r, r))
                        else:
                            step(V.reciprocal(r, ST2[:, 16 + j % 8:17 + j % 8]))
                        ready(of)
                        t = u["t"]
                        if u["h"] == 0 and t >= 2:
                            dve.wait_ge(flow(L, "probsT", 1).full, u0 + x0 + nth_turn(L, t - 2, n))
                        give(of, V.tensor_scalar(O[:, t % 2, u["h"] * dv:(u["h"] + 1) * dv], o_slot(j, dv), r, None, ALU.mult))

            def mixer0():
                g, r = flow(0, "v", NT), flow(0, "rot", 1)
                offer(g)
                for t in range(NT):
                    ready(g, T0[0, "in"] + 2 if t == NT - 1 else None)
                    give(g, V.tensor_copy(A_V[:, t, :], bank(t, 256)))
                offer(r)
                dve.wait_ge(S("attention_constants_in"), 32)
                step(V.tensor_scalar(A_SINK, A_SINK, float(DA) ** 0.5, None, ALU.mult))
                cosT, sinT = catt("cosT"), catt("sinT")
                for c in range(10):
                    ready(r)
                    give(r, V.tensor_tensor(A_ROT, bank(7), sinT, ALU.mult))
                    if c < 8:
                        step(V.tensor_tensor(A_QR[:, c, :], A_Q[:, c, 0:LAT], cosT, ALU.mult))
                        step(V.tensor_tensor(A_QR[:, c, :], A_QR[:, c, :], A_ROT, ALU.add))
                    else:
                        kc = A_KC[:, c - 8, 0:LAT]
                        step(V.tensor_tensor(kc, kc, cosT, ALU.mult))
                        step(V.tensor_tensor(kc, kc, A_ROT, ALU.add))
                for g_ in range(GA):
                    h0 = (g_ % 2) * 64
                    for h in range(2):
                        step(V.tensor_copy(A_KD[h * 64:h * 64 + 64, g_, :], A_KC[h0:h0 + 64, g_ // 2, :]))
                post("L0_keys_ready")
                attend(0)

            def mixer2():
                f = flow(2, "fx", 2)
                offer(f)
                for t in range(NT):
                    ready(f)
                    give(f, V.tensor_copy(C_X[:, t, :], PS[:, t % 2 * 1024:t % 2 * 1024 + 1024]))
                step(V.memset(C_ZT[0:17, :], 1.0))
                post("L2_ones_ready")
                la = C_LA[:, :, :].rearrange("p t n -> p (t n)")
                offer(flow(2, "vr", NT))
                dve.wait_ge(S("L2_logits_ready"), 1)
                step(V.scalar_tensor_tensor(C_T1, la, -1.0, la, ALU.mult, ALU.min))
                post("L2_minus_abs_ready")
                step(V.tensor_scalar(la, la, 0.0, 1.0 / 16.0, ALU.min, ALU.mult))
                dve.wait_ge(S("L2_log_ready"), 1)
                step(V.scalar_tensor_tensor(la, C_T1, -1.0 / 16.0, la, ALU.mult, ALU.add))
                post("L2_decays_ready")
                f = flow(2, "vr", NT)
                offer(f)
                t0 = T0[2, "in"]
                for t in range(NT):
                    ready(f, t0 + 2 if t == NT - 1 else None)
                    give(f, V.tensor_copy(C_V[:, t, :], bank(t)))
                dve.wait_ge(S("gate_weights_in"), 80)
                for t in range(NT):
                    dve.wait_ge(S("L2_r_ready"), t + 1)
                    step(V.tensor_tensor(C_R[:, t, :], C_R[:, t, :], C_GAIN, ALU.mult))
                step(V.memset(GB[:, 1, :], 0.0))
                f = flow(2, "bt", 4)
                offer(f)
                for a in range(4):
                    ready(f)
                    give(f, V.tensor_copy(C_BT[:, a, :], PS[:, a * 1024:a * 1024 + TOK]))
                    post("L2_sums_ready")
                def differences(n):
                    t, dr = n // 2, n % 2
                    for v_ in range(7):
                        e, b, ref = level_views(dr, t, v_)
                        step.go(V.tensor_tensor(e, b, ref, ALU.subtract))
                    step.settle()
                    post("L2_differences_ready")

                def products(n):
                    t = n // 2
                    ts = slice(t * 128, (t + 1) * 128)
                    dve.wait_ge(S("L2_level_decays_ready"), n + 1)
                    for dst, a in ((C_QL, 0), (C_KL, 2)):
                        step(V.tensor_tensor(dst, C_EXP, C_QK[:, a:a + 2, ts].unsqueeze(1).to_broadcast([128, 7, 2, 128]), ALU.mult))
                    post("L2_levels_ready")

                differences(0)
                f = flow(2, "kt", NT)
                offer(f)
                for t in range(NT):
                    ready(f)
                    dve.wait_ge(flow(2, "ec", NT).free, NT + NT + t + 1)
                    step(V.tensor_tensor(C_KE[:, t, 0:256], C_KE[:, t, 0:256], bank(t, 256), ALU.mult))
                    give(f, V.tensor_tensor(C_KE[:, t, 256:512], C_KE[:, t, 256:512], bank(t, 256), ALU.mult))
                dve.wait_ge(S("L2_query_decay_ready"), 1)
                for dr in range(2):
                    qb = C_QB[:, 2 * dr:2 * dr + 2, :]
                    last = qb.rearrange("p a (t l) -> p a t l", l=128)[:, :, :, 127 * (1 - dr)]
                    step(V.tensor_copy(C_DL[:, 2 * dr:2 * dr + 2, :], last))
                    step(V.tensor_tensor(qb, qb, C_QK[:, 0:2, :], ALU.mult))
                products(0)
                f = flow(2, "st", 2)
                offer(f)
                n = 0
                for dr in range(2):
                    o = gla_orders()[dr]
                    for j in range(NT - 1):
                        ready(f)
                        new = C_S[:, dr * 6 + o[j + 1], :]
                        if j == 0:
                            give(f, V.tensor_copy(new, bank(n % 2, 256)))
                        else:
                            old = C_S[:, dr * 6 + o[j], :]
                            dl = lambda a: C_DL[:, 2 * dr + a, o[j]:o[j] + 1]
                            step(V.scalar_tensor_tensor(new[:, 0:128], old[:, 0:128], dl(0), bank(n % 2, 128), ALU.mult, ALU.add))
                            give(f, V.scalar_tensor_tensor(new[:, 128:256], old[:, 128:256], dl(1), bank(n % 2, 128, 128), ALU.mult, ALU.add))
                        n += 1
                post("L2_states_ready")
                lv, go = flow(2, "levels", 2), flow(2, "mixed_heads", 1)
                offer(lv)
                got[go] = fulls[go] = 0
                dve.sem_inc(go.free, 1)
                dve.wait_ge(S("gla_masks_in"), 16)

                def heads(t):
                    dve.wait_ge(S("L2_head_rms_ready"), t + 1)
                    r = ST[:, 120:124]
                    step(V.reciprocal(r, ST2[:, 36:40]))
                    if t:
                        dve.wait_ge(flow(2, "turned", 1).full, t)
                    o3 = C_O.rearrange("p (a s e) -> p s a e", a=2, s=2)
                    ps = PS[:, 2048:3072].rearrange("p (s x) -> p s x", s=2)[:, :, 0:256].rearrange("p s (a e) -> p s a e", a=2)
                    r3 = r.rearrange("p (a s) -> p s a", s=2).unsqueeze(3).to_broadcast([128, 2, 2, 128])
                    give(go, V.tensor_tensor(o3, ps, r3, ALU.mult))
                    step(V.tensor_tensor(C_O, C_O, C_R[:, t, :], ALU.mult))
                    post("L2_heads_ready")

                for n in range(2 * NT):
                    t, dr = n // 2, n % 2
                    if n + 1 < 2 * NT:
                        differences(n + 1)
                    if t:
                        dve.wait_ge(go.full, t)
                    for v_ in range(GLA_LEVELS):
                        ready(lv)
                        b = (n * GLA_LEVELS + v_) % 2 * 2
                        data = PS[:, b * 512:b * 512 + 1024].rearrange("p (s x) -> p s x", s=2)[:, :, 0:256]
                        give(lv, V.copy_predicated(C_AT[:, dr].rearrange("p (s a) i -> p s a i", s=2),
                                                   C_MASK[:, dr, v_, :].unsqueeze(1).unsqueeze(1).to_broadcast([128, 2, 2, 128]),
                                                   data.rearrange("p s (a i) -> p s a i", a=2)))
                    post("L2_attention_ready")
                    if n + 1 < 2 * NT:
                        products(n + 1)
                    if dr == 0 and t:
                        heads(t - 1)
                heads(NT - 1)

            def mixer3():
                dve.wait_ge(S("second_attention_constants_in"), 48)
                cos = B_CONST[:, 0:256].rearrange("p (t n) -> p t n", t=TL)
                sin = B_CONST[:, 256:512].rearrange("p (t n) -> p t n", t=TL)
                q3 = lambda a: a.rearrange("p (h e) -> p h e", e=128)
                q4 = lambda a: a.rearrange("p (h s e) -> p h s e", s=2, e=64)
                for s_, (t, c0, nh) in enumerate(head_pieces()):
                    dve.wait_ge(S("L3_qk_in"), s_ + 1)
                    qk, sq, t2 = B_QK[:, t, c0:c0 + nh * 128], B_SQ[:, 0:nh * 128], B_T2[:, 0:nh * 128]
                    step(V.tensor_tensor(sq, qk, qk, ALU.mult))
                    step(V.reduce_sum(ST[:, 0:nh], q3(sq), AX.X))
                    post("L3_head_squares_ready")
                    dve.wait_ge(S("L3_head_rms_ready"), s_ + 1)
                    step(V.reciprocal(ST[:, 32:32 + nh], ST[:, 16:16 + nh]))
                    step(V.tensor_tensor(q3(qk), q3(qk), ST[:, 32:32 + nh].unsqueeze(2).to_broadcast([128, nh, 128]), ALU.mult))
                    gain = B_G[:, 128:256] if c0 == 1024 else B_G[:, 0:128]
                    step(V.tensor_tensor(q3(qk), q3(qk), gain.unsqueeze(1).to_broadcast([128, nh, 128]), ALU.mult))
                    if t < TL:
                        c = cos[:, t, :].unsqueeze(1).to_broadcast([128, nh, 64])
                        s = sin[:, t, :].unsqueeze(1).to_broadcast([128, nh, 64])
                        x, a, b = q4(qk), q4(sq), q4(t2)
                        for hf in range(2):
                            step.go(V.tensor_tensor(a[:, :, hf, :], x[:, :, hf, :], c, ALU.mult))
                            step.go(V.tensor_tensor(b[:, :, hf, :], x[:, :, 1 - hf, :], s, ALU.mult))
                        step.settle()
                        step.go(V.tensor_tensor(x[:, :, 0, :], a[:, :, 0, :], b[:, :, 0, :], ALU.subtract))
                        step(V.tensor_tensor(x[:, :, 1, :], a[:, :, 1, :], b[:, :, 1, :], ALU.add))
                    post("L3_heads_normed")
                attend(3)

            def mixer1():
                f = flow(1, "dt", NT)
                offer(f)
                dve.wait_ge(S("ssm_vectors_in"), 96)
                for t in range(NT):
                    ready(f)
                    give(f, V.tensor_tensor(SSM_DT[:, t, :], bank(t, 64), SSM_DTB, ALU.add))
                fb = flow(1, "bias", 1)
                ready(fb)
                give(fb, V.tensor_copy(SSM_CW[:, :, :].rearrange("p a j -> p (a j)"), bank(7, 144)))
                flat = lambda a: a.rearrange("p t n -> p (t n)")
                dt, am = flat(SSM_DT), flat(SSM_A)
                e, u, lg = flat(SSM_WD), flat(SSM_EACS), flat(SSM_ETOT)
                step(V.scalar_tensor_tensor(e, dt, -1.0, dt, ALU.mult, ALU.min))
                post("L1_minus_abs_ready")
                dve.wait_ge(S("L1_exp_ready"), 1)
                step(V.tensor_scalar(u, e, 1.0, None, ALU.add))
                post("L1_one_plus_ready")
                step(V.scalar_tensor_tensor(e, u, 1.0, e, ALU.subtract, ALU.subtract))
                dve.wait_ge(S("L1_log_ready"), 1)
                step(V.reciprocal(u, u))
                step(V.tensor_tensor(e, e, u, ALU.mult))
                step(V.tensor_tensor(lg, lg, e, ALU.subtract))
                step(V.scalar_tensor_tensor(dt, dt, 0.0, lg, ALU.max, ALU.add))
                step(V.scalar_tensor_tensor(SSM_A, SSM_DT, -1.0, SSM_ALOG.unsqueeze(1).to_broadcast([128, NT, 64]), ALU.mult, ALU.mult))
                post("L1_a_ready")
                cv = flow(1, "conv", 4)
                gf, sf, df, of, yf, tf = (flow(1, "bc", 1), flow(1, "state", 2), flow(1, "decay", 2), flow(1, "off", 1),
                                          flow(1, "diag", 1), flow(1, "turned", 1))
                for f in (cv, gf, sf, df, of):
                    offer(f)
                dve.sem_inc(yf.free, 1)
                got[yf] = 0

                for g in range(SSM_G):
                    t0 = T0[1, "in"] + per_group * g
                    for n in range(6):
                        ready(cv, t0 + n if n < 2 else t0 + 2 if n == 5 else None)
                        x = n % 4 * 1024
                        y, j = ((SSM_BT, 16 + g), (SSM_CT, 20 + g))[n] if n < 2 else (SSM_XT[:, n - 2, :], 4 * g + n - 2)
                        ends = ((0, LAT), (LAT, TOK))[:1 if n == 1 else 2]
                        w = lambda a: SSM_CW[:, a, j:j + 1]
                        m = ends[-1][1]
                        step(V.tensor_scalar(y[:, 0:m], PS[:, x:x + m], w(2), w(5), ALU.mult, ALU.add))
                        for k in (0, 1, 3, 4):
                            o = k - 2
                            for e_, (a, b) in enumerate(ends):
                                lo, hi = max(a, a - o), min(b, b - o)
                                ins = V.scalar_tensor_tensor(y[:, lo:hi], PS[:, x + lo + o:x + hi + o], w(k), y[:, lo:hi], ALU.mult, ALU.add)
                                if k == 4 and e_ == len(ends) - 1:
                                    give(cv, ins)
                                else:
                                    step(ins)
                        post("L1_convolved")
                    if g == 0:
                        f = flow(1, "acs", NT)
                        offer(f)
                        for t in range(NT):
                            ready(f)
                            step(V.tensor_copy(SSM_ACS[:, t, :], bank(t, 64)))
                            step(V.tensor_copy(SSM_ETOT[:, t, :], bank(t, 64, 64)))
                            give(f, V.tensor_tensor(SSM_WD[:, t, :], SSM_ETOT[:, t, :], SSM_ACS[:, t, :], ALU.subtract))
                        post("L1_sums_ready")
                        dve.wait_ge(S("L1_decays_ready"), 1)
                        step(V.tensor_tensor(SSM_WD, SSM_WD, SSM_DT, ALU.mult))
                    ready(gf)
                    for dr in range(2):
                        mask = cs(("upto", "downto")[dr]).unsqueeze(1).to_broadcast([128, TL, 128])
                        ins = V.tensor_tensor(SSM_GM[:, dr], bank(0).rearrange("p (c l) -> p c l", c=TL), mask, ALU.mult)
                        give(gf, ins) if dr else step(ins)
                    dve.wait_ge(S("L1_tokens_ready"), 5 * (g + 1))

                    for n in range(10):
                        dr, j = n // 5, n % 5
                        ready(sf)
                        new = SN[:, sn_slot(dr, j + 1), :]
                        ps = bank(1 + n % 2)
                        if j == 0:
                            give(sf, V.tensor_copy(new, ps))
                        else:
                            old = SN[:, sn_slot(dr, j), :]
                            step(V.tensor_tensor(by_head(new), by_head(old), heads_of(SSM_ETOT, SSM_ORDERS[dr][j], dr, g), ALU.mult))
                            give(sf, V.tensor_tensor(new, new, ps, ALU.add))
                    post("L1_states_ready")

                    def gated(c):
                        if c or g:
                            dve.wait_ge(tf.full, TL * g + c)
                        ready(of)
                        step.go(V.tensor_tensor(by_head(SSM_T1), by_head(bank(6)), heads_of(SSM_EACS, c, 0, g), ALU.mult))
                        give(of, V.tensor_tensor(by_head(SSM_T2), by_head(bank(7)), heads_of(SSM_EACS, c, 1, g), ALU.mult))
                        step(V.tensor_tensor(SSM_T1, SSM_T1, SSM_T2, ALU.add))
                        dve.wait_ge(S("L1_skip_ready"), TL * g + c + 1)
                        step(V.tensor_tensor(SSM_T1, SSM_T1, SSM_SKIP, ALU.add))
                        dve.wait_ge(S("L1_weights_used"), 16 * g + 4 * (c + 1))
                        give(yf, V.tensor_tensor(SSM_T1, SSM_T1, bank(5), ALU.add))
                        step(V.tensor_tensor(SSM_T1, SSM_T1, ssm_z(c), ALU.mult))
                        post("L1_gated")

                    def normed(c):
                        dve.wait_ge(S("L1_rms_ready"), TL * g + c + 1)
                        step(V.reciprocal(ST[:, 124:125], ST2[:, 33:34]))
                        dve.wait_ge(S("ssm_gain_in"), 16)
                        step(V.scalar_tensor_tensor(SSM_T1, SSM_T1, ST[:, 124:125], SSM_NG[:, g * 512:(g + 1) * 512], ALU.mult, ALU.mult))
                        post("L1_normed")

                    for k in range(19):
                        if k < 16:
                            c, q = k // 4, k % 4
                            ready(df)
                            if k >= 4 or g:
                                dve.wait_ge(S("L1_weights_used"), 16 * g + max(k - 3, 0))
                            dm = SSM_DM[:, k % 4, :]
                            for n in range(4):
                                col = n // 2 * 32 + g * 8 + 2 * q + n % 2
                                ins = V.tensor_scalar(dm[:, n * 128:(n + 1) * 128], bank(3 + k % 2, 128, n * 128), SSM_ACS[:, c, col:col + 1], 0.0, ALU.subtract, ALU.min)
                                give(df, ins) if n == 3 else step.go(ins)
                            post("L1_exponents_ready")
                        if k >= 5 and k % 4 == 1:
                            gated((k - 2) // 4)
                        if k >= 6 and k % 4 == 2:
                            normed((k - 3) // 4)
                post("L1_scan_done")

            def feed_forward(L):
                f = flow(L, "up", 4)
                nlat = LAT
                _, pieces = tiles_of(L)
                ends = ((0, LAT), (LAT, TOK))[:pieces]
                hid = big(0, NF2, TOK)
                cw = CONV_W2
                n = TOK if pieces == 2 else LAT
                fb = flow(L, "bias", 1)
                ready(fb)
                give(fb, V.tensor_copy(CONV_W2[:, :, :].rearrange("p a j -> p (a j)"), bank(0, 8 * NF2)))
                t0 = T0[L, "up"]
                offer(f)

                for tile in range(11):
                    for c in range(4):
                        j = tile * 4 + c
                        ready(f, t0 + tile if c == 3 else None)
                        x = (j % 4) * 1024
                        y = CONV_Y[:, j % 2, :]
                        if 2 <= j < NF2 + 2:
                            dve.wait_ge(S("gates_done"), NF2 * second.index(L) + j - 1)
                        w = lambda a: cw[:, a, j:j + 1]
                        step(V.tensor_scalar(y[:, 0:n], PS[:, x:x + n], w(1), w(3), ALU.mult, ALU.add))
                        for a, b in ends:
                            step(V.scalar_tensor_tensor(y[:, a + 1:b], PS[:, x + a:x + b - 1], w(0), y[:, a + 1:b], ALU.mult, ALU.add))
                        for e_, (a, b) in enumerate(ends):
                            ins = V.scalar_tensor_tensor(y[:, a:b - 1], PS[:, x + a + 1:x + b], w(2), y[:, a:b - 1], ALU.mult, ALU.add)
                            if e_ == len(ends) - 1:
                                give(f, ins)
                            else:
                                step(ins)
                        if j < NF2:
                            post("gates_convolved")
                        else:
                            h = hid[:, j - NF2, 0:n]
                            step(V.tensor_tensor(h, h, y[:, 0:n], ALU.mult))
                post("hidden_ready")
                post("conv_vectors_used")

            step(V.memset(EPSC, EPS2))
            step(V.memset(RMSC, RMS_EPS))
            post("eps_ready")
            for L in layers:
                ntok, _ = tiles_of(L)
                if L == layers[0]:
                    dve.wait_ge(S("tokens_in"), 32)
                    if L < 2:
                        post("m_tokens_ready", NT)
                elif L == 1:
                    post("m_tokens_ready", NT)
                modulation(L)
                if L >= 2 and L == layers[0]:
                    for t in range(NT):
                        rms_input(L, "m", t)
                transposed_input(L, "m")
                gates(L)
                (mixer0, mixer1, mixer2, mixer3)[L]()
                n = 2 if L == 1 else 1
                residual(L, "m", flow(L, "mixed", ntok), T0[L, "out"], n)
                transposed_input(L, "f")
                if L >= 2:
                    feed_forward(L)
                residual(L, "f", flow(L, "down", ntok), T0[L, "down"], 4)
                post("layer_done")
            if layers[-1] == 3:
                dve.wait_ge(S("norm_vectors_in"), NORM_FINAL)
                for t in range(TL):
                    dve.wait_ge(S("final_rms_ready"), t + 1)
                    step(V.reciprocal(ST[:, 104 + t:105 + t], ST2[:, 8 + t:9 + t]))
                    step(V.scalar_tensor_tensor(H[:, t, :], H[:, t, :], ST[:, 104 + t:105 + t], GB[:, 0, :], ALU.mult, ALU.mult))
                    post("output_ready")

        @block.scalar
        def _(act):
            A = nc.scalar.activation
            step = Link(act, "scalar_steps")
            got, fulls = {}, {}

            def offer(f):
                if f in got:
                    return
                act.sem_inc(f.free, f.slots)
                got[f] = fulls[f] = 0

            def ready(f, tile=None, i=None, per=0, tper=0):
                if tile is None:
                    fulls[f] += 1
                    act.wait_ge(f.full, v(fulls[f], i, per))
                else:
                    act.wait_ge(wused, v(tile + 1, i, tper))

            def give(f, ins, i=None, per=0):
                got[f] += 1
                ins.then_inc(f.free, 1)
                act.wait_ge(f.free, v(f.slots + got[f], i, per))

            def post(name, n=1):
                act.sem_inc(S(name), n)

            def mod_rows(L, m, bank_, rows):
                f = flow(L, "mod_rows", 2)
                offer(f)
                ready(f, MOD_TILES[L][m])
                give(f, A(rows[0:2, :], bank(bank_)[0:2, :], ACT.Copy))

            def mod_columns(L, m, bank_):
                f = flow(L, "mod_columns", 1)
                offer(f)
                ready(f)
                give(f, A(MODC[:, 4 * m:4 * m + 4, :].rearrange("p a b -> p (a b)"), bank(bank_, 8), ACT.Copy))
                post("mod_sums_ready")

            def modulation_start(L):
                offer(flow(L, "mod_rows", 2))
                fc = flow(L, "mod_columns", 1)
                offer(fc)
                ready(fc)
                give(fc, A(CV[:, :, :].rearrange("p k l -> p l k"), bank(7, 32).rearrange("p (l k) -> p l k", l=4), ACT.Silu))
                for m in range(13):
                    if m < 12:
                        mod_rows(L, m, 5 + m % 2, MOD_ROWS_START[:, m % 2, :])
                    if m:
                        mod_columns(L, m - 1, 7)

            def gates(L):
                f = flow(L, "gates", 4)
                offer(f)
                for a in range(4):
                    ready(f)
                    give(f, A(GATE[:, a // 2, a % 2, :], bank(2 * a, 1024), ACT.Copy))

            def transposed_input(L, which):
                f = flow(L, "u" + which + "_s", 2)
                offer(f)
                _, pieces = tiles_of(L)
                if which == "m":
                    pieces = 2
                w = 2 * (which == "f")
                act.wait_ge(S("columns_ready"), nth(L))
                for k in range(1, KD, 2):
                    ready(f)
                    x = (k // 2 % 2) * 2048 + 1024
                    for p in range(pieces):
                        a, n = ((0, LAT), (LAT, CTX))[p]
                        ins = A(UT[:, k, a:a + n], PS[:, x + a:x + a + n], ACT.Identity, scale=COL[:, w + 1, k, p:p + 1], bias=COL[:, w, k, p:p + 1])
                        if p == pieces - 1:
                            give(f, ins)
                        else:
                            step(ins)

            def roots(L, which, ntok):
                for t in range(ntok):
                    act.wait_ge(S("variance_ready"), normed_before(L, which) + t + 1)
                    step(A(ST[:, 112 + t:113 + t], ST[:, 96 + t:97 + t], ACT.Sqrt))
                    post("deviation_ready")
                    if which == "f" and next_of.get(L) == 2 and t:
                        rms(2, "m", t - 1, "f_residual_ready")

            def rms(L, which, t, wait, base=0):
                junk = UTF[:, 1024:2048] if L == 2 and which == "m" and 1 in layers else SQ_TMP
                if L == 2 and which == "m" and t >= TL:
                    act.wait_ge(S("second_context_in"), 16)
                elif wait:
                    act.wait_ge(S(wait), base + t + 1)
                step(A(junk, H[:, t, :], ACT.Square, accum_out=ST2[:, t:t + 1]))
                step(A(ST2[:, 8 + t:9 + t], ST2[:, t:t + 1], ACT.Sqrt, scale=1.0 / D, bias=EPSC[:, 0:1]))
                post(f"{which}_rms_ready")

            def attend(L):
                heads, dv, P, PT, O, scale = att_frame(L)
                units = att_units(L)
                n = len(units)
                sf, tf, of = flow(L, "scores", 2), flow(L, "probsT", 1), flow(L, "heads", 1)
                offer(sf)
                offer(tf)
                u0, x0 = units_before(L), turns_ahead(L)
                for k in range(n + 4):
                    if k < n:
                        u = units[k]
                        x = (k % 2) * 1024
                        act.wait_ge(S("maxima_ready"), u0 + k + 1)
                        if k >= 2:
                            act.wait_ge(tf.full, u0 + x0 + nth_probsT(L, k - 2))
                        if k >= 8:
                            act.wait_ge(of.free, of.slots + u0 + k - 7)
                        neg = ST[:, 136 + k % 8:137 + k % 8]
                        if L == 0:
                            step(A(ST2[:, 24 + k % 8:25 + k % 8], A_SINK[:, u["h"]:u["h"] + 1], ACT.Exp, scale=scale, bias=neg))
                        give(sf, A(P[:, k % 2, u["first"]:768], PS[:, x + u["first"]:x + 768], ACT.Exp, scale=scale, bias=neg,
                                   accum_out=ST2[:, 16 + k % 8:17 + k % 8]))
                        post("probs_ready")
                    if 1 <= k <= n:
                        w = 128 * len(units[k - 1]["vals"])
                        ready(tf)
                        if k >= 3:
                            act.wait_ge(of.full, u0 + k - 2)
                        give(tf, A(PT[:, (k - 1) % 2, 0:w], bank(4, w), ACT.Copy))
                    t = k // heads - 1
                    if t >= 0 and k == turn_step(L, t):
                        ready(tf)
                        give(tf, A(UT[:, :, t * 128:(t + 1) * 128], bank(4, D).rearrange("p (a b) -> p a b", a=KD), ACT.Copy))
                    if L in next_of and k % 8 == 4 and k < n:
                        mod_rows(next_of[L], k // 8, 7, MOD_ROWS[L])
                    if L in next_of and k % 8 == 7 and k < n:
                        mod_columns(next_of[L], k // 8, 7)

            def mixer0():
                t0 = T0[0, "in"]
                f = flow(0, "q", 4)
                offer(f)
                for c in range(10):
                    ready(f, t0 + c // 4 if c in (3, 7) else None)
                    x = (c % 4) * 1024
                    give(f, A(A_Q[:, c, :] if c < 8 else A_KC[:, c - 8, :], PS[:, x:x + TOK], ACT.Copy))
                attend(0)

            def mixer2():
                t0 = T0[2, "in"]
                f = flow(2, "uf", 4)
                offer(f)
                for c in range(4):
                    ready(f, t0 if c == 3 else None)
                    give(f, A(C_UF[:, c, :], PS[:, c * 1024:c * 1024 + TOK], ACT.Copy))
                f = flow(2, "ft", 2)
                offer(f)
                for g in range(4):
                    ready(f)
                    give(f, A(C_MIX[:, g, :], PS[:, g % 2 * 1024:g % 2 * 1024 + TOK], ACT.Copy))
                f = flow(2, "qk", 4)
                offer(f)
                for c in range(4):
                    ready(f, t0 + 1 if c == 3 else None)
                    give(f, A(C_QK[:, c, :], PS[:, c * 1024:c * 1024 + TOK], ACT.Copy, scale=GLA_DK ** -0.5 if c < 2 else 1.0))
                f = flow(2, "z", 1)
                offer(f)
                act.wait_ge(S("L2_ones_ready"), 1)
                ready(f)
                give(f, A(C_ZT[0:16, :], PS[0:16, 0:TOK], ACT.Copy))
                f = flow(2, "la", NT)
                offer(f)
                for t in range(NT):
                    ready(f)
                    give(f, A(C_LA[:, t, :], bank(t), ACT.Copy))
                post("L2_logits_ready")
                act.wait_ge(S("L2_minus_abs_ready"), 1)
                step(A(C_T1, C_T1, ACT.Exp))
                step(A(C_T1, C_T1, ACT.Ln, bias=1.0))
                post("L2_log_ready")
                vr = flow(2, "vr", NT)
                for t in range(NT):
                    if t == NT - 1:
                        act.wait_ge(wused, t0 + 4)
                    else:
                        act.wait_ge(vr.full, NT - 1 + t + 1)
                    ins = A(C_R[:, t, :], bank(t), ACT.Silu)
                    ins.then_inc(vr.free, 1)
                    act.wait_ge(vr.free, NT + NT + t + 1)
                    post("L2_r_ready")
                for a in range(4):
                    act.wait_ge(S("L2_sums_ready"), a + 1)
                    step(A(C_QB[:, a, :], C_BT[:, a, :], ACT.Exp))
                post("L2_query_decay_ready")
                f = flow(2, "ec", NT)
                offer(f)
                for t in range(NT):
                    ready(f)
                    give(f, A(C_KE[:, t, :], bank(t), ACT.Exp))
                go, gt = flow(2, "mixed_heads", 1), flow(2, "turned", 1)
                offer(gt)
                e = UTF[:, 0:1792]

                def level_decays(n):
                    act.wait_ge(S("L2_differences_ready"), n + 1)
                    step(A(e, e, ACT.Abs))
                    step(A(e, e, ACT.Exp, scale=-1.0))
                    post("L2_level_decays_ready")

                def turned(t):
                    ready(gt)
                    give(gt, A(C_MIX[:, 4:8, t * 128:(t + 1) * 128], bank(6).rearrange("p (a b) -> p a b", a=4), ACT.Copy))

                level_decays(0)
                for n in range(2 * NT):
                    t, dr = n // 2, n % 2
                    if n + 1 < 2 * NT:
                        level_decays(n + 1)
                    if n and 2 in next_of:
                        mod_columns(3, n - 1, 7)
                    if dr == 1:
                        if t:
                            turned(t - 1)
                        act.wait_ge(go.full, t + 1)
                        for h in range(GLA_H):
                            step(A(C_JUNK, bank(4 + h % 2, 128, h // 2 * 128), ACT.Square, accum_out=ST2[:, 32 + h:33 + h]))
                        step(A(ST2[:, 36:40], ST2[:, 32:36], ACT.Sqrt, scale=1.0 / GLA_DV, bias=EPSC))
                        post("L2_head_rms_ready")
                    if 2 in next_of:
                        mod_rows(3, n, 7, MOD_ROWS[2])
                if 2 in next_of:
                    mod_columns(3, 11, 7)
                turned(NT - 1)

            def mixer3():
                t0 = T0[3, "in"]
                kv, q = flow(3, "kv", NT), flow(3, "q", TL)
                offer(kv)
                offer(q)

                def root_of(s_):
                    nh = head_pieces()[s_][2]
                    act.wait_ge(S("L3_head_squares_ready"), s_ + 1)
                    step(A(ST[:, 16:16 + nh], ST[:, 0:nh], ACT.Sqrt, scale=1.0 / DB, bias=EPSC))
                    post("L3_head_rms_ready")

                for s_, (t, c0, nh) in enumerate(head_pieces()):
                    if c0 == 1024:
                        ready(kv, t0 if t == NT - 1 else None)
                        step(A(B_QK[:, t, 1024:1280], bank(t, 256), ACT.Copy))
                        give(kv, A(B_V[:, t, :], bank(t, 256, 256), ACT.Copy))
                    else:
                        ready(q, t0 + 1 + c0 // 512 if t == TL - 1 else None)
                        give(q, A(B_QK[:, t, c0:c0 + 512], bank(t), ACT.Copy))
                    post("L3_qk_in")
                    if s_:
                        root_of(s_ - 1)
                root_of(len(head_pieces()) - 1)
                f = flow(3, "turned", 2)
                offer(f)
                for n in range(2 + TL):
                    ready(f)
                    x = n % 2 * 1024
                    if n < 2:
                        give(f, A(B_KT[:, :, n * 384:(n + 1) * 384], PS[:, x:x + 768].rearrange("p (a b) -> p a b", a=2), ACT.Copy))
                    else:
                        t = n - 2
                        give(f, A(B_QT[:, :, t * 128:(t + 1) * 128], PS[:, x:x + 1024].rearrange("p (a b) -> p a b", a=8), ACT.Copy))
                attend(3)

            def mixer1():
                act.wait_ge(S("ssm_vectors_in"), 96)
                step(A(SSM_ALOG, SSM_ALOG, ACT.Exp))
                flat = lambda a: a.rearrange("p t n -> p (t n)")
                e, u, lg = flat(SSM_WD), flat(SSM_EACS), flat(SSM_ETOT)
                act.wait_ge(S("L1_minus_abs_ready"), 1)
                step(A(e, e, ACT.Exp))
                post("L1_exp_ready")
                act.wait_ge(S("L1_one_plus_ready"), 1)
                step(A(lg, u, ACT.Ln))
                post("L1_log_ready")
                z, xt, tf = flow(1, "z", TL), flow(1, "xt", 2), flow(1, "turned", 1)
                for f in (z, xt, tf):
                    offer(f)

                def turned(g, c):
                    ready(tf)
                    give(tf, A(SSM_YT[:, g * 4:g * 4 + 4, c * 128:(c + 1) * 128], bank(0).rearrange("p (a b) -> p a b", a=4), ACT.Copy))

                for g in range(SSM_G):
                    t0 = T0[1, "in"] + per_group * g
                    for n in range(6):
                        act.wait_ge(S("L1_convolved"), 6 * g + n + 1)
                        y = (SSM_BT, SSM_CT)[n] if n < 2 else SSM_XT[:, n - 2, :]
                        step(A(y, y, ACT.Silu))
                        post("L1_channels_ready")
                    if g == 0:
                        act.wait_ge(S("L1_sums_ready"), 1)
                        step(A(flat(SSM_EACS), flat(SSM_ACS), ACT.Exp))
                        step(A(flat(SSM_ETOT), flat(SSM_ETOT), ACT.Exp))
                        step(A(flat(SSM_WD), flat(SSM_WD), ACT.Exp))
                        post("L1_decays_ready")
                    for t in range(TL):
                        ready(z, t0 + 3 if t == TL - 1 else None)
                        give(z, A(ssm_z(t), bank(4 + t), ACT.Silu))
                    for n in range(5):
                        ready(xt)
                        src = PS[:, n % 2 * 1024:n % 2 * 1024 + TOK].rearrange("p (t c) -> p t c", t=NT)
                        give(xt, A(SSM_X[:, :, n * 128:(n + 1) * 128] if n < 4 else SSM_BK, src, ACT.Copy))
                        post("L1_tokens_ready")
                    for k in range(18):
                        if k < 16:
                            act.wait_ge(S("L1_exponents_ready"), 16 * g + k + 1)
                            dm = SSM_DM[:, k % 4, :]
                            step(A(dm, dm, ACT.Exp))
                            post("L1_exponentials_ready")
                        if k >= 8 and k % 4 == 0:
                            turned(g, k // 4 - 2)
                        if k >= 5 and k % 4 == 1:
                            act.wait_ge(S("L1_gated"), TL * g + k // 4)
                            step(A(SSM_T2, SSM_T1, ACT.Square, accum_out=ST2[:, 32:33]))
                            step(A(ST2[:, 33:34], ST2[:, 32:33], ACT.Sqrt, scale=1.0 / 512, bias=RMSC))
                            post("L1_rms_ready")
                        if 1 in next_of and k in (5, 9, 13):
                            mod_rows(next_of[1], 3 * g + k // 4 - 1, 1, MOD_ROWS[1])
                        if 1 in next_of and k in (7, 11, 15):
                            mod_columns(next_of[1], 3 * g + k // 4 - 1, 1)
                    turned(g, TL - 1)

            def feed_forward(L):
                f = flow(L, "up", 4)
                _, pieces = tiles_of(L)
                n = TOK if pieces == 2 else LAT
                if L < 2:
                    offer(f)
                    hid = big(0, 32, TOK)
                    t0 = T0[L, "up"]
                    with act.Fori(0, 4, 1) as i:
                        step.begin(i, 8)
                        for s in range(2):
                            for c in range(4):
                                ready(f, t0 + s if c == 3 else None, i, 6, 2)
                                x = c * 1024
                                out = hid[:, bass.ds(i * 8 + s * 4 + c, 1), 0:n].rearrange("p a b -> p (a b)")
                                act.sem_inc(S("scalar_ticks"), 1)
                                give(f, A(out, PS[:, x:x + n], ACT.Relu), i, 8)
                                act.sem_inc(S("scalar_ticks"), 1)
                                step(A(out, out, ACT.Square))
                    step.end(4)
                    got[f] += 24
                    fulls[f] += 18
                    post("hidden_ready")
                    return
                hid = big(0, NF2, TOK)
                for j in range(NF2):
                    act.wait_ge(S("gates_convolved"), NF2 * second.index(L) + j + 1)
                    step(A(hid[:, j, 0:n], CONV_Y[:, j % 2, 0:n], ACT.Silu))
                    post("gates_done")

            act.wait_ge(S("eps_ready"), 1)
            modulation_start(layers[0])
            for L in layers:
                ntok, _ = tiles_of(L)
                if L >= 2:
                    if L == layers[0]:
                        act.wait_ge(S("tokens_in"), 32)
                    for t in range(TL - 1 if L == 2 and 1 in layers else 0, NT):
                        if L == 2:
                            rms(L, "m", t, "f_residual_ready" if 1 in layers else None)
                        else:
                            rms(L, "m", t, "f_residual_ready" if 2 in layers else None, border_tiles)
                transposed_input(L, "m")
                gates(L)
                (mixer0, mixer1, mixer2, mixer3)[L]()
                if L < 2:
                    roots(L, "m", ntok)
                else:
                    for t in range(ntok):
                        rms(L, "f", t, "m_residual_ready", tiles_before(L, "f"))
                transposed_input(L, "f")
                feed_forward(L)
                if L < 2:
                    roots(L, "f", ntok)
            if layers[-1] == 3:
                for t in range(TL):
                    rms(3, "final", t, "f_residual_ready", border_tiles + tiles_before(3, "f"))

        @block.gpsimd
        def _(pool):
            def bring(name, dst, src):
                pool.dma_start(dst, src, allow_slow_non_contiguous=True).then_inc(S(name), 16)

            def spread(a, n):
                return a.unsqueeze(0).to_broadcast([128, n])

            rows = lambda a: a.rearrange("(k p) -> k p", p=128)
            for n, a in enumerate((d["c"][0], d["c_ctx"], d["c_2"][0], d["c_ctx_2"])):
                bring("conditioning_in", CONDITIONING_ROWS[n * KD:(n + 1) * KD, :], rows(a))
            bring("constants_in", CS[:, :], d["c_small"])
            bring("tokens_in", H[:, 0:TL, :], d["x"][0].rearrange("(t p) n -> p t n", p=128))
            bring("tokens_in", H[:, TL:NT, :], d["ctx"][0].rearrange("(t p) n -> p t n", p=128))
            def bring_bias(L):
                bm = d["b_mod"] if L < 2 else d["b_mod_2"]
                bring("mod_bias_in", BIAS_ROWS, rows(bm[L % 2]))
                if L >= 2:
                    bring("mod_bias_in", GAIN_ROWS[0:KD, :], rows(d["g_norm_mix_2"][L % 2]))
                    bring("mod_bias_in", GAIN_ROWS[KD:2 * KD, :], rows(d["g_norm_ffn_2"][L % 2]))

            def scan_products():
                G = nc.gpsimd

                def times(name, out, a, b):
                    G.tensor_tensor(out, a, b, ALU.mult).then_inc(S(name), 1)

                def input_of(g, c):
                    over = 16 * g + 4 * max(c - 1, 0)
                    if over:
                        pool.wait_ge(S("L1_weights_used"), over)
                    for dr in range(2):
                        times("L1_inputs_ready", by_head(SSM_XDT[:, c % 2, dr, :]), by_head(SSM_X[:, c, :]), heads_of(SSM_DT, c, dr, g))

                for g in range(SSM_G):
                    pool.wait_ge(S("L1_tokens_ready"), 5 * (g + 1))
                    if g == 0:
                        pool.wait_ge(flow(1, "bc", 1).free, 2)
                    for n in range(10):
                        c = SSM_ORDERS[n // 5][n % 5]
                        if n == 0 and g:
                            pool.wait_ge(S("L1_weights_used"), 16 * g)
                        if n >= 2:
                            pool.wait_ge(flow(1, "state", 2).full, 10 * g + n - 1)
                        times("L1_state_input_ready", by_head(SSM_XW[:, n % 2, :]), by_head(SSM_X[:, c, :]), heads_of(SSM_WD, c, n // 5, g))
                    for k in range(16):
                        c = k // 4
                        if k == 0:
                            input_of(g, 0)
                        pool.wait_ge(S("L1_exponentials_ready"), 16 * g + k + 1)
                        dm = SSM_DM[:, k % 4, :].rearrange("p (d h l) -> p d h l", d=2, h=2)
                        times("L1_weights_ready", dm, dm, SSM_GM[:, :, c, :].unsqueeze(2).to_broadcast([128, 2, 2, 128]))
                        if k % 4 == 2:
                            if c or g:
                                pool.wait_ge(S("L1_gated"), TL * g + c)
                            times("L1_skip_ready", by_head(SSM_SKIP), by_head(SSM_X[:, c, :]), SSM_DSK[:, g * 8:(g + 1) * 8].unsqueeze(2).to_broadcast([128, 8, 64]))
                        if k % 4 == 1 and c < TL - 1:
                            input_of(g, c + 1)

            bring_bias(layers[0])
            for n, L in enumerate(layers):
                if n:
                    pool.wait_ge(S("layer_done"), n)
                l = L % 2
                if L == 2 and n == 0:
                    pool.wait_ge(S("tokens_in"), 32)
                    bring("second_context_in", H[:, TL:NT, :], d["ctx_2"][0].rearrange("(t p) n -> p t n", p=128))
                if L == 0:
                    bring("attention_constants_in", A_CONST, d["c_att"])
                    bring("attention_constants_in", A_SINK, spread(d["att_sink"][0], HA))
                if L == 2:
                    bring("fourier_tables_in", C_TABS, d["c_four"])
                    bring("gate_weights_in", C_WZ, d["w_even_in_2"][0].rearrange("(k p) n -> p k n", p=128)[:, :, 2048:2064])
                    for dr in range(2):
                        bring("gate_weights_in", C_WG[0:16, dr * 256:(dr + 1) * 256], d["w_gla_gate_2"][0, dr])
                    bring("gate_weights_in", C_WG[16:17, :].rearrange("p (a b) -> p a b", a=2), d["b_gla_gate_2"][0:1, :, :])
                    bring("gate_weights_in", C_GAIN, spread(d["g_gla_out_2"][0], 512))
                    pool.wait_ge(S("L2_sums_ready"), 1)
                    bring("gla_masks_in", UTF[:, 5376:5888].bitcast(U32), d["c_mask"])
                if L == 3:
                    bring("second_attention_constants_in", B_CONST, d["c_att2"])
                    bring("second_attention_constants_in", B_G[:, 0:128], spread(d["g_q_2"][0], 128))
                    bring("second_attention_constants_in", B_G[:, 128:256], spread(d["g_k_2"][0], 128))
                if L == 1:
                    bring("ssm_vectors_in", SSM_WDT, d["ssm_w_in"][0].rearrange("(k p) n -> p k n", p=128)[:, :, SSM_DI + CONV_SSM:SSM_DI + CONV_SSM + 64])
                    bring("ssm_vectors_in", SSM_DTB, spread(d["ssm_dt_bias"][0].rearrange("a b -> (a b)"), 64))
                    bring("ssm_vectors_in", SSM_ALOG, spread(d["ssm_a_log"][0].rearrange("a b -> (a b)"), 64))
                    bring("ssm_vectors_in", SSM_DSK, spread(d["ssm_d"][0], SSM_H))
                    bring("ssm_vectors_in", SSM_CW_ROWS[:, 0:640].rearrange("j (a p) -> j a p", a=5), d["ssm_conv_w"][0].rearrange("a (j p) -> j a p", p=128))
                    bring("ssm_vectors_in", SSM_CW_ROWS[:, 640:768], rows(d["ssm_conv_b"][0]))
                    pool.wait_ge(flow(1, "um_v", 2).free, 2 + 4 * (n + 1))
                    pool.wait_ge(flow(1, "um_s", 2).free, 2 + 4 * (n + 1))
                    bring("ssm_gain_in", SSM_NG, spread(d["ssm_norm_g"][0], SSM_DI))
                    scan_products()
                    pool.wait_ge(S("L1_scan_done"), 1)
                    if 2 in layers:
                        bring("second_context_in", H[:, TL:NT, :], d["ctx_2"][0].rearrange("(t p) n -> p t n", p=128))
                if L < 2:
                    for w, kind in enumerate(("mix", "ff")):
                        if 2 * n + w:
                            pool.wait_ge(S("norm_vectors_used"), 2 * n + w)
                        bring("norm_vectors_in", GB[:, 0, :], spread(d[f"ln_{kind}_g"][l], D))
                        bring("norm_vectors_in", GB[:, 1, :], spread(d[f"ln_{kind}_b"][l], D))
                else:
                    pool.wait_ge(S("m_residual_ready"), tiles_before(L, "m") + 1)
                    bring("conv_vectors_in", CONV_ROWS[:, 0:384].rearrange("j (a p) -> j a p", a=3), d["w_ffn_conv_2"][l].rearrange("a (j p) -> j a p", p=128))
                    bring("conv_vectors_in", CONV_ROWS[:, 384:512], rows(d["b_ffn_conv_2"][l]))
                if L in next_of:
                    pool.wait_ge(S("hidden_ready"), nth(L))
                    bring_bias(next_of[L])
            if layers[-1] == 3:
                pool.wait_ge(S("conv_vectors_used"), len(second))
                bring("norm_vectors_in", GB[:, 0, :], spread(d["g_norm_final_2"], D))


def kernel(**inputs):
    import numpy as _np
    import concourse.bacc as _bacc
    from concourse import mybir as _mybir
    from concourse.bass_utils import run_bass_kernel_spmd as _run

    nc = _bacc.Bacc("TRN2", target_bir_lowering=False, num_devices=1)
    arrays, d, at = {}, {}, {}
    for name, (a, where) in constants().items():
        at[name] = where
        arrays[name + "_dram"] = a
    for name in inputs:
        arrays[name + "_dram"] = _np.ascontiguousarray(inputs[name])
    for name, a in arrays.items():
        d[name[:-5]] = nc.dram_tensor(name, a.shape, _mybir.dt.from_np(a.dtype), kind="ExternalInput").ap()
    d["at"] = at
    d["out"] = nc.dram_tensor("out_dram", (LAT, D), F32, kind="ExternalOutput").ap()
    build(nc, d)
    r = _run(nc, [arrays], core_ids=[0])
    return r.results[0]["out_dram"].reshape(1, LAT, D)
```
